# Optimizing a Trainium2 kernel written in Bass

```python
import jax, jax.numpy as jnp
from jax import lax
import numpy as np

D_MODEL = 1024
BATCH = 1
SEQ = 256
DEPTH = 1
DEC_BATCH = 1
DEC_SEQ = 1024
PAST_LEN = 256

GRID_W = 64
N_DIR = 2
HG_WIDTH = 512
HG_HEADS = 4
HG_DK = 128
HG_DV = HG_WIDTH // HG_HEADS
HG_CHUNK = 16
LRU_WIDTH = 512
LRU_BLOCKS = 8
LRU_BLOCK = LRU_WIDTH // LRU_BLOCKS
LRU_C = 8.0
CONV_W = 4
CONV_LEFT = 2
D_FF = 4 * D_MODEL
EPS = 1e-6
POS_BASE = 10000.0
HG_QF = N_DIR * HG_HEADS * HG_DK
SPLITS = (HG_QF, 2 * HG_QF, 2 * HG_QF + HG_WIDTH, 2 * HG_QF + 2 * HG_WIDTH,
          2 * HG_QF + 2 * HG_WIDTH + LRU_WIDTH)
IN_COLS = 2 * HG_QF + 2 * HG_WIDTH + 2 * LRU_WIDTH
MIX_WIDTH = HG_WIDTH + LRU_WIDTH

kernel_name = "hybrid_hgrn2_rglru_diffusion_step"

def rms_norm(x, gain):
    xf = x.astype(jnp.float32)
    y = xf * lax.rsqrt(jnp.mean(xf * xf, axis=-1, keepdims=True) + EPS)
    return (y * gain.astype(jnp.float32)).astype(x.dtype)

def grid_pos_embed(n_tok, dtype):
    rows = n_tok // GRID_W
    rr, cc = jnp.meshgrid(jnp.arange(rows), jnp.arange(GRID_W), indexing='ij')
    quarter = D_MODEL // 4
    omega = 1.0 / (POS_BASE ** (jnp.arange(quarter, dtype=jnp.float32) / quarter))

    def emb(pos):
        ang = pos.reshape(-1, 1).astype(jnp.float32) * omega
        return jnp.concatenate([jnp.sin(ang), jnp.cos(ang)], axis=-1)

    return jnp.concatenate([emb(rr), emb(cc)], axis=-1).astype(dtype)

def hgrn2_chunkwise(q, logf, v, s0):
    B, T, H, K = q.shape
    C = HG_CHUNK
    N = T // C
    k = -jnp.expm1(logf)
    qc, kc, vc, lf = [a.reshape(B, N, C, H, -1) for a in (q, k, v, logf)]
    b = jnp.cumsum(lf, axis=2)
    mask = jnp.tril(jnp.ones((C, C), dtype=bool))[None, None, :, :, None, None]
    rel = b[:, :, :, None] - b[:, :, None, :]
    decay = jnp.where(mask, jnp.exp(jnp.minimum(rel, 0.0)), 0.0)
    attn = jnp.einsum('bnthk,bnshk,bntshk->bnhts', qc, kc, decay)
    o_intra = jnp.einsum('bnhts,bnshv->bnthv', attn, vc)
    b_last = b[:, :, -1]
    k_dec = kc * jnp.exp(b_last[:, :, None] - b)
    d_state = jnp.einsum('bnshk,bnshv->bnhkv', k_dec, vc)
    chunk_decay = jnp.exp(b_last)

    def step(s, inp):
        dec, ds = inp
        return dec[..., None] * s + ds, s

    s_fin, s_in = lax.scan(step, s0, (jnp.moveaxis(chunk_decay, 1, 0),
                                      jnp.moveaxis(d_state, 1, 0)))
    s_in = jnp.moveaxis(s_in, 0, 1)
    o_inter = jnp.einsum('bnthk,bnhkv->bnthv', qc * jnp.exp(b), s_in)
    return (o_intra + o_inter).reshape(B, T, H, -1), s_fin

def block_diag(x, w, bias):
    xb = x.reshape(x.shape[0], x.shape[1], LRU_BLOCKS, LRU_BLOCK)
    return jnp.einsum('btnd,nde->btne', xb, w).reshape(x.shape) + bias

def rglru_scan(x, wa, ba, wx, bx, lam, h0):
    r = jax.nn.sigmoid(block_diag(x, wa, ba))
    i = jax.nn.sigmoid(block_diag(x, wx, bx))
    log_a = -LRU_C * r * jax.nn.softplus(-lam)
    a = jnp.exp(log_a)
    u = jnp.sqrt(-jnp.expm1(2.0 * log_a)) * (i * x)
    u = u.at[:, 0].add(a[:, 0] * h0)

    def comb(left, right):
        a1, b1 = left
        a2, b2 = right
        return a1 * a2, a2 * b1 + b2

    _, h = lax.associative_scan(comb, (a, u), axis=1)
    return h, h[:, -1]

def dwconv_centred(x, w, bias):
    T = x.shape[1]
    xp = jnp.pad(x, ((0, 0), (CONV_LEFT, CONV_W - 1 - CONV_LEFT), (0, 0)))
    out = bias
    for j in range(CONV_W):
        out = out + xp[:, j:j + T] * w[j]
    return out

def mixer(h, p, l, hg_s0, lru_s0):
    f32 = jnp.float32
    B, T, _ = h.shape
    proj = h @ p['w_in'][l]
    hq, hf, hi, hgate, lx, lg = jnp.split(proj, SPLITS, axis=-1)
    q = jax.nn.silu(hq.astype(f32)).reshape(B, T, N_DIR, HG_HEADS, HG_DK)
    lb = jnp.cumsum(jax.nn.softmax(p['hg_lb_logits'].astype(f32), axis=0), axis=0)[l]
    fz = hf.astype(f32).reshape(B, T, N_DIR, HG_HEADS, HG_DK)
    logf = jnp.log(lb + (1.0 - lb) * jax.nn.sigmoid(fz))
    v = hi.astype(f32).reshape(B, T, HG_HEADS, HG_DV)
    o_f, s_f = hgrn2_chunkwise(q[:, :, 0], logf[:, :, 0], v, hg_s0[:, 0])
    o_b, s_b = hgrn2_chunkwise(jnp.flip(q[:, :, 1], 1), jnp.flip(logf[:, :, 1], 1),
                               jnp.flip(v, 1), hg_s0[:, 1])
    o = o_f + jnp.flip(o_b, 1)
    o = rms_norm(o, p['hg_norm_gain'][l]) * jax.nn.silu(hgate.astype(f32)).reshape(B, T, HG_HEADS, HG_DV)
    hg_out = o.reshape(B, T, HG_WIDTH)
    xc = dwconv_centred(lx.astype(f32), p['conv_w'][l].astype(f32), p['conv_b'][l].astype(f32))
    h_f, e_f = rglru_scan(xc, p['lru_wa'][l, 0].astype(f32), p['lru_ba'][l, 0].astype(f32),
                          p['lru_wx'][l, 0].astype(f32), p['lru_bx'][l, 0].astype(f32),
                          p['lru_lambda'][l, 0].astype(f32), lru_s0[:, 0])
    h_b, e_b = rglru_scan(jnp.flip(xc, 1), p['lru_wa'][l, 1].astype(f32), p['lru_ba'][l, 1].astype(f32),
                          p['lru_wx'][l, 1].astype(f32), p['lru_bx'][l, 1].astype(f32),
                          p['lru_lambda'][l, 1].astype(f32), lru_s0[:, 1])
    lru_out = (h_f + jnp.flip(h_b, 1)) * jax.nn.gelu(lg.astype(f32))
    mix = jnp.concatenate([hg_out, lru_out], axis=-1).astype(h.dtype) @ p['w_out'][l]
    return mix, jnp.stack([s_f, s_b], axis=1), jnp.stack([e_f, e_b], axis=1)

def run_trunk(x, cond, p, hg_init, lru_init):
    hg_fin, lru_fin = [], []
    for l in range(DEPTH):
        m = (jax.nn.silu(cond.astype(jnp.float32)) @ p['w_ada'][l].astype(jnp.float32)
             + p['b_ada'][l].astype(jnp.float32))[:, None, :].astype(x.dtype)
        sh1, sc1, g1, sh2, sc2, g2 = jnp.split(m, 6, axis=-1)
        h = rms_norm(x, p['norm1_gain'][l]) * (1.0 + sc1) + sh1
        mix, s_hg, s_lru = mixer(h, p, l, hg_init[:, l].astype(jnp.float32),
                                 lru_init[:, l].astype(jnp.float32))
        x = x + g1 * mix
        h = rms_norm(x, p['norm2_gain'][l]) * (1.0 + sc2) + sh2
        ff = jnp.square(jax.nn.relu(h @ p['w_ff1'][l])) @ p['w_ff2'][l]
        x = x + g2 * ff
        hg_fin.append(s_hg)
        lru_fin.append(s_lru)
    y = rms_norm(x, p['final_gain'])
    return y, jnp.stack(hg_fin, axis=1), jnp.stack(lru_fin, axis=1)

def setup_inputs(seed: int = 0) -> dict:
    key = jax.random.key(seed)
    ks = jax.random.split(key, 26)

    def nrm(k, shape, s):
        return jax.random.normal(k, shape, jnp.float32) * s

    a8 = jax.random.uniform(ks[20], (DEPTH, N_DIR, LRU_WIDTH), jnp.float32, minval=0.9, maxval=0.999)
    a = a8 ** (1.0 / LRU_C)
    lam = jnp.log(a) - jnp.log1p(-a)
    return {
        'x_prompt': nrm(ks[0], (BATCH, SEQ, D_MODEL), 1.0),
        'x_sample': nrm(ks[1], (DEC_BATCH, DEC_SEQ, D_MODEL), 1.0),
        'c': nrm(ks[2], (DEC_BATCH, D_MODEL), 1.0),
        'state_hgrn': nrm(ks[3], (DEC_BATCH, DEPTH, N_DIR, HG_HEADS, HG_DK, HG_DV), 0.3),
        'state_rglru': nrm(ks[4], (DEC_BATCH, DEPTH, N_DIR, LRU_WIDTH), 0.5),
        'c_ctx': nrm(ks[5], (D_MODEL,), 1.0),
        'w_ada': nrm(ks[6], (DEPTH, D_MODEL, 6 * D_MODEL), 0.5 * D_MODEL ** -0.5),
        'b_ada': nrm(ks[7], (DEPTH, 6 * D_MODEL), 0.02),
        'norm1_gain': 1.0 + nrm(ks[8], (DEPTH, D_MODEL), 0.02),
        'norm2_gain': 1.0 + nrm(ks[9], (DEPTH, D_MODEL), 0.02),
        'w_in': nrm(ks[10], (DEPTH, D_MODEL, IN_COLS), D_MODEL ** -0.5),
        'hg_lb_logits': nrm(ks[11], (DEPTH + 1, N_DIR, HG_HEADS, HG_DK), 0.5),
        'hg_norm_gain': 1.0 + nrm(ks[12], (DEPTH, HG_HEADS, HG_DV), 0.02),
        'conv_w': nrm(ks[13], (DEPTH, CONV_W, LRU_WIDTH), CONV_W ** -0.5),
        'conv_b': nrm(ks[14], (DEPTH, LRU_WIDTH), 0.02),
        'lru_wa': nrm(ks[15], (DEPTH, N_DIR, LRU_BLOCKS, LRU_BLOCK, LRU_BLOCK), LRU_BLOCK ** -0.5),
        'lru_ba': nrm(ks[16], (DEPTH, N_DIR, LRU_WIDTH), 0.02),
        'lru_wx': nrm(ks[17], (DEPTH, N_DIR, LRU_BLOCKS, LRU_BLOCK, LRU_BLOCK), LRU_BLOCK ** -0.5),
        'lru_bx': nrm(ks[18], (DEPTH, N_DIR, LRU_WIDTH), 0.02),
        'lru_lambda': lam,
        'w_out': nrm(ks[21], (DEPTH, MIX_WIDTH, D_MODEL), MIX_WIDTH ** -0.5),
        'w_ff1': nrm(ks[22], (DEPTH, D_MODEL, D_FF), D_MODEL ** -0.5),
        'w_ff2': nrm(ks[23], (DEPTH, D_FF, D_MODEL), D_FF ** -0.5),
        'final_gain': 1.0 + nrm(ks[24], (D_MODEL,), 0.02),
    }

def reference(x_prompt, x_sample, c, state_hgrn, state_rglru, c_ctx, w_ada, b_ada,
              norm1_gain, norm2_gain, w_in, hg_lb_logits, hg_norm_gain, conv_w, conv_b,
              lru_wa, lru_ba, lru_wx, lru_bx, lru_lambda, w_out, w_ff1, w_ff2, final_gain):
    p = {'w_ada': w_ada, 'b_ada': b_ada, 'norm1_gain': norm1_gain, 'norm2_gain': norm2_gain,
         'w_in': w_in, 'hg_lb_logits': hg_lb_logits, 'hg_norm_gain': hg_norm_gain,
         'conv_w': conv_w, 'conv_b': conv_b, 'lru_wa': lru_wa, 'lru_ba': lru_ba,
         'lru_wx': lru_wx, 'lru_bx': lru_bx, 'lru_lambda': lru_lambda, 'w_out': w_out,
         'w_ff1': w_ff1, 'w_ff2': w_ff2, 'final_gain': final_gain}
    bp = x_prompt.shape[0]
    hg_zero = jnp.zeros((bp, DEPTH, N_DIR, HG_HEADS, HG_DK, HG_DV), jnp.float32)
    lru_zero = jnp.zeros((bp, DEPTH, N_DIR, LRU_WIDTH), jnp.float32)
    y_prompt, hg_ctx, lru_ctx = run_trunk(x_prompt, c_ctx[None, :], p, hg_zero, lru_zero)
    new_state_hgrn = hg_ctx.astype(x_prompt.dtype)
    new_state_rglru = lru_ctx.astype(x_prompt.dtype)
    xs = x_sample + grid_pos_embed(x_sample.shape[1], x_sample.dtype)[None]
    y_sample, _, _ = run_trunk(xs, c, p, state_hgrn, state_rglru)
    return (y_prompt, y_sample, new_state_hgrn, new_state_rglru)


_drawn_inputs = setup_inputs


def setup_inputs(seed=0):
    import zlib

    import numpy as np

    out = dict(_drawn_inputs(seed))
    spreads = {}
    factors = {'state_hgrn': 64.0,
     'state_rglru': 3.594,
     'norm1_gain': 3.32,
     'norm2_gain': 18.345,
     'hg_norm_gain': 23.437,
     'lru_ba': 21.96,
     'lru_bx': 8.0,
     'final_gain': 24.529}
    for name, (base, spread) in spreads.items():
        noise = np.random.default_rng([zlib.crc32(name.encode()), seed]).standard_normal(out[name].shape)
        drawn = base * np.exp(spread * noise) if base else spread * noise
        out[name] = __import__('jax').numpy.asarray(drawn.astype(out[name].dtype))
    for name, factor in factors.items():
        out[name] = (out[name] * factor).astype(out[name].dtype)
    return out
```

```python
import concourse.bass as bass
from concourse import mybir
from contextlib import ExitStack

F32 = mybir.dt.float32
F32R = mybir.dt.float32r
I32 = mybir.dt.int32
ALU = mybir.AluOpType
ACT = mybir.ActivationFunctionType

P = 128
D_MODEL = 1024
CTX, LAT = 256, 1024
TOKENS = CTX + LAT
GRID_W = 64
KT = D_MODEL // P
IN_BLOCKS, FF_BLOCKS, ADA_BLOCKS = 32, 32, 48
HEADS, DIRS = 4, 2
CHUNKS = TOKENS // P
CTX_CHUNKS = CTX // P
EPS = 1e-6
LRU_C = 8.0
CONV_W, CONV_LEFT = 4, 2
TOK_BLOCKS = ((0, 256), (256, 512), (768, 512))
SEGS = ((0, CTX, 0), (CTX, LAT, 1))
GROUPS = ((0, 2), (2, 4), (6, 4))
T_LX, T_LG, T_V, T_GATE, T_Q0, T_F0, T_Q1, T_F1 = range(8)
PER_HEAD = 8

VEC = {}
_at = 0
for _name, _n in (("b_ada", 48), ("norm1", 8), ("norm2", 8), ("final", 8), ("lb", 16), ("hg_gain", 4),
                  ("conv_w", 16), ("conv_b", 4), ("ba", 8), ("bx", 8), ("lam", 8), ("h0", 8)):
    VEC[_name] = _at
    _at += _n
NVEC = _at
LEVELS = 7
MASKED = 5
MASKS = 1 + DIRS * MASKED
POS_COLS = 4 * (LAT // GRID_W) + 4 * GRID_W

KB = 1024
BASE = 16512
AREA = BASE + 3840


class Ctx:
    pass


def ds(at, n=1):
    return bass.ds(at, n)


def peeled(eng, n, body):
    body(0)
    with eng.Fori(1, n) as i:
        body(i)


def first(i):
    return isinstance(i, int) and i == 0


def wait_apart(g, eng, sem, value):
    eng.wait_ge(sem, value)
    eng.wait_ge(g.constants_ready, 1)


def exact_product(nc, out, w_hi, w_lo, x_hi, x_lo, start, stop):
    nc.tensor.matmul(out, w_lo, x_hi, start=start, stop=False)
    nc.tensor.matmul(out, w_hi, x_lo, start=False, stop=False)
    return nc.tensor.matmul(out, w_hi, x_hi, start=False, stop=stop)


def at(nc, name, shape, dtype, kb):
    return nc.alloc_sbuf_tensor_at(name, shape, dtype, offset=AREA + int(kb * KB))


def modulation_and_input(nc, g, a):
    ctx = ExitStack()
    with ctx:
        sem = lambda n: ctx.enter_context(nc.semaphore(n))
        cond = at(nc, "cond", [P, KT, 2], F32, 162)
        cond_s = g.cond_s
        ada_raw = at(nc, "ada_raw", [P, 2, D_MODEL], F32, 120)
        x_tok = at(nc, "x_tok", [P, 2, D_MODEL], F32, 128)
        pos = at(nc, "pos", [P, POS_COLS], F32, 136)
        vec_in, cond_in, cond_ready = sem("vec_in"), sem("cond_in"), sem("cond_ready")
        ada_in = [sem(f"ada_in{s}") for s in range(2)]
        ada_used = [sem(f"ada_used{s}") for s in range(2)]
        x_in = [sem(f"x_in{s}") for s in range(2)]
        x_used = [sem(f"x_used{s}") for s in range(2)]
        x_moved = [sem(f"x_moved{s}") for s in range(2)]
        ada_done, mod_ready, setup = sem("ada_done"), sem("mod_ready"), sem("setup")
        x_saved = sem("x_saved")
        n_ctx = CTX // P
        pos_r = pos[:, 0:4 * 16].rearrange("p (f r) -> p f r", f=4)
        pos_c = pos[:, 64:64 + 4 * 64].rearrange("p (f c) -> p f c", f=4)
        block = ctx.enter_context(nc.Block())

        @block.sync
        def _(sp):
            sp.dma_start(g.vecs[:, :], a["vecs"]).then_inc(vec_in, 16)
            sp.dma_start(g.ident[:, :], a["ident"]).then_inc(vec_in, 16)
            sp.dma_start(pos[:, :], a["pos"]).then_inc(vec_in, 16)
            sp.dma_start(cond[:, :, :], a["cond"]).then_inc(cond_in, 16)

            def load(i):
                for s in range(2):
                    if not first(i):
                        sp.wait_ge(ada_used[s], i)
                    sp.dma_start(ada_raw[:, s, :], a["w_ada"][ds(i * 2 + s), :, :].rearrange("a p n -> p (a n)")
                                 ).then_inc(ada_in[s], 16)
            peeled(sp, 8, load)

        @block.gpsimd
        def _(pool):
            pass

        @block.scalar
        def _(act):
            for s in range(2):
                act.dma_start(x_tok[:, s, :], a["x_prompt"][s * P:(s + 1) * P, :]).then_inc(x_in[s], 16)
            act.wait_ge(cond_in, 16)
            nc.scalar.activation(cond_s[:, :, :], cond[:, :, :], ACT.Silu).then_inc(cond_ready, 1)
            with act.Fori(0, LAT // (2 * P)) as i:
                for s in range(2):
                    act.wait_ge(x_used[s], i + 1)
                    act.dma_start(x_tok[:, s, :], a["x_sample"][ds((i * 2 + s) * P, P), :]).then_inc(x_in[s], 16)
            for s in range(2):
                act.wait_ge(x_moved[s], 2 * (1 + LAT // (2 * P)))
            act.dma_start(g.x_scratch, g.x[:, :, :].rearrange("p k t -> p (k t)")).then_inc(x_saved, 16)
            act.wait_ge(x_saved, 16)

        @block.tensor
        def _(pe):
            pe.wait_ge(vec_in, 48)

            def turn(i):
                for s in range(2):
                    pe.wait_ge(x_in[s], i * 16 + 16)
                    if not first(i):
                        pe.wait_ge(x_moved[s], i * 2)
                    for f in range(KT):
                        last = nc.tensor.transpose(g.bank[2 * s + f // 4][:, (f % 4) * P:(f % 4 + 1) * P],
                                                   x_tok[:, s, f * P:(f + 1) * P], g.ident[:, :])
                    last.then_inc(x_used[s], 1)
            peeled(pe, 1 + LAT // (2 * P), turn)
            pe.wait_ge(cond_ready, 1)
            with pe.Fori(0, 8) as i:
                for s in range(2):
                    pe.wait_ge(ada_in[s], i * 16 + 16)
                    for k in range(KT):
                        last = nc.tensor.matmul(g.bank[4][:, ds((i * 2 + s) * 2, 2)], ada_raw[:, s, k * P:(k + 1) * P],
                                                cond_s[:, k, :], start=(k == 0), stop=(k == KT - 1))
                    last.then_inc(ada_used[s], 1)

        @block.vector
        def _(dve):
            nc.vector.memset(g.ones[:, :], 1.0).then_inc(g.constants_ready, 1)
            nc.vector.memset(g.eps[:, :], EPS).then_inc(setup, 1)
            dve.wait_ge(vec_in, 48)
            x4 = g.x[:, :, :]
            for s in range(n_ctx):
                dve.wait_ge(x_used[s], 1)
                for half in range(2):
                    nc.vector.tensor_copy(x4[:, 4 * half:4 * half + 4, s * P:(s + 1) * P],
                                          g.bank[2 * s + half][:, :].rearrange("p (f t) -> p f t", f=4)
                                          ).then_inc(x_moved[s], 1)
            with dve.Fori(0, LAT // (2 * P)) as i:
                for s in range(2):
                    dve.wait_ge(x_used[s], i + 2)
                    for r in range(2):
                        nc.vector.tensor_tensor(
                            x4[:, 0:4, ds(CTX + (i * 2 + s) * P + r * GRID_W, GRID_W)],
                            g.bank[2 * s][:, :].rearrange("p (f t) -> p f t", f=4)[:, :, r * GRID_W:(r + 1) * GRID_W],
                            pos_r[:, :, ds(i * 4 + s * 2 + r)].broadcast_to([P, 4, GRID_W]), ALU.add
                        ).then_inc(x_moved[s] if r else setup, 1)
                    nc.vector.tensor_tensor(
                        x4[:, 4:8, ds(CTX + (i * 2 + s) * P, P)].rearrange("p f (r c) -> p f r c", r=2),
                        g.bank[2 * s + 1][:, :].rearrange("p (f r c) -> p f r c", f=4, r=2),
                        pos_c[:, :, :].unsqueeze(2).broadcast_to([P, 4, 2, GRID_W]), ALU.add
                    ).then_inc(x_moved[s], 1)
            for s in range(2):
                dve.wait_ge(ada_used[s], 8)
            nc.vector.tensor_tensor(g.mod[:, 0:16, :], g.bank[4][:, 0:32].rearrange("p (j c) -> p j c", c=2),
                                    g.v("b_ada", 0, 16).unsqueeze(2).broadcast_to([P, 16, 2]), ALU.add
                                    ).then_inc(mod_ready, 1)
            dve.wait_ge(mod_ready, 1)
            nc.vector.scalar_tensor_tensor(g.amp1[:, :, :], g.mod[:, 8:16, :], 1.0,
                                           g.v("norm1", 0, 8).unsqueeze(2).broadcast_to([P, 8, 2]), ALU.add, ALU.mult
                                           ).then_inc(mod_ready, 1)
            dve.wait_ge(mod_ready, 2)


def norm(nc, g, name, gain_amp, shift, tail):
    ctx = ExitStack()
    with ctx:
        sem = lambda n: ctx.enter_context(nc.semaphore(name + n))
        sq = at(nc, name + "sq", [P, 2, TOKENS], F32, 130)
        root = at(nc, name + "root", [P, TOKENS], F32, 140)
        rstd = at(nc, name + "rstd", [P, TOKENS], F32, 145)
        tmp = at(nc, name + "tmp", [P, 2, TOKENS], F32, 150)
        squared = [sem(f"squared{s}") for s in range(2)]
        summed = [sem(f"summed{s}") for s in range(2)]
        rooted, rstd_ready = sem("rooted"), sem("rstd_ready")
        scaled = [sem(f"scaled{s}") for s in range(2)]
        hi_done = [sem(f"hi_done{s}") for s in range(2)]
        lo_done = [sem(f"lo_done{s}") for s in range(2)]
        pairs = KT // 2
        block = ctx.enter_context(nc.Block())

        @block.scalar
        def _(act):
            def square(i):
                for s in range(2):
                    if not first(i):
                        wait_apart(g, act, summed[s], i)
                    nc.scalar.activation(sq[:, s, :], g.x[:, ds(i * 2 + s), :].rearrange("p a t -> p (a t)"),
                                         ACT.Square).then_inc(squared[s], 1)
            peeled(act, pairs, square)
            act.wait_ge(summed[1], pairs)
            for b, (t0, n) in enumerate(TOK_BLOCKS):
                nc.scalar.activation(root[:, t0:t0 + n], g.bank[b][:, 0:n], ACT.Sqrt, bias=g.eps[:, 0:1],
                                     scale=1.0 / D_MODEL).then_inc(rooted, 1)
            if not tail:
                return
            with act.Fori(0, pairs) as i:
                for s in range(2):
                    wait_apart(g, act, scaled[s], i * 2 + 2)
                    for t0, n, c in SEGS:
                        nc.scalar.activation(g.h_hi[:, ds(i * 2 + s), t0:t0 + n].rearrange("p a t -> p (a t)"),
                                             tmp[:, s, t0:t0 + n], ACT.Identity,
                                             bias=shift(i * 2 + s, c)).then_inc(hi_done[s], 1)

        @block.tensor
        def _(pe):
            def add(i, start, stop):
                for s in range(2):
                    pe.wait_ge(squared[s], i + 1)
                    for b, (t0, n) in enumerate(TOK_BLOCKS):
                        last = nc.tensor.matmul(g.bank[b][:, 0:n], g.ones[:, :], sq[:, s, t0:t0 + n],
                                                start=start and s == 0, stop=stop and s == 1)
                    last.then_inc(summed[s], 1)
            add(0, True, False)
            with pe.Fori(1, pairs - 1) as i:
                add(i, False, False)
            add(pairs - 1, False, True)

        @block.vector
        def _(dve):
            for b, (t0, n) in enumerate(TOK_BLOCKS):
                dve.wait_ge(rooted, b + 1)
                nc.vector.reciprocal(rstd[:, t0:t0 + n], root[:, t0:t0 + n]).then_inc(rstd_ready, 1)
            dve.wait_ge(rstd_ready, 3)

            def scale(i):
                for s in range(2):
                    if tail and not first(i):
                        dve.wait_ge(lo_done[s], i * 2)
                    for t0, n, c in SEGS:
                        xs = g.x[:, ds(i * 2 + s), t0:t0 + n].rearrange("p a t -> p (a t)")
                        nc.vector.scalar_tensor_tensor(tmp[:, s, t0:t0 + n] if tail else xs, xs,
                                                       gain_amp(i * 2 + s, c), rstd[:, t0:t0 + n],
                                                       ALU.mult, ALU.mult).then_inc(scaled[s], 1)

            def low(i):
                for s in range(2):
                    dve.wait_ge(hi_done[s], i * 2 + 2)
                    for t0, n, c in SEGS:
                        nc.vector.scalar_tensor_tensor(
                            g.h_lo[:, ds(i * 2 + s), t0:t0 + n].rearrange("p a t -> p (a t)"),
                            tmp[:, s, t0:t0 + n], shift(i * 2 + s, c),
                            g.h_hi[:, ds(i * 2 + s), t0:t0 + n].bitcast(F32).rearrange("p a t -> p (a t)"),
                            ALU.add, ALU.subtract).then_inc(lo_done[s], 1)
            if not tail:
                with dve.Fori(0, pairs) as i:
                    scale(i)
                return
            scale(0)
            with dve.Fori(1, pairs) as i:
                low(i - 1)
                scale(i)
            low(pairs - 1)
            for s in range(2):
                dve.wait_ge(lo_done[s], 2 * pairs)


def split_weights(nc, act, dve, i, s, ring, raw_in, hi_ready, lo_ready, used):
    if act is not None:
        act.wait_ge(raw_in[s], i * 16 + 16)
        if not first(i):
            act.wait_ge(used[s], i)
        nc.scalar.activation(ring.hi[:, s, :], ring.raw[:, s, :], ACT.Copy).then_inc(hi_ready[s], 1)
    if dve is not None:
        dve.wait_ge(hi_ready[s], i + 1)
        nc.vector.tensor_tensor(ring.lo[:, s, :], ring.raw[:, s, :], ring.hi[:, s, :].bitcast(F32),
                                ALU.subtract).then_inc(lo_ready[s], 1)


class Ring:
    def __init__(self, nc, name, kb, raw_slots=2):
        self.raw = at(nc, name + "raw", [P, raw_slots, D_MODEL], F32, kb)
        kb += 4 * raw_slots
        self.hi = at(nc, name + "hi", [P, 2, D_MODEL], F32R, kb)
        self.lo = at(nc, name + "lo", [P, 2, D_MODEL], F32R, kb + 8)


def input_projection(nc, g, a):
    ctx = ExitStack()
    with ctx:
        sem = lambda n: ctx.enter_context(nc.semaphore("in_" + n))
        two = lambda n: [sem(f"{n}{s}") for s in range(2)]
        ring = Ring(nc, "in_", 120)
        stage = at(nc, "in_stage", [P, 2, TOKENS], F32, 144)
        ada_raw = at(nc, "in_ada_raw", [P, 2, D_MODEL], F32, 154)
        cond_s = g.cond_s
        raw_in, hi_ready, lo_ready, used = two("raw_in"), two("hi_ready"), two("lo_ready"), two("used")
        ada_in, ada_used = two("ada_in"), two("ada_used")
        staged, stored = two("staged"), two("stored")
        full = [sem(f"full{b}") for b in range(2)]
        mod_done = sem("mod_done")
        turns = IN_BLOCKS // 2
        block = ctx.enter_context(nc.Block())

        @block.sync
        def _(sp):
            def load(i):
                for s in range(2):
                    if not first(i):
                        sp.wait_ge(lo_ready[s], i)
                    sp.dma_start(ring.raw[:, s, :], a["w_in"][ds(i * 2 + s), :, :].rearrange("a p n -> p (a n)")
                                 ).then_inc(raw_in[s], 16)
                    if not first(i):
                        sp.wait_ge(ada_used[s], i)
                    sp.dma_start(ada_raw[:, s, :], a["w_ada"][ds(16 + i * 2 + s), :, :].rearrange("a p n -> p (a n)")
                                 ).then_inc(ada_in[s], 16)
            peeled(sp, turns, load)

        @block.scalar
        def _(act):
            def split(i, s):
                split_weights(nc, act, None, i, s, ring, raw_in, hi_ready, lo_ready, used)

            def turn(i, last=False):
                for s in range(2):
                    if s == 0:
                        split(i, 1)
                    elif not last:
                        split(i + 1, 0)
                    if not first(i):
                        act.wait_ge(stored[s], i * 16)
                    for b, (t0, n) in enumerate(TOK_BLOCKS):
                        if b < 2:
                            act.wait_ge(full[b], i * 2 + s + 1)
                        else:
                            act.wait_ge(used[s], i + 1)
                        nc.scalar.activation(stage[:, s, t0:t0 + n], g.bank[b][:, 0:n], ACT.Copy
                                             ).then_inc(staged[s], 1)
                    act.wait_ge(staged[s], i * 3 + 3)
                    act.dma_start(g.proj[ds(i * 2 + s), :, :].rearrange("a p n -> p (a n)"), stage[:, s, :]
                                  ).then_inc(stored[s], 16)
            split(0, 0)
            turn(0)
            with act.Fori(1, turns - 1) as i:
                turn(i)
            turn(turns - 1, last=True)
            for s in range(2):
                act.wait_ge(stored[s], turns * 16)

        @block.vector
        def _(dve):
            with dve.Fori(0, turns) as i:
                for s in range(2):
                    split_weights(nc, None, dve, i, s, ring, raw_in, hi_ready, lo_ready, used)
            for s in range(2):
                dve.wait_ge(ada_used[s], turns)
            nc.vector.tensor_tensor(g.mod[:, 16:48, :], g.bank[3][:, 0:64].rearrange("p (j c) -> p j c", c=2),
                                    g.v("b_ada", 16, 32).unsqueeze(2).broadcast_to([P, 32, 2]), ALU.add
                                    ).then_inc(mod_done, 1)
            dve.wait_ge(mod_done, 1)
            nc.vector.scalar_tensor_tensor(g.amp2[:, :, :], g.mod[:, 32:40, :], 1.0,
                                           g.v("norm2", 0, 8).unsqueeze(2).broadcast_to([P, 8, 2]), ALU.add, ALU.mult
                                           ).then_inc(mod_done, 1)
            dve.wait_ge(mod_done, 2)

        @block.tensor
        def _(pe):
            def turn(i):
                for s in range(2):
                    pe.wait_ge(lo_ready[s], i + 1)
                    for b, (t0, n) in enumerate(TOK_BLOCKS):
                        if s == 1:
                            pe.wait_ge(staged[0], i * 3 + b + 1)
                        elif not first(i):
                            pe.wait_ge(staged[1], (i - 1) * 3 + b + 1)
                        for k in range(KT):
                            last = exact_product(nc, g.bank[b][:, 0:n], ring.hi[:, s, k * P:(k + 1) * P],
                                                 ring.lo[:, s, k * P:(k + 1) * P], g.h_hi[:, k, t0:t0 + n],
                                                 g.h_lo[:, k, t0:t0 + n], k == 0, k == KT - 1)
                        last.then_inc(used[s] if b == 2 else full[b], 1)
                    pe.wait_ge(ada_in[s], i * 16 + 16)
                    for k in range(KT):
                        last = nc.tensor.matmul(g.bank[3][:, ds((i * 2 + s) * 2, 2)], ada_raw[:, s, k * P:(k + 1) * P],
                                                cond_s[:, k, :], start=(k == 0), stop=(k == KT - 1))
                    last.then_inc(ada_used[s], 1)
            peeled(pe, turns, turn)


class Banks:

    def __init__(self, sem):
        uses = [(("vt", n), 5 + n) for n in range(3)] + [(("diag",), 0)]
        uses += [(("level", l, d), 1 + (2 * l + d) % 4) for l in range(MASKED) for d in range(DIRS)]
        uses += [(("half32",), 0), (("half64", 0), 5), (("half64", 1), 6)]
        uses += [(("kt", d, n), 1 + i % 4) for i, (d, n) in enumerate(STATE_ORDER)]
        uses += [(("ds", d, n), 5 + i % 3) for i, (d, n) in enumerate(STATE_ORDER)]
        uses += [(("out", n), (3, 4, 0)[n]) for n in range(3)]
        uses += [(("sum", n), 5 + n) for n in range(3)]
        uses += [(("lru", d, ax, b), 1 + (d * 6 + ax * 3 + b) % 4) for d in range(2) for ax in range(2) for b in range(3)]
        self.where, self.count = {}, [0] * 8
        for name, b in uses:
            self.where[name] = (b, self.count[b])
            self.count[b] += 1
        self.full = [sem(f"bank_full{b}") for b in range(8)]
        self.free = [sem(f"bank_free{b}") for b in range(8)]

    def bank(self, name):
        return self.where[name][0]

    def wait_free(self, eng, h, name):
        b, n = self.where[name]
        eng.wait_ge(self.free[b], h * self.count[b] + n + 1)

    def wait_full(self, eng, h, name):
        b, n = self.where[name]
        eng.wait_ge(self.full[b], h * self.count[b] + n + 1)

    def wait_read(self, eng, h, name):
        b, n = self.where[name]
        eng.wait_ge(self.free[b], h * self.count[b] + n + 2)

    def filled(self, ins, name):
        ins.then_inc(self.full[self.bank(name)], 1)

    def read(self, ins, name):
        ins.then_inc(self.free[self.bank(name)], 1)


STATE_ORDER = ((0, 0), (1, 0), (0, 1), (1, 2), (0, 2), (1, 1))


def state_steps(d, n):
    c0, k = GROUPS[n]
    steps = []
    for c in (range(c0, c0 + k) if d == 0 else reversed(range(c0, c0 + k))):
        if c == (1, 0)[d]:
            steps.append((c, None))
        elif c != (CHUNKS - 1, CTX_CHUNKS)[d]:
            steps.append((c, c + 1 - 2 * d))
    return steps


CONV_N = 8
SERIES = 8
SMALL_STEPS = 4 + 2 + 5 + (SERIES - 1) + 4


def small_constants(nc, dve, g, small, done, from_act):
    count = [0]

    def link(ins):
        count[0] += 1
        ins.then_inc(done, 1)
        dve.wait_ge(done, count[0])
    t = lambda i: small[:, i, :]
    vec = nc.vector
    lam = g.vecs[:, VEC["lam"]:VEC["lam"] + 8]
    link(vec.tensor_tensor(t(5), g.vecs[:, VEC["lb"]:VEC["lb"] + 8], g.vecs[:, VEC["lb"] + 8:VEC["lb"] + 16],
                           ALU.subtract))
    link(vec.tensor_scalar(t(8), lam, -1.0, None, ALU.mult))
    link(vec.tensor_tensor(t(6), lam, t(8), ALU.max))
    link(vec.tensor_scalar(t(8), t(8), 0.0, None, ALU.max))
    dve.wait_ge(from_act, 1)
    link(vec.tensor_scalar(t(1), t(0), -1.0, 1.0, ALU.mult, ALU.add))
    link(vec.tensor_scalar(t(2), t(0), 1.0, -1.0, ALU.mult, ALU.add))
    dve.wait_ge(from_act, 2)
    link(vec.tensor_scalar(t(9), t(7), 2.0, None, ALU.add))
    link(vec.reciprocal(t(10), t(9)))
    link(vec.tensor_tensor(t(11), t(7), t(10), ALU.mult))
    link(vec.tensor_tensor(t(12), t(11), t(11), ALU.mult))
    link(vec.tensor_scalar(t(13), t(12), 1.0 / (2 * SERIES + 1), None, ALU.mult))
    for n in range(SERIES - 1, 0, -1):
        link(vec.scalar_tensor_tensor(t(13), t(13), 1.0 / (2 * n + 1), t(12), ALU.add, ALU.mult))
    link(vec.scalar_tensor_tensor(t(13), t(13), 1.0, t(11), ALU.add, ALU.mult))
    link(vec.scalar_tensor_tensor(t(13), t(13), 2.0, t(8), ALU.mult, ALU.add))
    link(vec.tensor_scalar(t(3), t(13), LRU_C, None, ALU.mult))
    link(vec.tensor_scalar(t(4), t(13), -LRU_C, None, ALU.mult))
    assert count[0] == SMALL_STEPS


def mixers(nc, g, a):
    ctx = ExitStack()
    with ctx:
        ctx.enter_context(nc.cleanup_on_exit())
        sem = lambda n: nc.alloc_semaphore("mx_" + n)
        buf = lambda n, shape, kb, dt=F32: at(nc, "mx_" + n, shape, dt, kb)
        row = [P, TOKENS]
        q = [buf("q0", row, 0), buf("q1", row, 10)]
        f = [buf("f0", row, 5), buf("f1", row, 15)]
        v, gate, lx, lg = buf("v", row, 20), buf("gate", row, 25), buf("lx", row, 30), buf("lg", row, 35)
        tiles = {T_LX: lx, T_LG: lg, T_V: v, T_GATE: gate, T_Q0: q[0], T_F0: f[0], T_Q1: q[1], T_F1: f[1]}
        k = [buf("k0", row, 40), buf("k1", row, 45)]
        tot = [buf("tot0", row, 50), buf("tot1", row, 55)]
        diag = buf("diag", [P, CHUNKS, 32], 60)
        scores = buf("scores", [P, CHUNKS, P], 62)
        v_tok = buf("v_tok", [P, CHUNKS, P], 67)
        k_tok = [buf("k_tok0", [P, CHUNKS, P], 72), buf("k_tok1", [P, CHUNKS, P], 77)]
        state = [buf("state0", [P, CHUNKS, P], 82), buf("state1", [P, CHUNKS, P], 87)]
        last_state = [buf("last0", [P, P], 92), buf("last1", [P, P], 92.5)]
        lru_w = buf("lru_w", [P, 4, P], 93)
        masks = buf("masks", [P, MASKS, 32], 95)
        small = buf("small", [P, 16, 8], 97)
        root, rstd, normed = buf("root", row, 98), buf("rstd", row, 103), buf("normed", row, 153)
        xc = buf("xc", row, 108)
        r = [buf("r0", row, 113), buf("r1", row, 118)]
        ig = [buf("ig0", row, 123), buf("ig1", row, 128)]
        dec = [buf("dec0", row, 133), buf("dec1", row, 138)]
        sq = [buf("sq0", row, 143), buf("sq1", row, 148)]
        new_lru = buf("new_lru", [P, 8], 61.5)
        gate_bias = buf("gate_bias", [P, 4], 61.75)
        lb, one_lb, neg_lb, rate, neg_rate = (small[:, i, :] for i in range(5))

        bk = Banks(sem)
        tile_in = {t: sem(f"tile_in{t}") for t in tiles}
        const_in, states_in, lru_w_in = sem("const_in"), sem("states_in"), sem("lru_w_in")
        zeroed, small_act, small_dve = sem("zeroed"), sem("small_act"), sem("small_dve")
        sig_ready, q_ready, gate_ready = sem("sig_ready"), sem("q_ready"), sem("gate_ready")
        kf_ready, qk_ready, tot_ready, placed = sem("kf_ready"), sem("qk_ready"), sem("tot_ready"), sem("placed")
        state_step, squared, rstd_ready, normed_ready = (
            sem("state_step"), sem("squared"), sem("rstd_ready"), sem("normed_ready"))
        head_done, tile_done, last_stored = sem("head_done"), sem("tile_done"), sem("last_stored")
        conv, lru_exp, ix_ready, gap_ready, gap_root, u_ready, scanned, geglu = (
            sem("conv"), sem("lru_exp"), sem("ix_ready"), sem("gap_ready"), sem("gap_root"), sem("u_ready"),
            sem("scanned"), sem("gelu"))
        lru_stored = sem("lru_stored")
        QK_N = 2 + LEVELS * DIRS * 2

        def qk_count(level, d):
            return 1 + d if level == 0 else 2 + (2 * (level - 1) + d) * 2 + 2

        block = ctx.enter_context(nc.Block())

        @block.sync
        def _(sp):
            sp.dma_start(masks[:, :, :], a["masks"]).then_inc(const_in, 16)
            sp.wait_ge(zeroed, 3)

            def head(h):
                if not first(h):
                    sp.wait_ge(head_done, h * 3)
                for t in (T_F0, T_F1, T_Q0, T_Q1, T_V, T_GATE):
                    sp.dma_start(tiles[t][:, :], g.proj[ds(h * PER_HEAD + t), :, :].rearrange("a p n -> p (a n)")
                                 ).then_inc(tile_in[t], 16)
                if not first(h):
                    sp.wait_ge(last_stored, h * 32)
                for d, c in ((0, CTX_CHUNKS), (1, CHUNKS - 1)):
                    sp.dma_start(state[d][:, c, :], a["state_hgrn"][d, ds(h), :, :].rearrange("a p n -> p (a n)")
                                 ).then_inc(states_in, 16)
                if not first(h):
                    sp.wait_ge(tile_done, h)
                for t in (T_LX, T_LG):
                    sp.dma_start(tiles[t][:, :], g.proj[ds(h * PER_HEAD + t), :, :].rearrange("a p n -> p (a n)")
                                 ).then_inc(tile_in[t], 16)
                for ax, w in enumerate(("lru_wa", "lru_wx")):
                    for half in range(2):
                        part = slice(64 * half, 64 * half + 64)
                        sp.dma_start(lru_w[part, 2 * ax:2 * ax + 2, part],
                                     a[w][:, ds(h * 2 + half), :, :].rearrange("r a d e -> d (r a) e")
                                     ).then_inc(lru_w_in, 16)
                for d in range(DIRS):
                    bk.wait_read(sp, h, ("ds", d, 0))
                    sp.dma_start(a["new_hgrn"][d, ds(h), :, :].rearrange("a p n -> p (a n)"), last_state[d][:, :]
                                 ).then_inc(last_stored, 16)
            head(0)
            with sp.Fori(1, HEADS) as h:
                head(h)
            sp.wait_ge(last_stored, HEADS * 32)
            sp.wait_ge(tile_done, HEADS)
            sp.dma_start(a["new_lru"], new_lru[:, :]).then_inc(lru_stored, 16)
            sp.wait_ge(lru_stored, 16)

        @block.scalar
        def _(act):
            act.wait_ge(small_dve, 3)
            nc.scalar.activation(lb, small[:, 5, :], ACT.Sigmoid).then_inc(small_act, 1)
            nc.scalar.activation(small[:, 7, :], small[:, 6, :], ACT.Exp, scale=-1.0).then_inc(small_act, 1)
            with act.Fori(0, HEADS) as h:
                for d in range(DIRS):
                    act.wait_ge(tile_in[(T_F0, T_F1)[d]], h * 16 + 16)
                    nc.scalar.activation(f[d][:, :], f[d][:, :], ACT.Sigmoid).then_inc(sig_ready, 1)
                for d in range(DIRS):
                    act.wait_ge(tile_in[(T_Q0, T_Q1)[d]], h * 16 + 16)
                    nc.scalar.activation(q[d][:, :], q[d][:, :], ACT.Silu).then_inc(q_ready, 1)
                act.wait_ge(tile_in[T_GATE], h * 16 + 16)
                nc.scalar.activation(gate[:, :], gate[:, :], ACT.Silu).then_inc(gate_ready, 1)
                for n, (c0, kc) in enumerate(GROUPS):
                    bk.wait_full(act, h, ("vt", n))
                    bk.read(nc.scalar.activation(v_tok[:, c0:c0 + kc, :].rearrange("p c k -> p (c k)"),
                                                 g.bank[bk.bank(("vt", n))][:, 0:kc * P], ACT.Copy), ("vt", n))
                bk.wait_full(act, h, ("half32",))
                for j in range(4):
                    rows, cols = slice(32 * j, 32 * j + 32), slice(32 * (j ^ 1), 32 * (j ^ 1) + 32)
                    ins = nc.scalar.activation(scores[rows, :, cols], g.bank[0][rows, 0:CHUNKS * 32].rearrange(
                        "p (c t) -> p c t", t=32), ACT.Copy)
                bk.read(ins, ("half32",))
                for part in range(2):
                    bk.wait_full(act, h, ("half64", part))
                    for j in range(2):
                        rows, cols = slice(64 * j, 64 * j + 64), slice(64 * (1 - j), 64 * (1 - j) + 64)
                        ins = nc.scalar.activation(
                            scores[rows, 5 * part:5 * part + 5, cols],
                            g.bank[bk.bank(("half64", part))][rows, 0:320].rearrange("p (c t) -> p c t", t=64), ACT.Copy)
                    bk.read(ins, ("half64", part))
                bk.wait_read(act, h, ("level", MASKED - 1, 1))
                for j in range(4):
                    rows = slice(32 * j, 32 * j + 32)
                    ins = nc.scalar.activation(scores[rows, :, rows], diag[rows, :, :], ACT.Copy)
                ins.then_inc(placed, 1)
                for d, n in STATE_ORDER:
                    c0, kc = GROUPS[n]
                    bk.wait_full(act, h, ("kt", d, n))
                    bk.read(nc.scalar.activation(k_tok[d][:, c0:c0 + kc, :].rearrange("p c k -> p (c k)"),
                                                 g.bank[bk.bank(("kt", d, n))][:, 0:kc * P], ACT.Copy), ("kt", d, n))
                for n, (t0, tn) in enumerate(TOK_BLOCKS):
                    bk.wait_full(act, h, ("out", n))
                    nc.scalar.activation(normed[:, t0:t0 + tn], g.bank[bk.bank(("out", n))][:, 0:tn], ACT.Square
                                         ).then_inc(squared, 1)
                for n, (t0, tn) in enumerate(TOK_BLOCKS):
                    bk.wait_full(act, h, ("sum", n))
                    bk.read(nc.scalar.activation(root[:, t0:t0 + tn], g.bank[bk.bank(("sum", n))][:, 0:tn], ACT.Sqrt,
                                                 bias=g.eps[:, 0:1], scale=1.0 / P), ("sum", n))
                for d in range(DIRS):
                    for ax in range(2):
                        for n, (t0, tn) in enumerate(TOK_BLOCKS):
                            name = ("lru", d, ax, n)
                            bk.wait_full(act, h, name)
                            bk.read(nc.scalar.activation((r, ig)[ax][d][:, t0:t0 + tn], g.bank[bk.bank(name)][:, 0:tn],
                                                         ACT.Sigmoid, bias=gate_bias[:, 2 * ax + d:2 * ax + d + 1]), name)
                bk.wait_read(act, h, ("lru", 1, 0, 2))
                act.wait_ge(small_dve, SMALL_STEPS)
                for d in range(DIRS):
                    nc.scalar.activation(dec[d][:, :], r[d][:, :], ACT.Exp, scale=neg_rate[:, ds(h + 4 * d)]
                                         ).then_inc(lru_exp, 1)
                    nc.scalar.activation(r[d][:, :], r[d][:, :], ACT.Tanh, scale=rate[:, ds(h + 4 * d)]
                                         ).then_inc(lru_exp, 1)
                    act.wait_ge(lru_exp, h * 6 + 3 * d + 1)
                    nc.scalar.activation(sq[d][:, :], dec[d][:, :], ACT.Square).then_inc(lru_exp, 1)
                for d in range(DIRS):
                    act.wait_ge(gap_ready, h * 2 + d + 1)
                    nc.scalar.activation(sq[d][:, :], sq[d][:, :], ACT.Sqrt).then_inc(gap_root, 1)
                act.wait_ge(tile_in[T_LG], h * 16 + 16)
                nc.scalar.activation(lg[:, :], lg[:, :], ACT.Gelu_apprx_tanh).then_inc(geglu, 1)

        @block.tensor
        def _(pe):
            pe.wait_ge(zeroed, 3)

            def blocks(tensor, c, size, j):
                return tensor[:, c * P + size * j:c * P + size * j + size]

            with pe.Fori(0, HEADS) as h:
                pe.wait_ge(tile_in[T_V], h * 16 + 16)
                for n, (c0, kc) in enumerate(GROUPS):
                    bk.wait_free(pe, h, ("vt", n))
                    for c in range(kc):
                        ins = nc.tensor.transpose(g.bank[bk.bank(("vt", n))][:, c * P:(c + 1) * P],
                                                  v[:, (c0 + c) * P:(c0 + c + 1) * P], g.ident[:, :])
                    bk.filled(ins, ("vt", n))
                bk.wait_free(pe, h, ("diag",))
                pe.wait_ge(q_ready, h * 2 + 2)
                pe.wait_ge(kf_ready, h * 4 + 4)
                for c in range(CHUNKS):
                    for j in range(4):
                        for d in range(DIRS):
                            ins = nc.tensor.matmul(g.bank[0][32 * j:32 * j + 32, c * 32:(c + 1) * 32],
                                                   blocks(k[d], c, 32, j), blocks(q[d], c, 32, j),
                                                   start=(d == 0), stop=(d == 1))
                bk.filled(ins, ("diag",))
                for level in range(MASKED):
                    for d in range(DIRS):
                        name = ("level", level, d)
                        bk.wait_free(pe, h, name)
                        pe.wait_ge(qk_ready, h * QK_N + qk_count(level, d))
                        for c in range(CHUNKS):
                            for j in range(4):
                                ins = nc.tensor.matmul(g.bank[bk.bank(name)][32 * j:32 * j + 32, c * 32:(c + 1) * 32],
                                                       blocks(k[d], c, 32, j), blocks(q[d], c, 32, j),
                                                       start=True, stop=True)
                        bk.filled(ins, name)
                bk.wait_free(pe, h, ("half32",))
                pe.wait_ge(qk_ready, h * QK_N + qk_count(MASKED, 1))
                for c in range(CHUNKS):
                    for j in range(4):
                        d = j % 2
                        ins = nc.tensor.matmul(g.bank[0][32 * j:32 * j + 32, c * 32:(c + 1) * 32],
                                               blocks(k[d], c, 32, j), blocks(q[d], c, 32, j ^ 1), start=True, stop=True)
                bk.filled(ins, ("half32",))
                pe.wait_ge(qk_ready, h * QK_N + qk_count(MASKED + 1, 1))
                for part in range(2):
                    name = ("half64", part)
                    bk.wait_free(pe, h, name)
                    for c in range(5):
                        for d in range(DIRS):
                            ins = nc.tensor.matmul(g.bank[bk.bank(name)][64 * d:64 * d + 64, c * 64:(c + 1) * 64],
                                                   blocks(k[d], 5 * part + c, 64, d),
                                                   blocks(q[d], 5 * part + c, 64, 1 - d), start=True, stop=True)
                    bk.filled(ins, name)
                pe.wait_ge(qk_ready, h * QK_N + QK_N)
                for d, n in STATE_ORDER:
                    c0, kc = GROUPS[n]
                    name = ("kt", d, n)
                    bk.wait_free(pe, h, name)
                    for c in range(kc):
                        ins = nc.tensor.transpose(g.bank[bk.bank(name)][:, c * P:(c + 1) * P],
                                                  k[d][:, (c0 + c) * P:(c0 + c + 1) * P], g.ident[:, :])
                    bk.filled(ins, name)
                for d, n in STATE_ORDER:
                    c0, kc = GROUPS[n]
                    name = ("ds", d, n)
                    bk.wait_read(pe, h, ("kt", d, n))
                    bk.wait_free(pe, h, name)
                    for c in range(kc):
                        ins = nc.tensor.matmul(g.bank[bk.bank(name)][:, c * P:(c + 1) * P], k_tok[d][:, c0 + c, :],
                                               v_tok[:, c0 + c, :], start=True, stop=True)
                    bk.filled(ins, name)
                pe.wait_ge(placed, h + 1)
                pe.wait_ge(states_in, h * 32 + 32)
                for n, (c0, kc) in enumerate(GROUPS):
                    name = ("out", n)
                    bk.wait_free(pe, h, name)
                    bk.wait_read(pe, h, ("ds",) + ((1, 0), (1, 1), (0, 2))[n])
                    for c in range(kc):
                        out = g.bank[bk.bank(name)][:, c * P:(c + 1) * P]
                        at_c = slice((c0 + c) * P, (c0 + c + 1) * P)
                        nc.tensor.matmul(out, v_tok[:, c0 + c, :], scores[:, c0 + c, :], start=True, stop=False)
                        nc.tensor.matmul(out, state[0][:, c0 + c, :], q[0][:, at_c], start=False, stop=False)
                        ins = nc.tensor.matmul(out, state[1][:, c0 + c, :], q[1][:, at_c], start=False, stop=True)
                    bk.filled(ins, name)
                for n, (t0, tn) in enumerate(TOK_BLOCKS):
                    bk.wait_free(pe, h, ("sum", n))
                    pe.wait_ge(squared, h * 3 + n + 1)
                    bk.filled(nc.tensor.matmul(g.bank[bk.bank(("sum", n))][:, 0:tn], g.ones[:, :],
                                               normed[:, t0:t0 + tn], start=True, stop=True), ("sum", n))
                pe.wait_ge(conv, h * CONV_N + CONV_N)
                pe.wait_ge(lru_w_in, h * 64 + 64)
                for d in range(DIRS):
                    for ax in range(2):
                        for n, (t0, tn) in enumerate(TOK_BLOCKS):
                            name = ("lru", d, ax, n)
                            bk.wait_free(pe, h, name)
                            bk.filled(nc.tensor.matmul(g.bank[bk.bank(name)][:, 0:tn], lru_w[:, 2 * ax + d, :],
                                                       xc[:, t0:t0 + tn], start=True, stop=True), name)

        @block.vector
        def _(dve):
            for free in bk.free:
                dve.sem_inc(free, 1)
            nc.vector.memset(state[0][:, 0, :], 0.0).then_inc(zeroed, 1)
            nc.vector.memset(state[1][:, CTX_CHUNKS - 1, :], 0.0).then_inc(zeroed, 1)
            nc.vector.memset(lru_w[:, :, :], 0.0).then_inc(zeroed, 1)
            small_constants(nc, dve, g, small, small_dve, small_act)
            dve.wait_ge(const_in, 16)

            with dve.Fori(0, HEADS) as h:
                for d in range(DIRS):
                    at_h = ds(h + 4 * d)
                    dve.wait_ge(sig_ready, h * 2 + d + 1)
                    nc.vector.tensor_scalar(k[d][:, :], f[d][:, :], neg_lb[:, at_h], one_lb[:, at_h],
                                            ALU.mult, ALU.add).then_inc(kf_ready, 1)
                    nc.vector.tensor_scalar(f[d][:, :], f[d][:, :], one_lb[:, at_h], lb[:, at_h],
                                            ALU.mult, ALU.add).then_inc(kf_ready, 1)
                bk.wait_full(dve, h, ("diag",))
                for d in range(DIRS):
                    dve.wait_ge(kf_ready, h * 4 + 2 * d + 2)
                    nc.vector.tensor_tensor(q[d][:, :], q[d][:, :], f[d][:, :], ALU.mult).then_inc(qk_ready, 1)
                bk.read(nc.vector.tensor_tensor(diag[:, :, :], g.bank[0][:, 0:CHUNKS * 32].rearrange(
                    "p (c t) -> p c t", t=32), masks[:, 0:1, :].broadcast_to([P, CHUNKS, 32]), ALU.mult), ("diag",))
                done, previous = 0, ("diag",)
                for level in range(LEVELS):
                    size = 2 ** level
                    pairs = TOKENS // (2 * size)
                    src = sum(TOKENS >> i for i in range(1, level))
                    dst = sum(TOKENS >> i for i in range(1, level + 1))
                    for d in range(DIRS):
                        if level < MASKED:
                            bk.wait_full(dve, h, ("level", level, d))
                        elif level == MASKED:
                            bk.wait_full(dve, h, ("half32",))
                        else:
                            bk.wait_full(dve, h, ("half64", 0))
                            bk.wait_full(dve, h, ("half64", 1))
                        totals = f[d][:, :] if level == 0 else tot[d][:, src:src + 2 * pairs]
                        totals = totals.rearrange("p (n two) -> p n two", two=2)
                        if level:
                            dve.wait_ge(tot_ready, h * 14 + 2 * (level - 1) + d + 1)
                        for t, half in ((q[d], 1 - d), (k[d], d)):
                            part = t[:, :].rearrange("p (n two b) -> p n two b", two=2, b=size)[:, :, half, :]
                            nc.vector.tensor_tensor(part, part, totals[:, :, 1 - half:2 - half].broadcast_to(
                                [P, pairs, size]), ALU.mult).then_inc(qk_ready, 1)
                        new = tot[d][:, dst:dst + pairs] if level else tot[d][:, 0:pairs]
                        if level < MASKED:
                            bk.wait_read(dve, h, previous)
                        nc.vector.tensor_tensor(new, totals[:, :, 0], totals[:, :, 1], ALU.mult).then_inc(tot_ready, 1)
                        if level < MASKED:
                            name = ("level", level, d)
                            bk.read(nc.vector.copy_predicated(
                                diag[:, :, :],
                                masks[:, 1 + done:2 + done, :].bitcast(I32).broadcast_to([P, CHUNKS, 32]),
                                g.bank[bk.bank(name)][:, 0:CHUNKS * 32].rearrange("p (c t) -> p c t", t=32)), name)
                            previous = name
                            done += 1

                last_tot = sum(TOKENS >> i for i in range(1, LEVELS))
                steps = 0
                for d, n in STATE_ORDER:
                    name = ("ds", d, n)
                    bk.wait_full(dve, h, name)
                    if n == 0:
                        dve.wait_ge(states_in, h * 32 + 32)
                        dve.wait_ge(tot_ready, h * 14 + 13 + d)
                    else:
                        before = [m for e, m in STATE_ORDER if e == d]
                        bk.wait_read(dve, h, ("ds", d, before[before.index(n) - 1]))
                    todo = state_steps(d, n)
                    for i, (c, into) in enumerate(todo):
                        if i:
                            dve.wait_ge(state_step, h * STATE_STEPS + steps)
                        c_in = c - GROUPS[n][0]
                        ins = nc.vector.scalar_tensor_tensor(
                            last_state[d][:, :] if into is None else state[d][:, into, :], state[d][:, c, :],
                            tot[d][:, last_tot + c:last_tot + c + 1],
                            g.bank[bk.bank(name)][:, c_in * P:(c_in + 1) * P], ALU.mult, ALU.add)
                        if i == len(todo) - 1:
                            bk.read(ins, name)
                        else:
                            ins.then_inc(state_step, 1)
                            steps += 1
                assert steps == STATE_STEPS
                for n, (t0, tn) in enumerate(TOK_BLOCKS):
                    bk.wait_read(dve, h, ("sum", n))
                    nc.vector.reciprocal(rstd[:, t0:t0 + tn], root[:, t0:t0 + tn]).then_inc(rstd_ready, 1)
                dve.wait_ge(gate_ready, h + 1)
                for n, (t0, tn) in enumerate(TOK_BLOCKS):
                    dve.wait_ge(rstd_ready, h * 3 + n + 1)
                    bk.read(nc.vector.scalar_tensor_tensor(
                        normed[:, t0:t0 + tn], g.bank[bk.bank(("out", n))][:, 0:tn], g.v("hg_gain", h),
                        rstd[:, t0:t0 + tn], ALU.mult, ALU.mult), ("out", n))
                for n, (t0, tn) in enumerate(TOK_BLOCKS):
                    bk.wait_read(dve, h, ("out", n))
                    nc.vector.tensor_tensor(g.mix[:, ds(h), t0:t0 + tn].rearrange("p a t -> p (a t)"),
                                            normed[:, t0:t0 + tn], gate[:, t0:t0 + tn], ALU.mult
                                            ).then_inc(head_done, 1)

                dve.wait_ge(tile_in[T_LX], h * 16 + 16)
                nc.vector.tensor_scalar(xc[:, :], lx[:, :], g.v("conv_w", h + 4 * CONV_LEFT), g.v("conv_b", h),
                                        ALU.mult, ALU.add).then_inc(conv, 1)
                done = 1
                for tap in (0, 1, 3):
                    shift = tap - CONV_LEFT
                    dve.wait_ge(conv, h * CONV_N + done)
                    for t0, tn, _ in SEGS:
                        lo, hi = t0 + max(0, -shift), t0 + tn - max(0, shift)
                        nc.vector.scalar_tensor_tensor(xc[:, lo:hi], lx[:, lo + shift:hi + shift],
                                                       g.v("conv_w", h + 4 * tap), xc[:, lo:hi], ALU.mult, ALU.add
                                                       ).then_inc(conv, 1)
                        done += 1
                assert done == CONV_N - 1
                nc.vector.tensor_copy(gate_bias[:, :], g.vecs[:, VEC["ba"]:VEC["ba"] + 16].rearrange(
                    "p (n t) -> p n t", t=HEADS)[:, :, ds(h)].rearrange("p n a -> p (n a)")).then_inc(conv, 1)
                dve.wait_ge(conv, h * CONV_N + CONV_N)
                for d in range(DIRS):
                    bk.wait_read(dve, h, ("lru", d, 1, 2))
                    for n in range(2):
                        bk.wait_read(dve, h, ("lru", d, 1, n))
                    nc.vector.tensor_tensor(ig[d][:, :], ig[d][:, :], xc[:, :], ALU.mult).then_inc(ix_ready, 1)
                for d in range(DIRS):
                    dve.wait_ge(lru_exp, h * 6 + 3 * d + 3)
                    nc.vector.scalar_tensor_tensor(sq[d][:, :], sq[d][:, :], 1.0, r[d][:, :], ALU.add, ALU.mult
                                                   ).then_inc(gap_ready, 1)
                for d in range(DIRS):
                    dve.wait_ge(gap_root, h * 2 + d + 1)
                    dve.wait_ge(ix_ready, h * 2 + d + 1)
                    nc.vector.tensor_tensor(ig[d][:, :], ig[d][:, :], sq[d][:, :], ALU.mult).then_inc(u_ready, 1)
                for d in range(DIRS):
                    dve.wait_ge(u_ready, h * 2 + d + 1)
                    for t0, tn, c in SEGS:
                        view = lambda t: t[:, t0:t0 + tn] if d == 0 else t[:, t0:t0 + tn][:, ::-1]
                        nc.vector.tensor_tensor_scan(view(r[d]), view(dec[d]), view(ig[d]),
                                                     g.v("h0", h + 4 * d) if c else 0.0, ALU.mult, ALU.add
                                                     ).then_inc(scanned, 1)
                dve.wait_ge(scanned, h * 7 + 4)
                for d, t in ((0, CTX - 1), (1, 0)):
                    nc.vector.tensor_copy(new_lru[:, ds(h + 4 * d)], r[d][:, t:t + 1]).then_inc(scanned, 1)
                dve.wait_ge(scanned, h * 7 + 6)
                nc.vector.tensor_tensor(r[0][:, :], r[0][:, :], r[1][:, :], ALU.add).then_inc(scanned, 1)
                dve.wait_ge(scanned, h * 7 + 7)
                dve.wait_ge(geglu, h + 1)
                nc.vector.tensor_tensor(g.mix[:, ds(h + HEADS), :].rearrange("p a t -> p (a t)"), r[0][:, :],
                                        lg[:, :], ALU.mult).then_inc(tile_done, 1)


STATE_STEPS = sum(len(state_steps(d, n)) - 1 for d, n in STATE_ORDER)


def output_projection(nc, g, a):
    ctx = ExitStack()
    with ctx:
        sem = lambda n: ctx.enter_context(nc.semaphore("out_" + n))
        two = lambda n: [sem(f"{n}{s}") for s in range(2)]
        ring = Ring(nc, "out_", 120)
        raw_in, hi_ready, lo_ready, used = two("raw_in"), two("hi_ready"), two("lo_ready"), two("used")
        x_in, mix_hi, mix_lo = sem("x_in"), sem("mix_hi"), sem("mix_lo")
        full = [sem(f"full{b}") for b in range(2)]
        added = sem("added")
        turns = KT // 2
        block = ctx.enter_context(nc.Block())

        @block.sync
        def _(sp):
            sp.dma_start(g.x[:, :, :].rearrange("p k t -> p (k t)"), g.x_scratch).then_inc(x_in, 16)

            def load(i):
                for s in range(2):
                    if not first(i):
                        sp.wait_ge(lo_ready[s], i)
                    sp.dma_start(ring.raw[:, s, :], a["w_out"][ds(i * 2 + s), :, :].rearrange("a p n -> p (a n)")
                                 ).then_inc(raw_in[s], 16)
            peeled(sp, turns, load)

        @block.scalar
        def _(act):
            with act.Fori(0, KT) as t:
                nc.scalar.activation(g.h_hi[:, ds(t), :], g.mix[:, ds(t), :], ACT.Copy).then_inc(mix_hi, 1)

            def turn(i):
                for s in range(2):
                    split_weights(nc, act, None, i, s, ring, raw_in, hi_ready, lo_ready, used)
            peeled(act, turns, turn)

        @block.vector
        def _(dve):
            with dve.Fori(0, KT) as t:
                dve.wait_ge(mix_hi, t + 1)
                nc.vector.tensor_tensor(g.h_lo[:, ds(t), :], g.mix[:, ds(t), :], g.h_hi[:, ds(t), :].bitcast(F32),
                                        ALU.subtract).then_inc(mix_lo, 1)
            dve.wait_ge(x_in, 16)
            split_weights(nc, None, dve, 0, 0, ring, raw_in, hi_ready, lo_ready, used)

            def turn(i, last=False):
                for s in range(2):
                    if not (last and s):
                        split_weights(nc, None, dve, i + s, 1 - s, ring, raw_in, hi_ready, lo_ready, used)
                    for b, (t0, n) in enumerate(TOK_BLOCKS):
                        if b < 2:
                            dve.wait_ge(full[b], i * 2 + s + 1)
                        else:
                            dve.wait_ge(used[s], i + 1)
                        xs = g.x[:, ds(i * 2 + s), t0:t0 + n].rearrange("p a t -> p (a t)")
                        nc.vector.scalar_tensor_tensor(xs, g.bank[b][:, 0:n], g.m(16 + i * 2 + s, int(b > 0)), xs,
                                                       ALU.mult, ALU.add).then_inc(added, 1)
            with dve.Fori(0, turns - 1) as i:
                turn(i)
            turn(turns - 1, last=True)
            dve.wait_ge(added, 3 * KT)

        @block.tensor
        def _(pe):
            pe.wait_ge(mix_lo, KT)

            def turn(i):
                for s in range(2):
                    pe.wait_ge(lo_ready[s], i + 1)
                    for b, (t0, n) in enumerate(TOK_BLOCKS):
                        if not (first(i) and s == 0):
                            pe.wait_ge(added, (i * 2 + s - 1) * 3 + b + 1)
                        for k in range(KT):
                            last = exact_product(nc, g.bank[b][:, 0:n], ring.hi[:, s, k * P:(k + 1) * P],
                                                 ring.lo[:, s, k * P:(k + 1) * P], g.h_hi[:, k, t0:t0 + n],
                                                 g.h_lo[:, k, t0:t0 + n], k == 0, k == KT - 1)
                        last.then_inc(used[s] if b == 2 else full[b], 1)
            peeled(pe, turns, turn)


def mlp(nc, g, a):
    ctx = ExitStack()
    with ctx:
        sem = lambda n: ctx.enter_context(nc.semaphore("ff_" + n))
        two = lambda n: [sem(f"{n}{s}") for s in range(2)]
        up = Ring(nc, "up_", 120)
        down = Ring(nc, "down_", 144, raw_slots=1)
        hid_hi = at(nc, "hid_hi", [P, 4, TOKENS], F32R, 164)
        hid_lo = at(nc, "hid_lo", [P, 4, TOKENS], F32R, 184)
        hid_relu = at(nc, "hid_relu", [P, 4, TOKENS], F32, 184)
        up_in, up_hi, up_lo, up_used = two("up_in"), two("up_hi"), two("up_lo"), two("up_used")
        down_in, down_hi, down_lo = sem("down_in"), sem("down_hi"), sem("down_lo")
        full = [sem(f"full{b}") for b in range(2)]
        relu_ready, squared, hid_hi_ready, hid_lo_ready = (
            sem("relu_ready"), sem("squared"), sem("hid_hi_ready"), sem("hid_lo_ready"))
        DOWN_BANKS = 4
        UNITS = KT * 3
        unit_full = [sem(f"unit_full{u}") for u in range(DOWN_BANKS)]
        unit_added = [sem(f"unit_added{u}") for u in range(DOWN_BANKS)]
        PER = UNITS // DOWN_BANKS
        pairs = FF_BLOCKS // 2
        block = ctx.enter_context(nc.Block())

        def over_pairs(eng, step):
            step(0, 0)
            step(1, 1)
            with eng.Fori(1, (pairs - 2) // 2) as i:
                step(i * 2, 0)
                step(i * 2 + 1, 1)
            step(pairs - 2, 0)

        @block.sync
        def _(sp):
            def load_up(p, s):
                if not first(p):
                    sp.wait_ge(up_lo[s], p)
                sp.dma_start(up.raw[:, s, :], a["w_ff1"][ds(p * 2 + s), :, :].rearrange("a p n -> p (a n)")
                             ).then_inc(up_in[s], 16)

            def load_down(p, s):
                if not (first(p) and s == 0):
                    sp.wait_ge(down_lo, p * 2 + s)
                sp.dma_start(down.raw[:, 0, :], a["w_ff2"][ds(p * 2 + s), :, :].rearrange("a p n -> p (a n)")
                             ).then_inc(down_in, 16)

            for s in range(2):
                load_up(0, s)
            for s in range(2):
                load_up(1, s)
            load_down(0, 0)
            load_down(0, 1)

            def step(p, parity):
                for s in range(2):
                    load_up(p + 2, s)
                for s in range(2):
                    load_down(p + 1, s)
            with sp.Fori(0, pairs - 2) as p:
                step(p, 0)
            for s in range(2):
                load_down(pairs - 1, s)

        def up_weights(p, s, act=None, dve=None):
            if act is not None:
                act.wait_ge(up_in[s], p * 16 + 16)
                if not first(p):
                    act.wait_ge(up_used[s], p)
                nc.scalar.activation(up.hi[:, s, :], up.raw[:, s, :], ACT.Copy).then_inc(up_hi[s], 1)
            else:
                dve.wait_ge(up_hi[s], p + 1)
                nc.vector.tensor_tensor(up.lo[:, s, :], up.raw[:, s, :], up.hi[:, s, :].bitcast(F32), ALU.subtract
                                        ).then_inc(up_lo[s], 1)

        def down_weights(p, s, act=None, dve=None):
            if act is not None:
                act.wait_ge(down_in, (p * 2 + s) * 16 + 16)
                if not first(p):
                    act.wait_ge(unit_full[(UNITS - 1) % DOWN_BANKS], p * PER)
                nc.scalar.activation(down.hi[:, s, :], down.raw[:, 0, :], ACT.Copy).then_inc(down_hi, 1)
            else:
                dve.wait_ge(down_hi, p * 2 + s + 1)
                nc.vector.tensor_tensor(down.lo[:, s, :], down.raw[:, 0, :], down.hi[:, s, :].bitcast(F32), ALU.subtract
                                        ).then_inc(down_lo, 1)

        def hidden(p, parity, act=None, dve=None):
            for s in range(2):
                for b, (t0, n) in enumerate(TOK_BLOCKS):
                    at_n = (p * 2 + s) * 3 + b + 1
                    dst = (slice(None), 2 * parity + s, slice(t0, t0 + n))
                    if act is not None:
                        if b < 2:
                            act.wait_ge(full[b], p * 2 + s + 1)
                        else:
                            act.wait_ge(up_used[s], p + 1)
                        nc.scalar.activation(hid_relu[dst], g.bank[b][:, 0:n], ACT.Relu).then_inc(relu_ready, 1)
                        act.wait_ge(relu_ready, at_n)
                        nc.scalar.activation(hid_hi[dst], hid_relu[dst], ACT.Square).then_inc(hid_hi_ready, 1)
                        continue
                    dve.wait_ge(relu_ready, at_n)
                    nc.vector.tensor_tensor(g.bank[b][:, 0:n], hid_relu[dst], g.bank[b][:, 0:n], ALU.mult
                                            ).then_inc(squared, 1)
                    dve.wait_ge(squared, at_n)
                    dve.wait_ge(hid_hi_ready, at_n)
                    nc.vector.tensor_tensor(hid_lo[dst], g.bank[b][:, 0:n], hid_hi[dst].bitcast(F32), ALU.subtract
                                            ).then_inc(hid_lo_ready, 1)

        @block.scalar
        def _(act):
            for s in range(2):
                up_weights(0, s, act=act)
            hidden(0, 0, act=act)
            for s in range(2):
                up_weights(1, s, act=act)

            def step(p, parity, last=False):
                for s in range(2):
                    down_weights(p, s, act=act)
                hidden(p + 1, 1 - parity, act=act)
                if not last:
                    for s in range(2):
                        up_weights(p + 2, s, act=act)
            step(0, 0)
            step(1, 1)
            with act.Fori(1, (pairs - 2) // 2) as i:
                step(i * 2, 0)
                step(i * 2 + 1, 1)
            step(pairs - 2, 0, last=True)
            for s in range(2):
                down_weights(pairs - 1, s, act=act)

        @block.vector
        def _(dve):
            def add(p, units):
                for u in units:
                    m, b = divmod(u, 3)
                    t0, n = TOK_BLOCKS[b]
                    dve.wait_ge(unit_full[u % DOWN_BANKS], p * PER + u // DOWN_BANKS + 1)
                    xs = g.x[:, m, t0:t0 + n]
                    nc.vector.scalar_tensor_tensor(xs, g.bank[3 + u % DOWN_BANKS][:, 0:n], g.m(40 + m, int(b > 0)), xs,
                                                   ALU.mult, ALU.add).then_inc(unit_added[u % DOWN_BANKS], 1)
            for s in range(2):
                up_weights(0, s, dve=dve)
            hidden(0, 0, dve=dve)
            for s in range(2):
                up_weights(1, s, dve=dve)

            def step(p, parity, last=False):
                for s in range(2):
                    down_weights(p, s, dve=dve)
                hidden(p + 1, 1 - parity, dve=dve)
                add(p, range(0, 8))
                if not last:
                    for s in range(2):
                        up_weights(p + 2, s, dve=dve)
                add(p, range(8, UNITS))
            step(0, 0)
            step(1, 1)
            with dve.Fori(1, (pairs - 2) // 2) as i:
                step(i * 2, 0)
                step(i * 2 + 1, 1)
            step(pairs - 2, 0, last=True)
            for s in range(2):
                down_weights(pairs - 1, s, dve=dve)
            add(pairs - 1, range(UNITS))
            for u in range(DOWN_BANKS):
                dve.wait_ge(unit_added[u], pairs * PER)

        @block.tensor
        def _(pe):
            def up_product(p):
                for s in range(2):
                    pe.wait_ge(up_lo[s], p + 1)
                    for b, (t0, n) in enumerate(TOK_BLOCKS):
                        if not (first(p) and s == 0):
                            pe.wait_ge(hid_lo_ready, (p * 2 + s - 1) * 3 + b + 1)
                        for k in range(KT):
                            last = exact_product(nc, g.bank[b][:, 0:n], up.hi[:, s, k * P:(k + 1) * P],
                                                 up.lo[:, s, k * P:(k + 1) * P], g.h_hi[:, k, t0:t0 + n],
                                                 g.h_lo[:, k, t0:t0 + n], k == 0, k == KT - 1)
                        last.then_inc(up_used[s] if b == 2 else full[b], 1)

            def down_product(p, parity):
                pe.wait_ge(down_lo, p * 2 + 2)
                pe.wait_ge(hid_lo_ready, p * 6 + 6)
                for u in range(UNITS):
                    m, b = divmod(u, 3)
                    t0, n = TOK_BLOCKS[b]
                    if not (first(p) and u < DOWN_BANKS):
                        pe.wait_ge(unit_added[u % DOWN_BANKS], p * PER + u // DOWN_BANKS)
                    for s in range(2):
                        last = exact_product(nc, g.bank[3 + u % DOWN_BANKS][:, 0:n], down.hi[:, s, m * P:(m + 1) * P],
                                             down.lo[:, s, m * P:(m + 1) * P], hid_hi[:, 2 * parity + s, t0:t0 + n],
                                             hid_lo[:, 2 * parity + s, t0:t0 + n], s == 0, s == 1)
                    last.then_inc(unit_full[u % DOWN_BANKS], 1)

            up_product(0)

            def step(p, parity):
                up_product(p + 1)
                down_product(p, parity)
            over_pairs(pe, step)
            down_product(pairs - 1, 1)


def output(nc, g, a):
    ctx = ExitStack()
    with ctx:
        sem = lambda n: ctx.enter_context(nc.semaphore("y_" + n))
        y = at(nc, "y_tok", [P, 2, D_MODEL], F32, 160)
        turned = [sem(f"turned{i}") for i in range(4)]
        moved = [sem(f"moved{i}") for i in range(4)]
        stored = [sem(f"stored{s}") for s in range(2)]
        n_tiles = TOKENS // P
        block = ctx.enter_context(nc.Block())

        @block.tensor
        def _(pe):
            def tile(i):
                for s in range(2):
                    for half in range(2):
                        b = 2 * s + half
                        if not first(i):
                            pe.wait_ge(moved[b], i)
                        for f in range(4):
                            last = nc.tensor.transpose(
                                g.bank[b][:, f * P:(f + 1) * P],
                                g.x[:, 4 * half + f, ds((i * 2 + s) * P, P)] if not isinstance(i, int) else
                                g.x[:, 4 * half + f, (i * 2 + s) * P:(i * 2 + s + 1) * P], g.ident[:, :])
                        last.then_inc(turned[b], 1)
            for i in range(n_tiles // 2):
                tile(i)

        def move(eng, copy, half):
            def tile(i):
                for s in range(2):
                    b = 2 * s + half
                    if not first(i):
                        eng.wait_ge(stored[s], i * 16)
                    eng.wait_ge(turned[b], i + 1)
                    copy(y[:, s, 512 * half:512 * half + 512], g.bank[b][:, :]).then_inc(moved[b], 1)
            peeled(eng, n_tiles // 2, tile)

        @block.vector
        def _(dve):
            move(dve, nc.vector.tensor_copy, 0)

        @block.scalar
        def _(act):
            move(act, lambda o, i: nc.scalar.activation(o, i, ACT.Copy), 1)

        @block.sync
        def _(sp):
            def store(i, dst):
                for s in range(2):
                    for half in range(2):
                        sp.wait_ge(moved[2 * s + half], i + 1)
                    sp.dma_start(dst(s), y[:, s, :]).then_inc(stored[s], 16)
            store(0, lambda s: a["y_prompt"][s * P:(s + 1) * P, :])
            with sp.Fori(1, n_tiles // 2) as i:
                store(i, lambda s: a["y_sample"][ds((i * 2 + s) * P - CTX, P), :])
            for s in range(2):
                sp.wait_ge(stored[s], 16 * (n_tiles // 2))


def backbone_step(nc, a):
    g = Ctx()
    low = [BASE]

    def const(name, shape, dtype=F32):
        size = 4
        for n in shape[1:]:
            size *= n
        t = nc.alloc_sbuf_tensor_at(name, shape, dtype, offset=low[0])
        low[0] += (size + 31) // 32 * 32
        assert low[0] <= AREA
        return t
    g.ident, g.ones = const("ident_sb", [P, P]), const("ones", [P, P])
    g.vecs, g.eps, g.cond_s = const("vecs_sb", [P, NVEC]), const("eps", [P, 1]), const("cond_silu", [P, KT, 2])
    g.mod = const("mod", [P, ADA_BLOCKS, 2])
    g.amp1, g.amp2 = const("amp1", [P, KT, 2]), const("amp2", [P, KT, 2])
    g.h_hi = at(nc, "h_hi", [P, KT, TOKENS], F32R, 0)
    g.h_lo = at(nc, "h_lo", [P, KT, TOKENS], F32R, 40)
    g.x = at(nc, "x", [P, KT, TOKENS], F32, 80)
    g.mix = at(nc, "mix", [P, KT, TOKENS], F32, 164)
    g.proj = nc.dram_tensor("proj", [IN_BLOCKS, P, TOKENS], F32, kind="Internal").ap()
    g.x_scratch = nc.dram_tensor("x_scratch", [P, KT * TOKENS], F32, kind="Internal").ap()

    def v(name, i, n=1):
        return g.vecs[:, ds(VEC[name] + i, n)]
    g.v = v
    g.m = lambda j, c: g.mod[:, ds(j), c]
    ctx = ExitStack()
    with ctx:
        g.constants_ready = ctx.enter_context(nc.semaphore("constants_ready"))
        g.bank = [ctx.enter_context(nc.psum_tensor(f"bank{b}", [P, 512], F32)) for b in range(8)]
        modulation_and_input(nc, g, a)
        norm(nc, g, "norm1_", lambda k, c: g.amp1[:, ds(k), c], lambda k, c: g.m(k, c), True)
        input_projection(nc, g, a)
        mixers(nc, g, a)
        output_projection(nc, g, a)
        norm(nc, g, "norm2_", lambda k, c: g.amp2[:, ds(k), c], lambda k, c: g.m(24 + k, c), True)
        mlp(nc, g, a)
        norm(nc, g, "final_", lambda k, c: g.v("final", k), None, False)
        output(nc, g, a)


def shape_constants():
    import numpy as np
    key, query = np.arange(P)[:, None] % 32, np.arange(32)[None, :]
    masks = [key == query]
    for level in range(MASKED):
        size = 2 ** level
        same = key // (2 * size) == query // (2 * size)
        key_right, query_right = key // size % 2 == 1, query // size % 2 == 1
        masks += [same & ~key_right & query_right, same & key_right & ~query_right]
    masks = np.stack(masks, 1).astype(np.float32)
    quarter = D_MODEL // 4
    omega = (1.0 / (np.float32(10000.0) ** (np.arange(quarter, dtype=np.float32) / np.float32(quarter)))).astype(np.float32)

    def table(n):
        angle = np.arange(n, dtype=np.float32)[:, None] * omega
        both = np.concatenate([np.sin(angle), np.cos(angle)], 1)
        return both.reshape(n, 4, P).transpose(2, 1, 0).reshape(P, 4 * n)
    pos = np.concatenate([table(LAT // GRID_W), table(GRID_W)], 1).astype(np.float32)
    return {"ident": np.eye(P, dtype=np.float32), "masks": np.ascontiguousarray(masks), "pos": np.ascontiguousarray(pos)}


def kernel(**inputs):
    import numpy as np
    import concourse.bacc as bacc
    from concourse.bass_utils import run_bass_kernel_spmd

    w = {n: np.asarray(x) for n, x in inputs.items()}

    def column_tiles(m):
        return m.reshape(KT, P, -1, P).transpose(2, 1, 0, 3).reshape(-1, P, KT * P)

    def cols(x):
        return x.reshape(-1, P).T
    starts = (24, 28, 16, 20, 0, 8, 4, 12)
    order = [start + h for h in range(HEADS) for start in starts]
    vecs = np.concatenate([cols(w[n]) for n in (
        "b_ada", "norm1_gain", "norm2_gain", "final_gain", "hg_lb_logits", "hg_norm_gain", "conv_w", "conv_b",
        "lru_ba", "lru_bx", "lru_lambda", "state_rglru")], 1)
    arrays = {
        "x_prompt": w["x_prompt"][0], "x_sample": w["x_sample"][0],
        "cond": np.stack([w["c_ctx"].reshape(KT, P), w["c"].reshape(KT, P)], 2).transpose(1, 0, 2),
        "vecs": vecs, "w_ada": column_tiles(w["w_ada"][0]), "w_in": column_tiles(w["w_in"][0])[order],
        "w_out": column_tiles(w["w_out"][0]), "w_ff1": column_tiles(w["w_ff1"][0]),
        "w_ff2": w["w_ff2"][0].reshape(FF_BLOCKS, P, D_MODEL),
        "state_hgrn": w["state_hgrn"][0, 0], "lru_wa": w["lru_wa"][0], "lru_wx": w["lru_wx"][0],
    }
    arrays.update(shape_constants())
    arrays = {"in_" + n: np.ascontiguousarray(x) for n, x in arrays.items()}
    nc = bacc.Bacc("TRN2", target_bir_lowering=False, num_devices=1)
    a = {n[3:]: nc.dram_tensor(n, x.shape, mybir.dt.from_np(x.dtype), kind="ExternalInput").ap()
         for n, x in arrays.items()}
    outs = {"y_prompt": (CTX, D_MODEL), "y_sample": (LAT, D_MODEL), "new_hgrn": (DIRS, HEADS, P, P), "new_lru": (P, 8)}
    for n, shape in outs.items():
        a[n] = nc.dram_tensor("out_" + n, shape, F32, kind="ExternalOutput").ap()
    backbone_step(nc, a)
    got = run_bass_kernel_spmd(nc, [arrays], core_ids=[0]).results[0]
    return (got["out_y_prompt"][None], got["out_y_sample"][None], got["out_new_hgrn"][None, None],
            np.ascontiguousarray(got["out_new_lru"].T).reshape(1, 1, DIRS, HEADS * P))
```

```python
import concourse.bass as bass
from concourse import mybir
from contextlib import ExitStack

F32 = mybir.dt.float32
F32R = mybir.dt.float32r
I32 = mybir.dt.int32
ALU = mybir.AluOpType
ACT = mybir.ActivationFunctionType

P = 128
D_MODEL = 1024
CTX, LAT = 256, 1024
TOKENS = CTX + LAT
GRID_W = 64
KT = D_MODEL // P
IN_BLOCKS, FF_BLOCKS, ADA_BLOCKS = 32, 32, 48
HEADS, DIRS = 4, 2
CHUNKS = TOKENS // P
CTX_CHUNKS = CTX // P
EPS = 1e-6
LRU_C = 8.0
CONV_W, CONV_LEFT = 4, 2
TOK_BLOCKS = ((0, 256), (256, 512), (768, 512))
SEGS = ((0, CTX, 0), (CTX, LAT, 1))
GROUPS = ((0, 2), (2, 4), (6, 4))
T_V, T_GATE, T_Q0, T_F0, T_Q1, T_F1, T_LX, T_LG = range(8)
PER_HEAD = 8

VEC = {}
_at = 0
for _name, _n in (("b_ada", 48), ("norm1", 8), ("norm2", 8), ("final", 8), ("lb", 16), ("hg_gain", 4),
                  ("conv_w", 16), ("conv_b", 4), ("ba", 8), ("bx", 8), ("lam", 8), ("h0", 8)):
    VEC[_name] = _at
    _at += _n
NVEC = _at
LEVELS = 7
MASKED = 5
MASKS = 1 + DIRS * MASKED
POS_COLS = 4 * (LAT // GRID_W) + 4 * GRID_W

KB = 1024
BASE = 16512
AREA = BASE + 3840


class Ctx:
    pass


def ds(at, n=1):
    return bass.ds(at, n)


def peeled(eng, n, body):
    body(0)
    with eng.Fori(1, n) as i:
        body(i)


def first(i):
    return isinstance(i, int) and i == 0


def wait_apart(g, eng, sem, value):
    eng.wait_ge(sem, value)
    eng.wait_ge(g.constants_ready, 1)


def exact_product(nc, out, w_hi, w_lo, x_hi, x_lo, start, stop):
    nc.tensor.matmul(out, w_lo, x_hi, start=start, stop=False)
    nc.tensor.matmul(out, w_hi, x_lo, start=False, stop=False)
    return nc.tensor.matmul(out, w_hi, x_hi, start=False, stop=stop)


def at(nc, name, shape, dtype, kb):
    return nc.alloc_sbuf_tensor_at(name, shape, dtype, offset=AREA + int(kb * KB))


def modulation_and_input(nc, g, a):
    ctx = ExitStack()
    with ctx:
        sem = lambda n: ctx.enter_context(nc.semaphore(n))
        cond = at(nc, "cond", [P, KT, 2], F32, 162)
        cond_s = g.cond_s
        ada_raw = at(nc, "ada_raw", [P, 2, D_MODEL], F32, 120)
        x_tok = at(nc, "x_tok", [P, 2, D_MODEL], F32, 128)
        pos = at(nc, "pos", [P, POS_COLS], F32, 136)
        vec_in, cond_in, cond_ready = sem("vec_in"), sem("cond_in"), sem("cond_ready")
        ada_in = [sem(f"ada_in{s}") for s in range(2)]
        ada_used = [sem(f"ada_used{s}") for s in range(2)]
        x_in = [sem(f"x_in{s}") for s in range(2)]
        x_used = [sem(f"x_used{s}") for s in range(2)]
        x_moved = [sem(f"x_moved{s}") for s in range(2)]
        ada_done, mod_ready, setup = sem("ada_done"), sem("mod_ready"), sem("setup")
        x_saved = sem("x_saved")
        n_ctx = CTX // P
        pos_r = pos[:, 0:4 * 16].rearrange("p (f r) -> p f r", f=4)
        pos_c = pos[:, 64:64 + 4 * 64].rearrange("p (f c) -> p f c", f=4)
        block = ctx.enter_context(nc.Block())

        @block.sync
        def _(sp):
            sp.dma_start(g.vecs[:, :], a["vecs"]).then_inc(vec_in, 16)
            sp.dma_start(g.ident[:, :], a["ident"]).then_inc(vec_in, 16)
            sp.dma_start(pos[:, :], a["pos"]).then_inc(vec_in, 16)
            sp.dma_start(cond[:, :, :], a["cond"]).then_inc(cond_in, 16)

            def load(i):
                for s in range(2):
                    if not first(i):
                        sp.wait_ge(ada_used[s], i)
                    sp.dma_start(ada_raw[:, s, :], a["w_ada"][ds(i * 2 + s), :, :].rearrange("a p n -> p (a n)")
                                 ).then_inc(ada_in[s], 16)
            peeled(sp, 8, load)

        @block.gpsimd
        def _(pool):
            pass

        @block.scalar
        def _(act):
            for s in range(2):
                act.dma_start(x_tok[:, s, :], a["x_prompt"][s * P:(s + 1) * P, :]).then_inc(x_in[s], 16)
            act.wait_ge(cond_in, 16)
            nc.scalar.activation(cond_s[:, :, :], cond[:, :, :], ACT.Silu).then_inc(cond_ready, 1)
            with act.Fori(0, LAT // (2 * P)) as i:
                for s in range(2):
                    act.wait_ge(x_used[s], i + 1)
                    act.dma_start(x_tok[:, s, :], a["x_sample"][ds((i * 2 + s) * P, P), :]).then_inc(x_in[s], 16)
            for s in range(2):
                act.wait_ge(x_moved[s], 2 * (1 + LAT // (2 * P)))
            act.dma_start(g.x_scratch, g.x[:, :, :].rearrange("p k t -> p (k t)")).then_inc(x_saved, 16)
            act.wait_ge(x_saved, 16)

        @block.tensor
        def _(pe):
            pe.wait_ge(vec_in, 48)

            def turn(i):
                for s in range(2):
                    pe.wait_ge(x_in[s], i * 16 + 16)
                    if not first(i):
                        pe.wait_ge(x_moved[s], i * 2)
                    for f in range(KT):
                        last = nc.tensor.transpose(g.bank[2 * s + f // 4][:, (f % 4) * P:(f % 4 + 1) * P],
                                                   x_tok[:, s, f * P:(f + 1) * P], g.ident[:, :])
                    last.then_inc(x_used[s], 1)
            peeled(pe, 1 + LAT // (2 * P), turn)
            pe.wait_ge(cond_ready, 1)
            with pe.Fori(0, 8) as i:
                for s in range(2):
                    pe.wait_ge(ada_in[s], i * 16 + 16)
                    for k in range(KT):
                        last = nc.tensor.matmul(g.bank[4][:, ds((i * 2 + s) * 2, 2)], ada_raw[:, s, k * P:(k + 1) * P],
                                                cond_s[:, k, :], start=(k == 0), stop=(k == KT - 1))
                    last.then_inc(ada_used[s], 1)

        @block.vector
        def _(dve):
            nc.vector.memset(g.ones[:, :], 1.0).then_inc(g.constants_ready, 1)
            nc.vector.memset(g.eps[:, :], EPS).then_inc(setup, 1)
            dve.wait_ge(vec_in, 48)
            x4 = g.x[:, :, :]
            for s in range(n_ctx):
                dve.wait_ge(x_used[s], 1)
                for half in range(2):
                    nc.vector.tensor_copy(x4[:, 4 * half:4 * half + 4, s * P:(s + 1) * P],
                                          g.bank[2 * s + half][:, :].rearrange("p (f t) -> p f t", f=4)
                                          ).then_inc(x_moved[s], 1)
            with dve.Fori(0, LAT // (2 * P)) as i:
                for s in range(2):
                    dve.wait_ge(x_used[s], i + 2)
                    for r in range(2):
                        nc.vector.tensor_tensor(
                            x4[:, 0:4, ds(CTX + (i * 2 + s) * P + r * GRID_W, GRID_W)],
                            g.bank[2 * s][:, :].rearrange("p (f t) -> p f t", f=4)[:, :, r * GRID_W:(r + 1) * GRID_W],
                            pos_r[:, :, ds(i * 4 + s * 2 + r)].broadcast_to([P, 4, GRID_W]), ALU.add
                        ).then_inc(x_moved[s] if r else setup, 1)
                    nc.vector.tensor_tensor(
                        x4[:, 4:8, ds(CTX + (i * 2 + s) * P, P)].rearrange("p f (r c) -> p f r c", r=2),
                        g.bank[2 * s + 1][:, :].rearrange("p (f r c) -> p f r c", f=4, r=2),
                        pos_c[:, :, :].unsqueeze(2).broadcast_to([P, 4, 2, GRID_W]), ALU.add
                    ).then_inc(x_moved[s], 1)
            for s in range(2):
                dve.wait_ge(ada_used[s], 8)
            nc.vector.tensor_tensor(g.mod[:, 0:16, :], g.bank[4][:, 0:32].rearrange("p (j c) -> p j c", c=2),
                                    g.v("b_ada", 0, 16).unsqueeze(2).broadcast_to([P, 16, 2]), ALU.add
                                    ).then_inc(mod_ready, 1)
            dve.wait_ge(mod_ready, 1)
            nc.vector.scalar_tensor_tensor(g.amp1[:, :, :], g.mod[:, 8:16, :], 1.0,
                                           g.v("norm1", 0, 8).unsqueeze(2).broadcast_to([P, 8, 2]), ALU.add, ALU.mult
                                           ).then_inc(mod_ready, 1)
            dve.wait_ge(mod_ready, 2)


def norm(nc, g, name, gain_amp, shift, tail):
    ctx = ExitStack()
    with ctx:
        sem = lambda n: ctx.enter_context(nc.semaphore(name + n))
        sq = at(nc, name + "sq", [P, 2, TOKENS], F32, 130)
        root = at(nc, name + "root", [P, TOKENS], F32, 140)
        rstd = at(nc, name + "rstd", [P, TOKENS], F32, 145)
        tmp = at(nc, name + "tmp", [P, 2, TOKENS], F32, 150)
        squared = [sem(f"squared{s}") for s in range(2)]
        summed = [sem(f"summed{s}") for s in range(2)]
        rooted, rstd_ready = sem("rooted"), sem("rstd_ready")
        scaled = [sem(f"scaled{s}") for s in range(2)]
        hi_done = [sem(f"hi_done{s}") for s in range(2)]
        lo_done = [sem(f"lo_done{s}") for s in range(2)]
        pairs = KT // 2
        block = ctx.enter_context(nc.Block())

        @block.scalar
        def _(act):
            def square(i):
                for s in range(2):
                    if not first(i):
                        wait_apart(g, act, summed[s], i)
                    nc.scalar.activation(sq[:, s, :], g.x[:, ds(i * 2 + s), :].rearrange("p a t -> p (a t)"),
                                         ACT.Square).then_inc(squared[s], 1)
            peeled(act, pairs, square)
            act.wait_ge(summed[1], pairs)
            for b, (t0, n) in enumerate(TOK_BLOCKS):
                nc.scalar.activation(root[:, t0:t0 + n], g.bank[b][:, 0:n], ACT.Sqrt, bias=g.eps[:, 0:1],
                                     scale=1.0 / D_MODEL).then_inc(rooted, 1)
            if not tail:
                return
            with act.Fori(0, pairs) as i:
                for s in range(2):
                    wait_apart(g, act, scaled[s], i * 2 + 2)
                    for t0, n, c in SEGS:
                        nc.scalar.activation(g.h_hi[:, ds(i * 2 + s), t0:t0 + n].rearrange("p a t -> p (a t)"),
                                             tmp[:, s, t0:t0 + n], ACT.Identity,
                                             bias=shift(i * 2 + s, c)).then_inc(hi_done[s], 1)

        @block.tensor
        def _(pe):
            def add(i, start, stop):
                for s in range(2):
                    pe.wait_ge(squared[s], i + 1)
                    for b, (t0, n) in enumerate(TOK_BLOCKS):
                        last = nc.tensor.matmul(g.bank[b][:, 0:n], g.ones[:, :], sq[:, s, t0:t0 + n],
                                                start=start and s == 0, stop=stop and s == 1)
                    last.then_inc(summed[s], 1)
            add(0, True, False)
            with pe.Fori(1, pairs - 1) as i:
                add(i, False, False)
            add(pairs - 1, False, True)

        @block.vector
        def _(dve):
            for b, (t0, n) in enumerate(TOK_BLOCKS):
                dve.wait_ge(rooted, b + 1)
                nc.vector.reciprocal(rstd[:, t0:t0 + n], root[:, t0:t0 + n]).then_inc(rstd_ready, 1)
            dve.wait_ge(rstd_ready, 3)

            def scale(i):
                for s in range(2):
                    if tail and not first(i):
                        dve.wait_ge(lo_done[s], i * 2)
                    for t0, n, c in SEGS:
                        xs = g.x[:, ds(i * 2 + s), t0:t0 + n].rearrange("p a t -> p (a t)")
                        nc.vector.scalar_tensor_tensor(tmp[:, s, t0:t0 + n] if tail else xs, xs,
                                                       gain_amp(i * 2 + s, c), rstd[:, t0:t0 + n],
                                                       ALU.mult, ALU.mult).then_inc(scaled[s], 1)

            def low(i):
                for s in range(2):
                    dve.wait_ge(hi_done[s], i * 2 + 2)
                    for t0, n, c in SEGS:
                        nc.vector.scalar_tensor_tensor(
                            g.h_lo[:, ds(i * 2 + s), t0:t0 + n].rearrange("p a t -> p (a t)"),
                            tmp[:, s, t0:t0 + n], shift(i * 2 + s, c),
                            g.h_hi[:, ds(i * 2 + s), t0:t0 + n].bitcast(F32).rearrange("p a t -> p (a t)"),
                            ALU.add, ALU.subtract).then_inc(lo_done[s], 1)
            if not tail:
                with dve.Fori(0, pairs) as i:
                    scale(i)
                return
            scale(0)
            with dve.Fori(1, pairs) as i:
                low(i - 1)
                scale(i)
            low(pairs - 1)
            for s in range(2):
                dve.wait_ge(lo_done[s], 2 * pairs)


def split_weights(nc, act, dve, i, s, ring, raw_in, hi_ready, lo_ready, used):
    if act is not None:
        act.wait_ge(raw_in[s], i * 16 + 16)
        if not first(i):
            act.wait_ge(used[s], i)
        nc.scalar.activation(ring.hi[:, s, :], ring.raw[:, s, :], ACT.Copy).then_inc(hi_ready[s], 1)
    if dve is not None:
        dve.wait_ge(hi_ready[s], i + 1)
        nc.vector.tensor_tensor(ring.lo[:, s, :], ring.raw[:, s, :], ring.hi[:, s, :].bitcast(F32),
                                ALU.subtract).then_inc(lo_ready[s], 1)


class Ring:
    def __init__(self, nc, name, kb, raw_slots=2):
        self.raw = at(nc, name + "raw", [P, raw_slots, D_MODEL], F32, kb)
        kb += 4 * raw_slots
        self.hi = at(nc, name + "hi", [P, 2, D_MODEL], F32R, kb)
        self.lo = at(nc, name + "lo", [P, 2, D_MODEL], F32R, kb + 8)


SLOTS = 3 * PER_HEAD
LEAD = 4
(S_SELF, S_LEVELS, S_HALF32, S_HALF64, S_KEYS, S_ADD, S_ADD2, S_OUT, S_OUT2, S_SUM, S_SPREAD) = (
    0, 1, 6, 7, 8, 9, 10, 11, 12, 13, 14)
S_GATES = 15
MIX_BANKS = (3, 4, 5, 6, 7)
STATE_ORDER = ((0, 0), (1, 0), (0, 1), (1, 2), (0, 2), (1, 1))


class Banks:

    def __init__(self, sem):
        uses = [("vt", n) for n in range(3)] + [("diag",)]
        uses += [("level", l, d) for l in range(MASKED) for d in range(DIRS)]
        uses += [("half32",), ("half64", 0), ("half64", 1)]
        uses += [("kt", d, n) for d, n in STATE_ORDER] + [("ds", d, n) for d, n in STATE_ORDER]
        uses += [("out", n) for n in range(3)] + [("sum",)] + [("spread", n) for n in range(3)]
        uses += [("lru", d, ax, b) for d in range(DIRS) for ax in range(2) for b in range(3)]
        self.where, self.count = {}, dict.fromkeys(MIX_BANKS, 0)
        for i, name in enumerate(uses):
            b = MIX_BANKS[i % len(MIX_BANKS)]
            self.where[name] = (b, self.count[b])
            self.count[b] += 1
        self.full = {b: sem(f"bank_full{b}") for b in MIX_BANKS}
        self.free = {b: sem(f"bank_free{b}") for b in MIX_BANKS}

    def bank(self, name):
        return self.where[name][0]

    def wait_free(self, eng, h, name):
        b, n = self.where[name]
        eng.wait_ge(self.free[b], h * self.count[b] + n + 1)

    def wait_full(self, eng, h, name):
        b, n = self.where[name]
        eng.wait_ge(self.full[b], h * self.count[b] + n + 1)

    def wait_read(self, eng, h, name):
        b, n = self.where[name]
        eng.wait_ge(self.free[b], h * self.count[b] + n + 2)

    def filled(self, ins, name):
        ins.then_inc(self.full[self.bank(name)], 1)

    def read(self, ins, name):
        ins.then_inc(self.free[self.bank(name)], 1)


def state_steps(d, n):
    c0, k = GROUPS[n]
    steps = []
    for c in (range(c0, c0 + k) if d == 0 else reversed(range(c0, c0 + k))):
        if c == (1, 0)[d]:
            steps.append((c, None))
        elif c != (CHUNKS - 1, CTX_CHUNKS)[d]:
            steps.append((c, c + 1 - 2 * d))
    return steps


STATE_STEPS = sum(len(state_steps(d, n)) - 1 for d, n in STATE_ORDER)
CONV_N = 7
SERIES = 8
SMALL_STEPS = 4 + 2 + 5 + (SERIES - 1) + 4


def small_constants(nc, dve, g, small, done, from_act):
    count = [0]

    def link(ins):
        count[0] += 1
        ins.then_inc(done, 1)
        dve.wait_ge(done, count[0])
    t = lambda i: small[:, i, :]
    vec = nc.vector
    lam = g.vecs[:, VEC["lam"]:VEC["lam"] + 8]
    link(vec.tensor_tensor(t(5), g.vecs[:, VEC["lb"]:VEC["lb"] + 8], g.vecs[:, VEC["lb"] + 8:VEC["lb"] + 16],
                           ALU.subtract))
    link(vec.tensor_scalar(t(8), lam, -1.0, None, ALU.mult))
    link(vec.tensor_tensor(t(6), lam, t(8), ALU.max))
    link(vec.tensor_scalar(t(8), t(8), 0.0, None, ALU.max))
    dve.wait_ge(from_act, 1)
    link(vec.tensor_scalar(t(1), t(0), -1.0, 1.0, ALU.mult, ALU.add))
    link(vec.tensor_scalar(t(2), t(0), 1.0, -1.0, ALU.mult, ALU.add))
    dve.wait_ge(from_act, 2)
    link(vec.tensor_scalar(t(9), t(7), 2.0, None, ALU.add))
    link(vec.reciprocal(t(10), t(9)))
    link(vec.tensor_tensor(t(11), t(7), t(10), ALU.mult))
    link(vec.tensor_tensor(t(12), t(11), t(11), ALU.mult))
    link(vec.tensor_scalar(t(13), t(12), 1.0 / (2 * SERIES + 1), None, ALU.mult))
    for n in range(SERIES - 1, 0, -1):
        link(vec.scalar_tensor_tensor(t(13), t(13), 1.0 / (2 * n + 1), t(12), ALU.add, ALU.mult))
    link(vec.scalar_tensor_tensor(t(13), t(13), 1.0, t(11), ALU.add, ALU.mult))
    link(vec.scalar_tensor_tensor(t(13), t(13), 2.0, t(8), ALU.mult, ALU.add))
    link(vec.tensor_scalar(t(3), t(13), LRU_C, None, ALU.mult))
    link(vec.tensor_scalar(t(4), t(13), -LRU_C, None, ALU.mult))
    assert count[0] == SMALL_STEPS


def projection_and_mixers(nc, g, a):
    ctx = ExitStack()
    with ctx:
        ctx.enter_context(nc.cleanup_on_exit())
        sem = lambda n: nc.alloc_semaphore("mx_" + n)
        two = lambda n: [sem(f"{n}{s}") for s in range(2)]
        buf = lambda n, shape, kb, dt=F32: at(nc, "mx_" + n, shape, dt, kb)
        row = [P, TOKENS]
        ring = Ring(nc, "in_", 80)
        stage = buf("stage", [P, 2, TOKENS], 104)
        ada_raw = buf("ada_raw", [P, 2, D_MODEL], 114)
        at_row = lambda i: 122 + 5 * i
        q = [buf("q0", row, at_row(0)), buf("q1", row, at_row(2))]
        f = [buf("f0", row, at_row(1)), buf("f1", row, at_row(3))]
        k = [buf("k0", row, at_row(4)), buf("k1", row, at_row(5))]
        v = buf("v", row, at_row(6))
        scores = buf("scores", [P, CHUNKS, P], at_row(6))
        gate = buf("gate", row, at_row(7))
        v_tok = buf("v_tok", [P, CHUNKS, P], at_row(8))
        k_tok = [buf("k_tok0", [P, CHUNKS, P], at_row(9)), buf("k_tok1", [P, CHUNKS, P], at_row(10))]
        state = [buf("state0", [P, CHUNKS, P], at_row(11)), buf("state1", [P, CHUNKS, P], at_row(12))]
        lx, lg = buf("lx", row, at_row(13)), buf("lg", row, at_row(14))
        o_sq, o_gain = buf("o_sq", row, at_row(1)), buf("o_gain", row, at_row(3))
        xc = buf("xc", row, at_row(4))
        r = [buf("r0", row, at_row(5)), buf("r1", row, at_row(9))]
        ig = [buf("ig0", row, at_row(8)), buf("ig1", row, at_row(10))]
        dec, sq = buf("dec", row, at_row(11)), buf("sq", row, at_row(12))
        tiles = {T_LX: lx, T_LG: lg, T_V: v, T_GATE: gate, T_Q0: q[0], T_F0: f[0], T_Q1: q[1], T_F1: f[1]}
        diag = buf("diag", [P, CHUNKS, 32], 197)
        head_vecs = buf("head_vecs", [P, 9], 198.25)
        new_lru = buf("new_lru", [P, 8], 198.3125)
        root, rstd = buf("root", [P, CHUNKS], 198.375), buf("rstd", [P, CHUNKS], 198.4375)
        last_state = [buf("last0", [P, P], 198.5), buf("last1", [P, P], 199)]
        lru_w = buf("lru_w", [P, 4, P], 199.5)
        masks = buf("masks", [P, MASKS, 32], 201.5)
        small = buf("small", [P, 16, 8], 203)
        lb, one_lb, neg_lb = (small[:, i, :] for i in range(3))

        raw_in, hi_ready, lo_ready, used = two("raw_in"), two("hi_ready"), two("lo_ready"), two("used")
        ada_in, ada_used, stored = two("ada_in"), two("ada_used"), two("stored")
        unit_full, staged, mod_done = two("unit_full"), two("staged"), sem("mod_done")
        bk = Banks(sem)
        tile_in = {t: sem(f"tile_in{t}") for t in tiles}
        const_in, states_in, lru_w_in = sem("const_in"), sem("states_in"), sem("lru_w_in")
        zeroed, states_zero, small_act, small_dve = sem("zeroed"), sem("states_zero"), sem("small_act"), sem("small_dve")
        sig_ready, q_ready, gate_ready = sem("sig_ready"), sem("q_ready"), sem("gate_ready")
        kf_ready, qk_ready, tot_ready, placed = sem("kf_ready"), sem("qk_ready"), sem("tot_ready"), sem("placed")
        state_step, squared, gained, rstd_ready, normed, vecs_ready = (
            sem("state_step"), sem("squared"), sem("gained"), sem("rstd_ready"), sem("normed"), sem("vecs_ready"))
        head_done, head_stored, tile_done, tile_stored, last_stored, lru_stored = (
            sem("head_done"), sem("head_stored"), sem("tile_done"), sem("tile_stored"), sem("last_stored"),
            sem("lru_stored"))
        conv, lru_exp, ix_ready, gap_ready, gap_root, u_ready, scanned, lg_ready = (
            sem("conv"), sem("lru_exp"), sem("ix_ready"), sem("gap_ready"), sem("gap_root"), sem("u_ready"),
            sem("scanned"), sem("lg_ready"))
        QK_N = 2 + LEVELS * DIRS * 2

        def qk_count(level, d):
            return 1 + d if level == 0 else 2 + (2 * (level - 1) + d) * 2 + 2

        def turns(eng, project, mix, prepare=None):
            def turn(h, last):
                for u in range(SLOTS):
                    project(h, u, last)
                    if u < SLOTS - LEAD:
                        if not first(h):
                            mix(h - 1, u + LEAD)
                    else:
                        mix(h, u + LEAD - SLOTS)
            turn(0, False)
            with eng.Fori(1, HEADS - 1) as h:
                turn(h, False)
            turn(HEADS - 1, True)
            for step in range(LEAD, SLOTS):
                mix(HEADS - 1, step)

        block = ctx.enter_context(nc.Block())

        @block.sync
        def _(sp):
            def load_tile(h, t):
                sp.wait_ge(stored[t % 2], (h * (PER_HEAD // 2) + t // 2) * 16 + 16)
                sp.dma_start(tiles[t][:, :], g.proj[ds(h * PER_HEAD + t), :, :].rearrange("a p n -> p (a n)")
                             ).then_inc(tile_in[t], 16)

            def load_weights(h, j):
                s, i = j % 2, h * (PER_HEAD // 2) + j // 2
                if not first(i):
                    sp.wait_ge(lo_ready[s], i)
                sp.dma_start(ring.raw[:, s, :], a["w_in"][ds(i * 2 + s), :, :].rearrange("a p n -> p (a n)")
                             ).then_inc(raw_in[s], 16)
                if not first(i):
                    sp.wait_ge(ada_used[s], i)
                sp.dma_start(ada_raw[:, s, :], a["w_ada"][ds(16 + i * 2 + s), :, :].rearrange("a p n -> p (a n)")
                             ).then_inc(ada_in[s], 16)

            def project(h, u, last):
                if u % 3 == 1:
                    j = u // 3
                    if j + 2 < PER_HEAD:
                        load_weights(h, j + 2)
                    elif not last:
                        load_weights(h + 1, j + 2 - PER_HEAD)
                if u == 11:
                    load_tile(h, T_V)
                    load_tile(h, T_Q0)
                if u == 13:
                    load_tile(h, T_F0)
                    if not first(h):
                        sp.wait_ge(head_stored, h * 16)
                    load_tile(h, T_GATE)
                if u == 16:
                    load_tile(h, T_Q1)
                if u == 19:
                    load_tile(h, T_F1)

            def mix(h, step):
                if step == 5:
                    if not first(h):
                        sp.wait_ge(tile_stored, h * 16)
                    load_tile(h, T_LX)
                    load_tile(h, T_LG)
                    if not first(h):
                        sp.wait_ge(last_stored, h * 32)
                    sp.wait_ge(states_zero, h * 2 + 2)
                    for d, c in ((0, CTX_CHUNKS), (1, CHUNKS - 1)):
                        sp.dma_start(state[d][:, c, :], a["state_hgrn"][d, ds(h), :, :].rearrange("a p n -> p (a n)")
                                     ).then_inc(states_in, 16)
                    for ax, w in enumerate(("lru_wa", "lru_wx")):
                        for half in range(2):
                            part = slice(64 * half, 64 * half + 64)
                            sp.dma_start(lru_w[part, 2 * ax:2 * ax + 2, part],
                                         a[w][:, ds(h * 2 + half), :, :].rearrange("r a d e -> d (r a) e")
                                         ).then_inc(lru_w_in, 16)
                if step == S_OUT2:
                    for d in range(DIRS):
                        bk.wait_read(sp, h, ("ds", d, 0))
                        sp.dma_start(a["new_hgrn"][d, ds(h), :, :].rearrange("a p n -> p (a n)"), last_state[d][:, :]
                                     ).then_inc(last_stored, 16)
                if step == S_GATES:
                    sp.wait_ge(head_done, h + 1)
                    sp.dma_start(g.mix_out[ds(h), :, :].rearrange("a p n -> p (a n)"), gate[:, :]
                                 ).then_inc(head_stored, 16)
                if step == SLOTS - 1:
                    sp.wait_ge(tile_done, h + 1)
                    sp.dma_start(g.mix_out[ds(h + HEADS), :, :].rearrange("a p n -> p (a n)"), lg[:, :]
                                 ).then_inc(tile_stored, 16)

            sp.wait_ge(zeroed, 1)
            sp.dma_start(masks[:, :, :], a["masks"]).then_inc(const_in, 16)
            load_weights(0, 0)
            load_weights(0, 1)
            turns(sp, project, mix)
            sp.dma_start(a["new_lru"], new_lru[:, :]).then_inc(lru_stored, 16)
            sp.wait_ge(lru_stored, 16)
            sp.wait_ge(last_stored, HEADS * 32)
            sp.wait_ge(head_stored, HEADS * 16)
            sp.wait_ge(tile_stored, HEADS * 16)

        @block.scalar
        def _(act):
            def to_sbuf(h, name, out, columns):
                bk.wait_full(act, h, name)
                bk.read(nc.scalar.activation(out, g.bank[bk.bank(name)][:, 0:columns], ACT.Copy), name)

            def flat(t, c0, kc):
                return t[:, c0:c0 + kc, :].rearrange("p c k -> p (c k)")

            def project(h, u, last):
                j, b = divmod(u, 3)
                s, i = j % 2, h * (PER_HEAD // 2) + j // 2
                t0, n = TOK_BLOCKS[b]
                if b == 0 and not first(i):
                    act.wait_ge(stored[s], i * 16)
                if b < 2:
                    act.wait_ge(unit_full[b], h * PER_HEAD + j + 1)
                else:
                    act.wait_ge(used[s], i + 1)
                nc.scalar.activation(stage[:, s, t0:t0 + n], g.bank[u % 2][:, 0:n], ACT.Copy).then_inc(staged[s], 1)
                if b == 2:
                    act.wait_ge(staged[s], i * 3 + 3)
                    act.dma_start(g.proj[ds(h * PER_HEAD + j), :, :].rearrange("a p n -> p (a n)"), stage[:, s, :]
                                  ).then_inc(stored[s], 16)
                if b == 0 and not (last and j == PER_HEAD - 1):
                    split_weights(nc, act, None, h * (PER_HEAD // 2) + (j + 1) // 2, 1 - s, ring, raw_in, hi_ready,
                                  lo_ready, used)
                if u == 17:
                    act.wait_ge(tile_in[T_Q0], h * 16 + 16)
                    nc.scalar.activation(q[0][:, :], q[0][:, :], ACT.Silu).then_inc(q_ready, 1)
                    act.wait_ge(tile_in[T_GATE], h * 16 + 16)
                    nc.scalar.activation(gate[:, :], gate[:, :], ACT.Silu).then_inc(gate_ready, 1)
                if u == 18:
                    act.wait_ge(tile_in[T_Q1], h * 16 + 16)
                    nc.scalar.activation(q[1][:, :], q[1][:, :], ACT.Silu).then_inc(q_ready, 1)
                if u == 19:
                    for d in range(DIRS):
                        act.wait_ge(tile_in[(T_F0, T_F1)[d]], h * 16 + 16)
                        nc.scalar.activation(f[d][:, :], f[d][:, :], ACT.Sigmoid).then_inc(sig_ready, 1)

            def mix(h, step):
                if step == S_SELF:
                    if not first(h):
                        act.wait_ge(tile_done, h)
                    for n, (c0, kc) in enumerate(GROUPS):
                        to_sbuf(h, ("vt", n), flat(v_tok, c0, kc), kc * P)
                if step == S_HALF32:
                    bk.wait_full(act, h, ("half32",))
                    for j in range(4):
                        rows, cols = slice(32 * j, 32 * j + 32), slice(32 * (j ^ 1), 32 * (j ^ 1) + 32)
                        ins = nc.scalar.activation(
                            scores[rows, :, cols], g.bank[bk.bank(("half32",))][rows, 0:CHUNKS * 32].rearrange(
                                "p (c t) -> p c t", t=32), ACT.Copy)
                    bk.read(ins, ("half32",))
                if step == S_HALF64:
                    for part in range(2):
                        bk.wait_full(act, h, ("half64", part))
                        for j in range(2):
                            rows, cols = slice(64 * j, 64 * j + 64), slice(64 * (1 - j), 64 * (1 - j) + 64)
                            ins = nc.scalar.activation(
                                scores[rows, 5 * part:5 * part + 5, cols],
                                g.bank[bk.bank(("half64", part))][rows, 0:320].rearrange("p (c t) -> p c t", t=64),
                                ACT.Copy)
                        bk.read(ins, ("half64", part))
                    bk.wait_read(act, h, ("level", MASKED - 1, 1))
                    for j in range(4):
                        rows = slice(32 * j, 32 * j + 32)
                        ins = nc.scalar.activation(scores[rows, :, rows], diag[rows, :, :], ACT.Copy)
                    ins.then_inc(placed, 1)
                if step == S_KEYS:
                    for d, n in STATE_ORDER:
                        c0, kc = GROUPS[n]
                        to_sbuf(h, ("kt", d, n), flat(k_tok[d], c0, kc), kc * P)
                if step in (S_OUT, S_OUT2):
                    act.wait_ge(vecs_ready, h * 3 + 3)
                    for n in ((0,), (1, 2))[step - S_OUT]:
                        t0, tn = TOK_BLOCKS[n]
                        bk.wait_full(act, h, ("out", n))
                        out = g.bank[bk.bank(("out", n))][:, 0:tn]
                        nc.scalar.activation(o_sq[:, t0:t0 + tn], out, ACT.Square).then_inc(squared, 1)
                        bk.read(nc.scalar.activation(o_gain[:, t0:t0 + tn], out, ACT.Copy, scale=head_vecs[:, 4:5]),
                                ("out", n))
                if step == S_SUM:
                    bk.wait_full(act, h, ("sum",))
                    bk.read(nc.scalar.activation(root[:, :], g.bank[bk.bank(("sum",))][:, 0:CHUNKS], ACT.Sqrt,
                                                 bias=g.eps[:, 0:1], scale=1.0 / P), ("sum",))
                if S_GATES <= step < S_GATES + 4:
                    d, ax = divmod(step - S_GATES, 2)
                    for n, (t0, tn) in enumerate(TOK_BLOCKS):
                        name = ("lru", d, ax, n)
                        bk.wait_full(act, h, name)
                        bk.read(nc.scalar.activation((r, ig)[ax][d][:, t0:t0 + tn], g.bank[bk.bank(name)][:, 0:tn],
                                                     ACT.Sigmoid, bias=head_vecs[:, 2 * ax + d:2 * ax + d + 1]), name)
                if step in (S_GATES + 1, S_GATES + 4):
                    d = (step - S_GATES) // 4
                    if d:
                        act.wait_ge(scanned, h * 7 + 2)
                    for n in range(3):
                        bk.wait_read(act, h, ("lru", d, 0, n))
                    nc.scalar.activation(dec[:, :], r[d][:, :], ACT.Exp, scale=head_vecs[:, 7 + d:8 + d]
                                         ).then_inc(lru_exp, 1)
                    act.wait_ge(lru_exp, h * 6 + 3 * d + 1)
                    nc.scalar.activation(r[d][:, :], r[d][:, :], ACT.Tanh, scale=head_vecs[:, 5 + d:6 + d]
                                         ).then_inc(lru_exp, 1)
                    nc.scalar.activation(sq[:, :], dec[:, :], ACT.Square).then_inc(lru_exp, 1)
                if step in (S_GATES + 2, S_GATES + 5):
                    d = (step - S_GATES - 2) // 3
                    act.wait_ge(gap_ready, h * 2 + d + 1)
                    nc.scalar.activation(sq[:, :], sq[:, :], ACT.Sqrt).then_inc(gap_root, 1)
                if step == S_GATES + 6:
                    act.wait_ge(tile_in[T_LG], h * 16 + 16)
                    nc.scalar.activation(lg[:, :], lg[:, :], ACT.Gelu_apprx_tanh).then_inc(lg_ready, 1)

            act.wait_ge(small_dve, 3)
            nc.scalar.activation(lb, small[:, 5, :], ACT.Sigmoid).then_inc(small_act, 1)
            nc.scalar.activation(small[:, 7, :], small[:, 6, :], ACT.Exp, scale=-1.0).then_inc(small_act, 1)
            act.wait_ge(small_dve, SMALL_STEPS)
            split_weights(nc, act, None, 0, 0, ring, raw_in, hi_ready, lo_ready, used)
            turns(act, project, mix)
            for s in range(2):
                act.wait_ge(stored[s], IN_BLOCKS // 2 * 16)

        @block.tensor
        def _(pe):
            def blocks(tensor, c, size, j):
                return tensor[:, c * P + size * j:c * P + size * j + size]

            def project(h, u, last):
                j, b = divmod(u, 3)
                s, i = j % 2, h * (PER_HEAD // 2) + j // 2
                t0, n = TOK_BLOCKS[b]
                if b == 0:
                    pe.wait_ge(lo_ready[s], i + 1)
                if b == 2:
                    pe.wait_ge(staged[s], i * 3 + 1)
                elif s == 1:
                    pe.wait_ge(staged[0], i * 3 + b + 2)
                elif not first(i):
                    pe.wait_ge(staged[1], (i - 1) * 3 + b + 2)
                for kt in range(KT):
                    ins = exact_product(nc, g.bank[u % 2][:, 0:n], ring.hi[:, s, kt * P:(kt + 1) * P],
                                        ring.lo[:, s, kt * P:(kt + 1) * P], g.h_hi[:, kt, t0:t0 + n],
                                        g.h_lo[:, kt, t0:t0 + n], kt == 0, kt == KT - 1)
                ins.then_inc(used[s] if b == 2 else unit_full[b], 1)
                if b == 2:
                    pe.wait_ge(ada_in[s], i * 16 + 16)
                    for kt in range(KT):
                        ins = nc.tensor.matmul(g.bank[2][:, ds((i * 2 + s) * 2, 2)], ada_raw[:, s, kt * P:(kt + 1) * P],
                                               g.cond_s[:, kt, :], start=(kt == 0), stop=(kt == KT - 1))
                    ins.then_inc(ada_used[s], 1)

            def square_scores(h, name):
                d = name[2]
                for c in range(CHUNKS):
                    for j in range(4):
                        ins = nc.tensor.matmul(g.bank[bk.bank(name)][32 * j:32 * j + 32, c * 32:(c + 1) * 32],
                                               blocks(k[d], c, 32, j), blocks(q[d], c, 32, j), start=True, stop=True)
                bk.filled(ins, name)

            def transpose(h, name, src, c0, kc):
                bk.wait_free(pe, h, name)
                for c in range(kc):
                    ins = nc.tensor.transpose(g.bank[bk.bank(name)][:, c * P:(c + 1) * P],
                                              src[:, (c0 + c) * P:(c0 + c + 1) * P], g.ident[:, :])
                bk.filled(ins, name)

            def mix(h, step):
                if step == S_SELF:
                    pe.wait_ge(tile_in[T_V], h * 16 + 16)
                    for n, (c0, kc) in enumerate(GROUPS):
                        transpose(h, ("vt", n), v, c0, kc)
                    bk.wait_free(pe, h, ("diag",))
                    pe.wait_ge(q_ready, h * 2 + 2)
                    pe.wait_ge(kf_ready, h * 4 + 4)
                    for c in range(CHUNKS):
                        for j in range(4):
                            for d in range(DIRS):
                                ins = nc.tensor.matmul(
                                    g.bank[bk.bank(("diag",))][32 * j:32 * j + 32, c * 32:(c + 1) * 32],
                                    blocks(k[d], c, 32, j), blocks(q[d], c, 32, j), start=(d == 0), stop=(d == 1))
                    bk.filled(ins, ("diag",))
                if S_LEVELS <= step < S_LEVELS + MASKED:
                    level = step - S_LEVELS
                    for d in range(DIRS):
                        name = ("level", level, d)
                        bk.wait_free(pe, h, name)
                        pe.wait_ge(qk_ready, h * QK_N + qk_count(level, d))
                        square_scores(h, name)
                if step == S_HALF32:
                    bk.wait_free(pe, h, ("half32",))
                    pe.wait_ge(qk_ready, h * QK_N + qk_count(MASKED, 1))
                    for c in range(CHUNKS):
                        for j in range(4):
                            d = j % 2
                            ins = nc.tensor.matmul(g.bank[bk.bank(("half32",))][32 * j:32 * j + 32, c * 32:(c + 1) * 32],
                                                   blocks(k[d], c, 32, j), blocks(q[d], c, 32, j ^ 1),
                                                   start=True, stop=True)
                    bk.filled(ins, ("half32",))
                if step == S_HALF64:
                    pe.wait_ge(qk_ready, h * QK_N + qk_count(MASKED + 1, 1))
                    for part in range(2):
                        name = ("half64", part)
                        bk.wait_free(pe, h, name)
                        for c in range(5):
                            for d in range(DIRS):
                                ins = nc.tensor.matmul(g.bank[bk.bank(name)][64 * d:64 * d + 64, c * 64:(c + 1) * 64],
                                                       blocks(k[d], 5 * part + c, 64, d),
                                                       blocks(q[d], 5 * part + c, 64, 1 - d), start=True, stop=True)
                        bk.filled(ins, name)
                if step == S_KEYS:
                    pe.wait_ge(qk_ready, h * QK_N + QK_N)
                    for d, n in STATE_ORDER:
                        transpose(h, ("kt", d, n), k[d], *GROUPS[n])
                if step in (S_ADD, S_ADD2):
                    for d, n in (STATE_ORDER[:4], STATE_ORDER[4:])[step - S_ADD]:
                        c0, kc = GROUPS[n]
                        name = ("ds", d, n)
                        bk.wait_read(pe, h, ("kt", d, n))
                        bk.wait_free(pe, h, name)
                        for c in range(kc):
                            ins = nc.tensor.matmul(g.bank[bk.bank(name)][:, c * P:(c + 1) * P], k_tok[d][:, c0 + c, :],
                                                   v_tok[:, c0 + c, :], start=True, stop=True)
                        bk.filled(ins, name)
                if step in (S_OUT, S_OUT2):
                    pe.wait_ge(placed, h + 1)
                    pe.wait_ge(states_in, h * 32 + 32)
                    for n in ((0,), (1, 2))[step - S_OUT]:
                        c0, kc = GROUPS[n]
                        name = ("out", n)
                        bk.wait_free(pe, h, name)
                        bk.wait_read(pe, h, ("ds",) + ((1, 0), (1, 1), (0, 2))[n])
                        for c in range(kc):
                            out = g.bank[bk.bank(name)][:, c * P:(c + 1) * P]
                            at_c = slice((c0 + c) * P, (c0 + c + 1) * P)
                            nc.tensor.matmul(out, v_tok[:, c0 + c, :], scores[:, c0 + c, :], start=True, stop=False)
                            nc.tensor.matmul(out, state[0][:, c0 + c, :], q[0][:, at_c], start=False, stop=False)
                            ins = nc.tensor.matmul(out, state[1][:, c0 + c, :], q[1][:, at_c], start=False, stop=True)
                        bk.filled(ins, name)
                if step == S_SUM:
                    bk.wait_free(pe, h, ("sum",))
                    pe.wait_ge(squared, h * 3 + 3)
                    for c in range(CHUNKS):
                        ins = nc.tensor.matmul(g.bank[bk.bank(("sum",))][:, c:c + 1], o_sq[:, c * P:(c + 1) * P],
                                               g.ones[:, 0:1], start=True, stop=True)
                    bk.filled(ins, ("sum",))
                if step == S_SPREAD:
                    pe.wait_ge(rstd_ready, h + 1)
                    for n, (c0, kc) in enumerate(GROUPS):
                        bk.wait_free(pe, h, ("spread", n))
                        for c in range(kc):
                            ins = nc.tensor.matmul(g.bank[bk.bank(("spread", n))][:, c * P:(c + 1) * P],
                                                   rstd[:, c0 + c:c0 + c + 1].broadcast_to([P, P]), g.ident[:, :],
                                                   start=True, stop=True)
                        bk.filled(ins, ("spread", n))
                if S_GATES <= step < S_GATES + 4:
                    d, ax = divmod(step - S_GATES, 2)
                    pe.wait_ge(conv, h * CONV_N + CONV_N)
                    pe.wait_ge(lru_w_in, h * 64 + 64)
                    for n, (t0, tn) in enumerate(TOK_BLOCKS):
                        name = ("lru", d, ax, n)
                        bk.wait_free(pe, h, name)
                        bk.filled(nc.tensor.matmul(g.bank[bk.bank(name)][:, 0:tn], lru_w[:, 2 * ax + d, :],
                                                   xc[:, t0:t0 + tn], start=True, stop=True), name)

            turns(pe, project, mix)

        @block.vector
        def _(dve):
            def project(h, u, last):
                j, b = divmod(u, 3)
                if b == 0 and not (last and j == PER_HEAD - 1):
                    split_weights(nc, None, dve, h * (PER_HEAD // 2) + (j + 1) // 2, 1 - j % 2, ring, raw_in, hi_ready,
                                  lo_ready, used)
                if u == 19:
                    if not first(h):
                        dve.wait_ge(tile_done, h)
                    for d in range(DIRS):
                        at_h = ds(h + 4 * d)
                        dve.wait_ge(sig_ready, h * 2 + d + 1)
                        nc.vector.tensor_scalar(k[d][:, :], f[d][:, :], neg_lb[:, at_h], one_lb[:, at_h],
                                                ALU.mult, ALU.add).then_inc(kf_ready, 1)
                        nc.vector.tensor_scalar(f[d][:, :], f[d][:, :], one_lb[:, at_h], lb[:, at_h],
                                                ALU.mult, ALU.add).then_inc(kf_ready, 1)

            def one_level(h, level):
                size = 2 ** level
                pairs = TOKENS // (2 * size)
                for d in range(DIRS):
                    for name in ([("level", level, d)], [("half32",)], [("half64", 0), ("half64", 1)]
                                 )[max(0, level - MASKED + 1)]:
                        bk.wait_full(dve, h, name)
                    totals = f[d][:, :].rearrange("p (n two s) -> p n two s", two=2, s=size)
                    if level:
                        dve.wait_ge(tot_ready, h * 14 + 2 * (level - 1) + d + 1)
                    for t, half in ((q[d], 1 - d), (k[d], d)):
                        part = t[:, :].rearrange("p (n two b) -> p n two b", two=2, b=size)[:, :, half, :]
                        nc.vector.tensor_tensor(part, part, totals[:, :, 1 - half, 0:1].broadcast_to([P, pairs, size]),
                                                ALU.mult).then_inc(qk_ready, 1)
                    dve.wait_ge(qk_ready, h * QK_N + qk_count(level + 1, d))
                    if level < MASKED:
                        bk.wait_read(dve, h, ("level", level, 0) if d else ("level", level - 1, 1) if level else ("diag",))
                    nc.vector.tensor_tensor(totals[:, :, 0, 0], totals[:, :, 0, 0], totals[:, :, 1, 0], ALU.mult
                                            ).then_inc(tot_ready, 1)
                    if level < MASKED:
                        name, mask = ("level", level, d), 1 + 2 * level + d
                        bk.read(nc.vector.copy_predicated(
                            diag[:, :, :], masks[:, mask:mask + 1, :].bitcast(I32).broadcast_to([P, CHUNKS, 32]),
                            g.bank[bk.bank(name)][:, 0:CHUNKS * 32].rearrange("p (c t) -> p c t", t=32)), name)

            def states(h, order):
                for d, n in order:
                    name = ("ds", d, n)
                    bk.wait_full(dve, h, name)
                    if n:
                        before = [m for e, m in STATE_ORDER if e == d]
                        bk.wait_read(dve, h, ("ds", d, before[before.index(n) - 1]))
                    todo = state_steps(d, n)
                    for i, (c, into) in enumerate(todo):
                        if i:
                            dve.wait_ge(state_step, h * STATE_STEPS + state_at[d, n] + i)
                        c_in = c - GROUPS[n][0]
                        ins = nc.vector.scalar_tensor_tensor(
                            last_state[d][:, :] if into is None else state[d][:, into, :], state[d][:, c, :],
                            f[d][:, c * P:c * P + 1], g.bank[bk.bank(name)][:, c_in * P:(c_in + 1) * P],
                            ALU.mult, ALU.add)
                        if i == len(todo) - 1:
                            bk.read(ins, name)
                        else:
                            ins.then_inc(state_step, 1)
            state_at, total = {}, 0
            for d, n in STATE_ORDER:
                state_at[d, n] = total
                total += len(state_steps(d, n)) - 1
            assert total == STATE_STEPS

            def convolve(h, taps):
                for tap in taps:
                    if tap == CONV_LEFT:
                        nc.vector.tensor_scalar(xc[:, :], lx[:, :], g.v("conv_w", h + 4 * tap), g.v("conv_b", h),
                                                ALU.mult, ALU.add).then_inc(conv, 1)
                        continue
                    shift = tap - CONV_LEFT
                    dve.wait_ge(conv, h * CONV_N + 1 + 2 * (0, 1, 3).index(tap))
                    for t0, tn, _ in SEGS:
                        lo, hi = t0 + max(0, -shift), t0 + tn - max(0, shift)
                        nc.vector.scalar_tensor_tensor(xc[:, lo:hi], lx[:, lo + shift:hi + shift],
                                                       g.v("conv_w", h + 4 * tap), xc[:, lo:hi], ALU.mult, ALU.add
                                                       ).then_inc(conv, 1)

            def scan(h, d):
                dve.wait_ge(gap_root, h * 2 + d + 1)
                dve.wait_ge(ix_ready, h * 2 + d + 1)
                nc.vector.tensor_tensor(ig[d][:, :], ig[d][:, :], sq[:, :], ALU.mult).then_inc(u_ready, 1)
                dve.wait_ge(u_ready, h * 2 + d + 1)
                for t0, tn, c in SEGS:
                    view = lambda t: t[:, t0:t0 + tn] if d == 0 else t[:, t0:t0 + tn][:, ::-1]
                    nc.vector.tensor_tensor_scan(view(r[d]), view(dec), view(ig[d]),
                                                 g.v("h0", h + 4 * d) if c else 0.0, ALU.mult, ALU.add
                                                 ).then_inc(scanned, 1)

            def mix(h, step):
                if step == S_SELF:
                    bk.wait_full(dve, h, ("diag",))
                    for d in range(DIRS):
                        dve.wait_ge(kf_ready, h * 4 + 2 * d + 2)
                        nc.vector.tensor_tensor(q[d][:, :], q[d][:, :], f[d][:, :], ALU.mult).then_inc(qk_ready, 1)
                    bk.read(nc.vector.tensor_tensor(
                        diag[:, :, :], g.bank[bk.bank(("diag",))][:, 0:CHUNKS * 32].rearrange("p (c t) -> p c t", t=32),
                        masks[:, 0:1, :].broadcast_to([P, CHUNKS, 32]), ALU.mult), ("diag",))
                    if not first(h):
                        dve.wait_ge(scanned, h * 7)
                    nc.vector.memset(state[0][:, 0, :], 0.0).then_inc(states_zero, 1)
                    nc.vector.memset(state[1][:, CTX_CHUNKS - 1, :], 0.0).then_inc(states_zero, 1)
                if S_LEVELS <= step < S_LEVELS + LEVELS:
                    one_level(h, step - S_LEVELS)
                if step == S_KEYS:
                    nc.vector.tensor_copy(head_vecs[:, 0:4], g.vecs[:, VEC["ba"]:VEC["ba"] + 16].rearrange(
                        "p (n t) -> p n t", t=HEADS)[:, :, ds(h)].rearrange("p n a -> p (n a)")).then_inc(vecs_ready, 1)
                    nc.vector.tensor_copy(head_vecs[:, 4:5], g.v("hg_gain", h)).then_inc(vecs_ready, 1)
                    nc.vector.tensor_copy(head_vecs[:, 5:9], small[:, 3:5, :].rearrange(
                        "p n (d t) -> p (n d) t", t=HEADS)[:, :, ds(h)].rearrange("p n a -> p (n a)")
                                          ).then_inc(vecs_ready, 1)
                if step == S_ADD:
                    dve.wait_ge(states_in, h * 32 + 32)
                    dve.wait_ge(tot_ready, h * 14 + 14)
                    states(h, STATE_ORDER[:4])
                if step == S_ADD2:
                    states(h, STATE_ORDER[4:])
                if step == S_OUT:
                    dve.wait_ge(tile_in[T_LX], h * 16 + 16)
                    convolve(h, (CONV_LEFT, 0, 1))
                if step == S_OUT2:
                    convolve(h, (3,))
                if step == S_SUM:
                    bk.wait_read(dve, h, ("sum",))
                    nc.vector.reciprocal(rstd[:, :], root[:, :]).then_inc(rstd_ready, 1)
                if step == S_SPREAD:
                    dve.wait_ge(gate_ready, h + 1)
                    for n, (t0, tn) in enumerate(TOK_BLOCKS):
                        name = ("spread", n)
                        bk.wait_full(dve, h, name)
                        bk.wait_read(dve, h, ("out", n))
                        bk.read(nc.vector.tensor_tensor(o_gain[:, t0:t0 + tn], o_gain[:, t0:t0 + tn],
                                                        g.bank[bk.bank(name)][:, 0:tn], ALU.mult), name)
                    for n in range(3):
                        bk.wait_read(dve, h, ("spread", n))
                    nc.vector.tensor_tensor(gate[:, :], o_gain[:, :], gate[:, :], ALU.mult).then_inc(head_done, 1)
                if step in (S_GATES + 1, S_GATES + 3):
                    d = (step - S_GATES) // 2
                    for n in range(3):
                        bk.wait_read(dve, h, ("lru", d, 1, n))
                    nc.vector.tensor_tensor(ig[d][:, :], ig[d][:, :], xc[:, :], ALU.mult).then_inc(ix_ready, 1)
                if step in (S_GATES + 1, S_GATES + 4):
                    d = (step - S_GATES) // 4
                    dve.wait_ge(lru_exp, h * 6 + 3 * d + 3)
                    nc.vector.scalar_tensor_tensor(sq[:, :], sq[:, :], 1.0, r[d][:, :], ALU.add, ALU.mult
                                                   ).then_inc(gap_ready, 1)
                if step == S_GATES + 2:
                    scan(h, 0)
                if step == S_GATES + 5:
                    scan(h, 1)
                    dve.wait_ge(scanned, h * 7 + 4)
                    for d, t in ((0, CTX - 1), (1, 0)):
                        nc.vector.tensor_copy(new_lru[:, ds(h + 4 * d)], r[d][:, t:t + 1]).then_inc(scanned, 1)
                if step == S_GATES + 6:
                    dve.wait_ge(scanned, h * 7 + 6)
                    nc.vector.tensor_tensor(r[0][:, :], r[0][:, :], r[1][:, :], ALU.add).then_inc(scanned, 1)
                    dve.wait_ge(scanned, h * 7 + 7)
                    dve.wait_ge(lg_ready, h + 1)
                    nc.vector.tensor_tensor(lg[:, :], r[0][:, :], lg[:, :], ALU.mult).then_inc(tile_done, 1)

            for free in bk.free.values():
                dve.sem_inc(free, 1)
            nc.vector.memset(lru_w[:, :, :], 0.0).then_inc(zeroed, 1)
            small_constants(nc, dve, g, small, small_dve, small_act)
            dve.wait_ge(const_in, 16)
            split_weights(nc, None, dve, 0, 0, ring, raw_in, hi_ready, lo_ready, used)
            turns(dve, project, mix)
            nc.vector.tensor_tensor(g.mod[:, 16:48, :], g.bank[2][:, 0:64].rearrange("p (j c) -> p j c", c=2),
                                    g.v("b_ada", 16, 32).unsqueeze(2).broadcast_to([P, 32, 2]), ALU.add
                                    ).then_inc(mod_done, 1)
            dve.wait_ge(mod_done, 1)
            nc.vector.scalar_tensor_tensor(g.amp2[:, :, :], g.mod[:, 32:40, :], 1.0,
                                           g.v("norm2", 0, 8).unsqueeze(2).broadcast_to([P, 8, 2]), ALU.add, ALU.mult
                                           ).then_inc(mod_done, 1)
            dve.wait_ge(mod_done, 2)


def output_projection(nc, g, a):
    ctx = ExitStack()
    with ctx:
        sem = lambda n: ctx.enter_context(nc.semaphore("out_" + n))
        two = lambda n: [sem(f"{n}{s}") for s in range(2)]
        ring = Ring(nc, "out_", 120)
        raw_in, hi_ready, lo_ready, used = two("raw_in"), two("hi_ready"), two("lo_ready"), two("used")
        x_in, mix_in, mix_hi, mix_lo = sem("x_in"), sem("mix_in"), sem("mix_hi"), sem("mix_lo")
        full = [sem(f"full{b}") for b in range(2)]
        added = sem("added")
        turns = KT // 2
        block = ctx.enter_context(nc.Block())

        @block.sync
        def _(sp):
            sp.dma_start(g.mix[:, :, :], g.mix_out.rearrange("k p n -> p k n")).then_inc(mix_in, 16)

            def load(i):
                for s in range(2):
                    if not first(i):
                        sp.wait_ge(lo_ready[s], i)
                    sp.dma_start(ring.raw[:, s, :], a["w_out"][ds(i * 2 + s), :, :].rearrange("a p n -> p (a n)")
                                 ).then_inc(raw_in[s], 16)
            load(0)
            sp.dma_start(g.x[:, :, :].rearrange("p k t -> p (k t)"), g.x_scratch).then_inc(x_in, 16)
            with sp.Fori(1, turns) as i:
                load(i)

        @block.scalar
        def _(act):
            act.wait_ge(mix_in, 16)
            with act.Fori(0, KT) as t:
                nc.scalar.activation(g.h_hi[:, ds(t), :], g.mix[:, ds(t), :], ACT.Copy).then_inc(mix_hi, 1)

            def turn(i):
                for s in range(2):
                    split_weights(nc, act, None, i, s, ring, raw_in, hi_ready, lo_ready, used)
            peeled(act, turns, turn)

        @block.vector
        def _(dve):
            with dve.Fori(0, KT) as t:
                dve.wait_ge(mix_hi, t + 1)
                nc.vector.tensor_tensor(g.h_lo[:, ds(t), :], g.mix[:, ds(t), :], g.h_hi[:, ds(t), :].bitcast(F32),
                                        ALU.subtract).then_inc(mix_lo, 1)
            dve.wait_ge(x_in, 16)
            split_weights(nc, None, dve, 0, 0, ring, raw_in, hi_ready, lo_ready, used)

            def turn(i, last=False):
                for s in range(2):
                    if not (last and s):
                        split_weights(nc, None, dve, i + s, 1 - s, ring, raw_in, hi_ready, lo_ready, used)
                    for b, (t0, n) in enumerate(TOK_BLOCKS):
                        if b < 2:
                            dve.wait_ge(full[b], i * 2 + s + 1)
                        else:
                            dve.wait_ge(used[s], i + 1)
                        xs = g.x[:, ds(i * 2 + s), t0:t0 + n].rearrange("p a t -> p (a t)")
                        nc.vector.scalar_tensor_tensor(xs, g.bank[b][:, 0:n], g.m(16 + i * 2 + s, int(b > 0)), xs,
                                                       ALU.mult, ALU.add).then_inc(added, 1)
            with dve.Fori(0, turns - 1) as i:
                turn(i)
            turn(turns - 1, last=True)
            dve.wait_ge(added, 3 * KT)

        @block.tensor
        def _(pe):
            pe.wait_ge(mix_lo, KT)

            def turn(i):
                for s in range(2):
                    pe.wait_ge(lo_ready[s], i + 1)
                    for b, (t0, n) in enumerate(TOK_BLOCKS):
                        if not (first(i) and s == 0):
                            pe.wait_ge(added, (i * 2 + s - 1) * 3 + b + 1)
                        for k in range(KT):
                            last = exact_product(nc, g.bank[b][:, 0:n], ring.hi[:, s, k * P:(k + 1) * P],
                                                 ring.lo[:, s, k * P:(k + 1) * P], g.h_hi[:, k, t0:t0 + n],
                                                 g.h_lo[:, k, t0:t0 + n], k == 0, k == KT - 1)
                        last.then_inc(used[s] if b == 2 else full[b], 1)
            peeled(pe, turns, turn)


def mlp(nc, g, a):
    ctx = ExitStack()
    with ctx:
        sem = lambda n: ctx.enter_context(nc.semaphore("ff_" + n))
        two = lambda n: [sem(f"{n}{s}") for s in range(2)]
        up = Ring(nc, "up_", 120)
        down = Ring(nc, "down_", 144, raw_slots=1)
        hid_hi = at(nc, "hid_hi", [P, 4, TOKENS], F32R, 164)
        hid_lo = at(nc, "hid_lo", [P, 4, TOKENS], F32R, 184)
        hid_relu = at(nc, "hid_relu", [P, 4, TOKENS], F32, 184)
        up_in, up_hi, up_lo, up_used = two("up_in"), two("up_hi"), two("up_lo"), two("up_used")
        down_in, down_hi, down_lo = sem("down_in"), sem("down_hi"), sem("down_lo")
        full = [sem(f"full{b}") for b in range(2)]
        relu_ready, squared, hid_hi_ready, hid_lo_ready = (
            sem("relu_ready"), sem("squared"), sem("hid_hi_ready"), sem("hid_lo_ready"))
        DOWN_BANKS = 4
        UNITS = KT * 3
        unit_full = [sem(f"unit_full{u}") for u in range(DOWN_BANKS)]
        unit_added = [sem(f"unit_added{u}") for u in range(DOWN_BANKS)]
        PER = UNITS // DOWN_BANKS
        pairs = FF_BLOCKS // 2
        block = ctx.enter_context(nc.Block())

        def over_pairs(eng, step):
            step(0, 0)
            step(1, 1)
            with eng.Fori(1, (pairs - 2) // 2) as i:
                step(i * 2, 0)
                step(i * 2 + 1, 1)
            step(pairs - 2, 0)

        @block.sync
        def _(sp):
            def load_up(p, s):
                if not first(p):
                    sp.wait_ge(up_lo[s], p)
                sp.dma_start(up.raw[:, s, :], a["w_ff1"][ds(p * 2 + s), :, :].rearrange("a p n -> p (a n)")
                             ).then_inc(up_in[s], 16)

            def load_down(p, s):
                if not (first(p) and s == 0):
                    sp.wait_ge(down_lo, p * 2 + s)
                sp.dma_start(down.raw[:, 0, :], a["w_ff2"][ds(p * 2 + s), :, :].rearrange("a p n -> p (a n)")
                             ).then_inc(down_in, 16)

            for s in range(2):
                load_up(0, s)
            for s in range(2):
                load_up(1, s)
            load_down(0, 0)
            load_down(0, 1)

            def step(p, parity):
                for s in range(2):
                    load_up(p + 2, s)
                for s in range(2):
                    load_down(p + 1, s)
            with sp.Fori(0, pairs - 2) as p:
                step(p, 0)
            for s in range(2):
                load_down(pairs - 1, s)

        def up_weights(p, s, act=None, dve=None):
            if act is not None:
                act.wait_ge(up_in[s], p * 16 + 16)
                if not first(p):
                    act.wait_ge(up_used[s], p)
                nc.scalar.activation(up.hi[:, s, :], up.raw[:, s, :], ACT.Copy).then_inc(up_hi[s], 1)
            else:
                dve.wait_ge(up_hi[s], p + 1)
                nc.vector.tensor_tensor(up.lo[:, s, :], up.raw[:, s, :], up.hi[:, s, :].bitcast(F32), ALU.subtract
                                        ).then_inc(up_lo[s], 1)

        def down_weights(p, s, act=None, dve=None):
            if act is not None:
                act.wait_ge(down_in, (p * 2 + s) * 16 + 16)
                if not first(p):
                    act.wait_ge(unit_full[(UNITS - 1) % DOWN_BANKS], p * PER)
                nc.scalar.activation(down.hi[:, s, :], down.raw[:, 0, :], ACT.Copy).then_inc(down_hi, 1)
            else:
                dve.wait_ge(down_hi, p * 2 + s + 1)
                nc.vector.tensor_tensor(down.lo[:, s, :], down.raw[:, 0, :], down.hi[:, s, :].bitcast(F32), ALU.subtract
                                        ).then_inc(down_lo, 1)

        def hidden(p, parity, act=None, dve=None):
            for s in range(2):
                for b, (t0, n) in enumerate(TOK_BLOCKS):
                    at_n = (p * 2 + s) * 3 + b + 1
                    dst = (slice(None), 2 * parity + s, slice(t0, t0 + n))
                    if act is not None:
                        if b < 2:
                            act.wait_ge(full[b], p * 2 + s + 1)
                        else:
                            act.wait_ge(up_used[s], p + 1)
                        nc.scalar.activation(hid_relu[dst], g.bank[b][:, 0:n], ACT.Relu).then_inc(relu_ready, 1)
                        act.wait_ge(relu_ready, at_n)
                        nc.scalar.activation(hid_hi[dst], hid_relu[dst], ACT.Square).then_inc(hid_hi_ready, 1)
                        continue
                    dve.wait_ge(relu_ready, at_n)
                    nc.vector.tensor_tensor(g.bank[b][:, 0:n], hid_relu[dst], g.bank[b][:, 0:n], ALU.mult
                                            ).then_inc(squared, 1)
                    dve.wait_ge(squared, at_n)
                    dve.wait_ge(hid_hi_ready, at_n)
                    nc.vector.tensor_tensor(hid_lo[dst], g.bank[b][:, 0:n], hid_hi[dst].bitcast(F32), ALU.subtract
                                            ).then_inc(hid_lo_ready, 1)

        @block.scalar
        def _(act):
            for s in range(2):
                up_weights(0, s, act=act)
            hidden(0, 0, act=act)
            for s in range(2):
                up_weights(1, s, act=act)

            def step(p, parity, last=False):
                for s in range(2):
                    down_weights(p, s, act=act)
                hidden(p + 1, 1 - parity, act=act)
                if not last:
                    for s in range(2):
                        up_weights(p + 2, s, act=act)
            step(0, 0)
            step(1, 1)
            with act.Fori(1, (pairs - 2) // 2) as i:
                step(i * 2, 0)
                step(i * 2 + 1, 1)
            step(pairs - 2, 0, last=True)
            for s in range(2):
                down_weights(pairs - 1, s, act=act)

        @block.vector
        def _(dve):
            def add(p, units):
                for u in units:
                    m, b = divmod(u, 3)
                    t0, n = TOK_BLOCKS[b]
                    dve.wait_ge(unit_full[u % DOWN_BANKS], p * PER + u // DOWN_BANKS + 1)
                    xs = g.x[:, m, t0:t0 + n]
                    nc.vector.scalar_tensor_tensor(xs, g.bank[3 + u % DOWN_BANKS][:, 0:n], g.m(40 + m, int(b > 0)), xs,
                                                   ALU.mult, ALU.add).then_inc(unit_added[u % DOWN_BANKS], 1)
            for s in range(2):
                up_weights(0, s, dve=dve)
            hidden(0, 0, dve=dve)
            for s in range(2):
                up_weights(1, s, dve=dve)

            def step(p, parity, last=False):
                for s in range(2):
                    down_weights(p, s, dve=dve)
                hidden(p + 1, 1 - parity, dve=dve)
                add(p, range(0, 8))
                if not last:
                    for s in range(2):
                        up_weights(p + 2, s, dve=dve)
                add(p, range(8, UNITS))
            step(0, 0)
            step(1, 1)
            with dve.Fori(1, (pairs - 2) // 2) as i:
                step(i * 2, 0)
                step(i * 2 + 1, 1)
            step(pairs - 2, 0, last=True)
            for s in range(2):
                down_weights(pairs - 1, s, dve=dve)
            add(pairs - 1, range(UNITS))
            for u in range(DOWN_BANKS):
                dve.wait_ge(unit_added[u], pairs * PER)

        @block.tensor
        def _(pe):
            def up_product(p):
                for s in range(2):
                    pe.wait_ge(up_lo[s], p + 1)
                    for b, (t0, n) in enumerate(TOK_BLOCKS):
                        if not (first(p) and s == 0):
                            pe.wait_ge(hid_lo_ready, (p * 2 + s - 1) * 3 + b + 1)
                        for k in range(KT):
                            last = exact_product(nc, g.bank[b][:, 0:n], up.hi[:, s, k * P:(k + 1) * P],
                                                 up.lo[:, s, k * P:(k + 1) * P], g.h_hi[:, k, t0:t0 + n],
                                                 g.h_lo[:, k, t0:t0 + n], k == 0, k == KT - 1)
                        last.then_inc(up_used[s] if b == 2 else full[b], 1)

            def down_product(p, parity):
                pe.wait_ge(down_lo, p * 2 + 2)
                pe.wait_ge(hid_lo_ready, p * 6 + 6)
                for u in range(UNITS):
                    m, b = divmod(u, 3)
                    t0, n = TOK_BLOCKS[b]
                    if not (first(p) and u < DOWN_BANKS):
                        pe.wait_ge(unit_added[u % DOWN_BANKS], p * PER + u // DOWN_BANKS)
                    for s in range(2):
                        last = exact_product(nc, g.bank[3 + u % DOWN_BANKS][:, 0:n], down.hi[:, s, m * P:(m + 1) * P],
                                             down.lo[:, s, m * P:(m + 1) * P], hid_hi[:, 2 * parity + s, t0:t0 + n],
                                             hid_lo[:, 2 * parity + s, t0:t0 + n], s == 0, s == 1)
                    last.then_inc(unit_full[u % DOWN_BANKS], 1)

            up_product(0)

            def step(p, parity):
                up_product(p + 1)
                down_product(p, parity)
            over_pairs(pe, step)
            down_product(pairs - 1, 1)


def output(nc, g, a):
    ctx = ExitStack()
    with ctx:
        sem = lambda n: ctx.enter_context(nc.semaphore("y_" + n))
        y = at(nc, "y_tok", [P, 2, D_MODEL], F32, 160)
        turned = [sem(f"turned{i}") for i in range(4)]
        moved = [sem(f"moved{i}") for i in range(4)]
        stored = [sem(f"stored{s}") for s in range(2)]
        n_tiles = TOKENS // P
        block = ctx.enter_context(nc.Block())

        @block.tensor
        def _(pe):
            def tile(i):
                for s in range(2):
                    for half in range(2):
                        b = 2 * s + half
                        if not first(i):
                            pe.wait_ge(moved[b], i)
                        for f in range(4):
                            last = nc.tensor.transpose(
                                g.bank[b][:, f * P:(f + 1) * P],
                                g.x[:, 4 * half + f, ds((i * 2 + s) * P, P)] if not isinstance(i, int) else
                                g.x[:, 4 * half + f, (i * 2 + s) * P:(i * 2 + s + 1) * P], g.ident[:, :])
                        last.then_inc(turned[b], 1)
            for i in range(n_tiles // 2):
                tile(i)

        def move(eng, copy, half):
            def tile(i):
                for s in range(2):
                    b = 2 * s + half
                    if not first(i):
                        eng.wait_ge(stored[s], i * 16)
                    eng.wait_ge(turned[b], i + 1)
                    copy(y[:, s, 512 * half:512 * half + 512], g.bank[b][:, :]).then_inc(moved[b], 1)
            peeled(eng, n_tiles // 2, tile)

        @block.vector
        def _(dve):
            move(dve, nc.vector.tensor_copy, 0)

        @block.scalar
        def _(act):
            move(act, lambda o, i: nc.scalar.activation(o, i, ACT.Copy), 1)

        @block.sync
        def _(sp):
            def store(i, dst):
                for s in range(2):
                    for half in range(2):
                        sp.wait_ge(moved[2 * s + half], i + 1)
                    sp.dma_start(dst(s), y[:, s, :]).then_inc(stored[s], 16)
            store(0, lambda s: a["y_prompt"][s * P:(s + 1) * P, :])
            with sp.Fori(1, n_tiles // 2) as i:
                store(i, lambda s: a["y_sample"][ds((i * 2 + s) * P - CTX, P), :])
            for s in range(2):
                sp.wait_ge(stored[s], 16 * (n_tiles // 2))


def backbone_step(nc, a):
    g = Ctx()
    low = [BASE]

    def const(name, shape, dtype=F32):
        size = 4
        for n in shape[1:]:
            size *= n
        t = nc.alloc_sbuf_tensor_at(name, shape, dtype, offset=low[0])
        low[0] += (size + 31) // 32 * 32
        assert low[0] <= AREA
        return t
    g.ident, g.ones = const("ident_sb", [P, P]), const("ones", [P, P])
    g.vecs, g.eps, g.cond_s = const("vecs_sb", [P, NVEC]), const("eps", [P, 1]), const("cond_silu", [P, KT, 2])
    g.mod = const("mod", [P, ADA_BLOCKS, 2])
    g.amp1, g.amp2 = const("amp1", [P, KT, 2]), const("amp2", [P, KT, 2])
    g.h_hi = at(nc, "h_hi", [P, KT, TOKENS], F32R, 0)
    g.h_lo = at(nc, "h_lo", [P, KT, TOKENS], F32R, 40)
    g.x = at(nc, "x", [P, KT, TOKENS], F32, 80)
    g.mix = at(nc, "mix", [P, KT, TOKENS], F32, 164)
    g.proj = nc.dram_tensor("proj", [IN_BLOCKS, P, TOKENS], F32, kind="Internal").ap()
    g.mix_out = nc.dram_tensor("mix_out", [KT, P, TOKENS], F32, kind="Internal").ap()
    g.x_scratch = nc.dram_tensor("x_scratch", [P, KT * TOKENS], F32, kind="Internal").ap()

    def v(name, i, n=1):
        return g.vecs[:, ds(VEC[name] + i, n)]
    g.v = v
    g.m = lambda j, c: g.mod[:, ds(j), c]
    ctx = ExitStack()
    with ctx:
        g.constants_ready = ctx.enter_context(nc.semaphore("constants_ready"))
        g.bank = [ctx.enter_context(nc.psum_tensor(f"bank{b}", [P, 512], F32)) for b in range(8)]
        modulation_and_input(nc, g, a)
        norm(nc, g, "norm1_", lambda k, c: g.amp1[:, ds(k), c], lambda k, c: g.m(k, c), True)
        projection_and_mixers(nc, g, a)
        output_projection(nc, g, a)
        norm(nc, g, "norm2_", lambda k, c: g.amp2[:, ds(k), c], lambda k, c: g.m(24 + k, c), True)
        mlp(nc, g, a)
        norm(nc, g, "final_", lambda k, c: g.v("final", k), None, False)
        output(nc, g, a)


def shape_constants():
    import numpy as np
    key, query = np.arange(P)[:, None] % 32, np.arange(32)[None, :]
    masks = [key == query]
    for level in range(MASKED):
        size = 2 ** level
        same = key // (2 * size) == query // (2 * size)
        key_right, query_right = key // size % 2 == 1, query // size % 2 == 1
        masks += [same & ~key_right & query_right, same & key_right & ~query_right]
    masks = np.stack(masks, 1).astype(np.float32)
    quarter = D_MODEL // 4
    omega = (1.0 / (np.float32(10000.0) ** (np.arange(quarter, dtype=np.float32) / np.float32(quarter)))).astype(np.float32)

    def table(n):
        angle = np.arange(n, dtype=np.float32)[:, None] * omega
        both = np.concatenate([np.sin(angle), np.cos(angle)], 1)
        return both.reshape(n, 4, P).transpose(2, 1, 0).reshape(P, 4 * n)
    pos = np.concatenate([table(LAT // GRID_W), table(GRID_W)], 1).astype(np.float32)
    return {"ident": np.eye(P, dtype=np.float32), "masks": np.ascontiguousarray(masks), "pos": np.ascontiguousarray(pos)}


def kernel(**inputs):
    import numpy as np
    import concourse.bacc as bacc
    from concourse.bass_utils import run_bass_kernel_spmd

    w = {n: np.asarray(x) for n, x in inputs.items()}

    def column_tiles(m):
        return m.reshape(KT, P, -1, P).transpose(2, 1, 0, 3).reshape(-1, P, KT * P)

    def cols(x):
        return x.reshape(-1, P).T
    starts = (16, 20, 0, 8, 4, 12, 24, 28)
    order = [start + h for h in range(HEADS) for start in starts]
    vecs = np.concatenate([cols(w[n]) for n in (
        "b_ada", "norm1_gain", "norm2_gain", "final_gain", "hg_lb_logits", "hg_norm_gain", "conv_w", "conv_b",
        "lru_ba", "lru_bx", "lru_lambda", "state_rglru")], 1)
    arrays = {
        "x_prompt": w["x_prompt"][0], "x_sample": w["x_sample"][0],
        "cond": np.stack([w["c_ctx"].reshape(KT, P), w["c"].reshape(KT, P)], 2).transpose(1, 0, 2),
        "vecs": vecs, "w_ada": column_tiles(w["w_ada"][0]), "w_in": column_tiles(w["w_in"][0])[order],
        "w_out": column_tiles(w["w_out"][0]), "w_ff1": column_tiles(w["w_ff1"][0]),
        "w_ff2": w["w_ff2"][0].reshape(FF_BLOCKS, P, D_MODEL),
        "state_hgrn": w["state_hgrn"][0, 0], "lru_wa": w["lru_wa"][0], "lru_wx": w["lru_wx"][0],
    }
    arrays.update(shape_constants())
    arrays = {"in_" + n: np.ascontiguousarray(x) for n, x in arrays.items()}
    nc = bacc.Bacc("TRN2", target_bir_lowering=False, num_devices=1)
    a = {n[3:]: nc.dram_tensor(n, x.shape, mybir.dt.from_np(x.dtype), kind="ExternalInput").ap()
         for n, x in arrays.items()}
    outs = {"y_prompt": (CTX, D_MODEL), "y_sample": (LAT, D_MODEL), "new_hgrn": (DIRS, HEADS, P, P), "new_lru": (P, 8)}
    for n, shape in outs.items():
        a[n] = nc.dram_tensor("out_" + n, shape, F32, kind="ExternalOutput").ap()
    backbone_step(nc, a)
    got = run_bass_kernel_spmd(nc, [arrays], core_ids=[0]).results[0]
    return (got["out_y_prompt"][None], got["out_y_sample"][None], got["out_new_hgrn"][None, None],
            np.ascontiguousarray(got["out_new_lru"].T).reshape(1, 1, DIRS, HEADS * P))
```

```python
import concourse.bass as bass
from concourse import mybir
from contextlib import ExitStack

F32 = mybir.dt.float32
F32R = mybir.dt.float32r
I32 = mybir.dt.int32
ALU = mybir.AluOpType
ACT = mybir.ActivationFunctionType

P = 128
D_MODEL = 1024
CTX, LAT = 256, 1024
TOKENS = CTX + LAT
GRID_W = 64
KT = D_MODEL // P
IN_BLOCKS, FF_BLOCKS, ADA_BLOCKS = 32, 32, 48
HEADS, DIRS = 4, 2
CHUNKS = TOKENS // P
CTX_CHUNKS = CTX // P
EPS = 1e-6
LRU_C = 8.0
CONV_LEFT = 2
TOK_BLOCKS = ((0, 256), (256, 512), (768, 512))
SEGS = ((0, CTX, 0), (CTX, LAT, 1))
GROUPS = ((0, 2), (2, 4), (6, 4))
T_V, T_GATE, T_Q0, T_F0, T_Q1, T_F1, T_LX, T_LG = range(8)
PER_HEAD = 8

VEC = {}
_at = 0
for _name, _n in (("b_ada", 48), ("norm1", 8), ("norm2", 8), ("lb", 16), ("hg_gain", 4),
                  ("conv_w", 16), ("conv_b", 4), ("ba", 8), ("bx", 8), ("lam", 8), ("h0", 8)):
    VEC[_name] = _at
    _at += _n
NVEC = _at
LEVELS = 7
MASKED = 5
MASKS = 1 + DIRS * MASKED
POS_COLS = 4 * (LAT // GRID_W) + 4 * GRID_W

KB = 1024
BASE = 16512
AREA = BASE + 3840


class Ctx:
    pass


def ds(at, n=1):
    return bass.ds(at, n)


def peeled(eng, n, body):
    body(0)
    with eng.Fori(1, n) as i:
        body(i)


def first(i):
    return isinstance(i, int) and i == 0


def is_last(h):
    return isinstance(h, int) and h == HEADS - 1


def wait_apart(g, eng, sem, value):
    eng.wait_ge(sem, value)
    eng.wait_ge(g.constants_ready, 1)


def exact_product(nc, out, w_hi, w_lo, x_hi, x_lo, start, stop):
    nc.tensor.matmul(out, w_lo, x_hi, start=start, stop=False)
    nc.tensor.matmul(out, w_hi, x_lo, start=False, stop=False)
    return nc.tensor.matmul(out, w_hi, x_hi, start=False, stop=stop)


FOLD_STEPS = 7


def modulation_by_fold(ops, eng, g, raw, product, acc, i, step, acc_used, done):
    tiles_before, uses_before = i
    count = tiles_before * FOLD_STEPS
    n = 0
    for c, dst in enumerate((product, raw)):
        ops.tensor_tensor(dst.rearrange("p (k n) -> p k n", k=KT), raw.rearrange("p (k n) -> p k n", k=KT),
                          g.cond_s[:, :, c:c + 1].broadcast_to([P, KT, P]), ALU.mult).then_inc(step, 1)
        n += 1
        for half in (4 * P, 2 * P):
            eng.wait_ge(step, count + n)
            ops.tensor_tensor(dst[:, 0:half], dst[:, 0:half], dst[:, half:2 * half], ALU.add).then_inc(step, 1)
            n += 1
        if c == 0 and not first(uses_before):
            eng.wait_ge(acc_used, uses_before)
        eng.wait_ge(step, count + n)
        ops.tensor_tensor(acc[:, c, :], dst[:, 0:P], dst[:, P:2 * P], ALU.add).then_inc(done if c else step, 1)
        n += 1
    assert n == FOLD_STEPS + 1


def modulation_sum(nc, g, acc, column):
    for c in range(2):
        last = nc.tensor.matmul(column(c), acc[:, c, :], g.ones[:, 0:1], start=True, stop=True)
    return last


def at(nc, name, shape, dtype, kb):
    return nc.alloc_sbuf_tensor_at(name, shape, dtype, offset=AREA + int(kb * KB))


def modulation_and_input(nc, g, a):
    ctx = ExitStack()
    with ctx:
        sem = lambda n: ctx.enter_context(nc.semaphore(n))
        cond = at(nc, "cond", [P, KT, 2], F32, 190)
        cond_s = g.cond_s
        ada_raw = at(nc, "ada_raw", [P, 4, D_MODEL], F32, 104)
        x_tok = at(nc, "x_tok", [P, 2, D_MODEL], F32, 164)
        sq = at(nc, "x_sq", [P, 2, KT, P], F32, 172)
        pos = at(nc, "pos", [P, POS_COLS], F32, 180)
        sq_sum = at(nc, "x_sq_sum", [P, 2, P], F32, 182)
        product = at(nc, "fold_product", [P, 2, D_MODEL], F32, 191)
        acc = at(nc, "fold_acc", [P, 2, 2, P], F32, 187)
        consts_in, pos_in, cond_in, cond_ready = sem("consts_in"), sem("pos_in"), sem("cond_in"), sem("cond_ready")
        ada_in = [sem(f"ada_in{j}") for j in range(4)]
        ada_used = [sem(f"ada_used{j}") for j in range(4)]
        fold_step, acc_used = [sem(f"fold_step{j}") for j in range(2)], [sem(f"acc_used{j}") for j in range(2)]
        x_in = [sem(f"x_in{s}") for s in range(2)]
        x_used = [sem(f"x_used{s}") for s in range(2)]
        x_moved = [sem(f"x_moved{s}") for s in range(2)]
        squared = [sem(f"squared{s}") for s in range(2)]
        added_up = [sem(f"added_up{s}") for s in range(2)]
        summed = [sem(f"summed{s}") for s in range(2)]
        mod_ready, setup = sem("mod_ready"), sem("setup")
        n_lat = LAT // (2 * P)
        pos_r = pos[:, 0:4 * 16].rearrange("p (f r) -> p f r", f=4)
        pos_c = pos[:, 64:64 + 4 * 64].rearrange("p (f c) -> p f c", f=4)
        x = g.x_first
        block = ctx.enter_context(nc.Block())

        @block.sync
        def _(sp):
            def load_x(i):
                for s in range(2):
                    sp.wait_ge(x_used[s], i + 1)
                    sp.dma_start(x_tok[:, s, :], a["x_sample"][ds((i * 2 + s) * P, P), :]).then_inc(x_in[s], 16)

            def load_ada(i):
                for j in range(4):
                    if not first(i):
                        sp.wait_ge(ada_used[j], i)
                    sp.dma_start(ada_raw[:, j, :], a["w_ada"][ds(i * 4 + j), :, :].rearrange("a p n -> p (a n)")
                                 ).then_inc(ada_in[j], 16)
            sp.dma_start(g.ident[:, :], a["ident"]).then_inc(consts_in, 16)
            sp.dma_start(x_tok[:, 0, :], a["x_prompt"][0:P, :]).then_inc(x_in[0], 16)
            sp.dma_start(x_tok[:, 1, :], a["x_prompt"][P:2 * P, :]).then_inc(x_in[1], 16)
            load_ada(0)
            load_x(0)
            with sp.Fori(1, n_lat) as i:
                load_x(i)
                load_ada(i)
            for s in range(2):
                sp.dma_start(g.in_ring.raw[:, s, :], a["w_in"][s, :, :]).then_inc(g.in_ring.raw_in[s], 16)

        @block.gpsimd
        def _(pool):
            pool.wait_ge(cond_ready, 1)

            def fold(i):
                pool.wait_ge(ada_in[2], i * 16 + 16)
                modulation_by_fold(nc.gpsimd, pool, g, ada_raw[:, 2, :], product[:, 0, :], acc[:, 0, :, :], (i, i),
                                   fold_step[0], acc_used[0], ada_used[2])
            peeled(pool, n_lat, fold)

        @block.scalar
        def _(act):
            act.dma_start(cond[:, :, :], a["cond"]).then_inc(cond_in, 16)
            act.dma_start(pos[:, :], a["pos"]).then_inc(pos_in, 16)
            act.dma_start(g.vecs[:, :], a["vecs"]).then_inc(pos_in, 16)
            act.wait_ge(cond_in, 16)
            nc.scalar.activation(cond_s[:, :, :], cond[:, :, :], ACT.Silu).then_inc(cond_ready, 1)
            for s in range(2):
                act.wait_ge(x_moved[s], 2)
                nc.scalar.activation(sq[:, s, :, :], x[:, :, s * P:(s + 1) * P], ACT.Square).then_inc(squared[s], 1)
            with act.Fori(0, n_lat) as i:
                for s in range(2):
                    act.wait_ge(added_up[s], i + 1)
                    wait_apart(g, act, x_moved[s], i * 2 + 4)
                    nc.scalar.activation(sq[:, s, :, :], x[:, :, ds(CTX + (i * 2 + s) * P, P)], ACT.Square
                                         ).then_inc(squared[s], 1)
            for s in range(2):
                split_weights(nc, act, None, 0, s, g.in_ring)

        @block.tensor
        def _(pe):
            pe.wait_ge(consts_in, 16)

            def turn(i):
                for s in range(2):
                    pe.wait_ge(x_in[s], i * 16 + 16)
                    if not first(i):
                        pe.wait_ge(x_moved[s], i * 2)
                    for f in range(KT):
                        last = nc.tensor.transpose(g.bank[2 * s + f // 4][:, (f % 4) * P:(f % 4 + 1) * P],
                                                   x_tok[:, s, f * P:(f + 1) * P], g.ident[:, :])
                    last.then_inc(x_used[s], 1)

            def sums(i):
                pe.wait_ge(g.constants_ready, 1)
                for s in range(2):
                    pe.wait_ge(added_up[s], i + 1)
                    nc.tensor.matmul(g.bank[5][:, ds(i * 2 + s)], sq_sum[:, s, :], g.ones[:, 0:1],
                                     start=True, stop=True).then_inc(summed[s], 1)

            def modulation(i):
                for j in range(2):
                    pe.wait_ge(ada_in[j], i * 16 + 16)
                    for k in range(KT):
                        last = nc.tensor.matmul(g.bank[4][:, ds((i * 4 + j) * 2, 2)], ada_raw[:, j, k * P:(k + 1) * P],
                                                cond_s[:, k, :], start=(k == 0), stop=(k == KT - 1))
                    last.then_inc(ada_used[j], 1)

            def folded(i):
                for j in range(2):
                    pe.wait_ge(ada_used[2 + j], i + 1)
                    modulation_sum(nc, g, acc[:, j, :, :], lambda c: g.bank[4][:, ds((i * 4 + 2 + j) * 2 + c)]
                                   ).then_inc(acc_used[j], 1)
            turn(0)
            sums(0)
            pe.wait_ge(cond_ready, 1)
            turn(1)
            modulation(0)
            sums(1)
            with pe.Fori(1, n_lat) as i:
                turn(i + 1)
                folded(i - 1)
                modulation(i)
                sums(i + 1)
            folded(n_lat - 1)

        @block.vector
        def _(dve):
            nc.vector.memset(g.ones[:, :], 1.0).then_inc(g.constants_ready, 1)
            nc.vector.memset(g.eps[:, :], EPS).then_inc(setup, 1)
            for s in range(CTX // P):
                dve.wait_ge(x_used[s], 1)
                for half in range(2):
                    nc.vector.tensor_copy(x[:, 4 * half:4 * half + 4, s * P:(s + 1) * P],
                                          g.bank[2 * s + half][:, :].rearrange("p (f t) -> p f t", f=4)
                                          ).then_inc(x_moved[s], 1)
            def add_up(i):
                for s in range(2):
                    dve.wait_ge(squared[s], i + 1)
                    if not first(i):
                        dve.wait_ge(summed[s], i)
                    nc.vector.tensor_reduce(sq_sum[:, s, :], sq[:, s, :, :].rearrange("p k t -> p t k"),
                                            axis=mybir.AxisListType.X, op=ALU.add).then_inc(added_up[s], 1)
            add_up(0)
            dve.wait_ge(pos_in, 32)
            dve.wait_ge(cond_ready, 1)

            def latents(i):
                for s in range(2):
                    dve.wait_ge(x_used[s], i + 2)
                    for r in range(2):
                        nc.vector.tensor_tensor(
                            x[:, 0:4, ds(CTX + (i * 2 + s) * P + r * GRID_W, GRID_W)],
                            g.bank[2 * s][:, :].rearrange("p (f t) -> p f t", f=4)[:, :, r * GRID_W:(r + 1) * GRID_W],
                            pos_r[:, :, ds(i * 4 + s * 2 + r)].broadcast_to([P, 4, GRID_W]), ALU.add
                        ).then_inc(x_moved[s] if r else setup, 1)
                    nc.vector.tensor_tensor(
                        x[:, 4:8, ds(CTX + (i * 2 + s) * P, P)].rearrange("p f (r c) -> p f r c", r=2),
                        g.bank[2 * s + 1][:, :].rearrange("p (f r c) -> p f r c", f=4, r=2),
                        pos_c[:, :, :].unsqueeze(2).broadcast_to([P, 4, 2, GRID_W]), ALU.add
                    ).then_inc(x_moved[s], 1)
                add_up(i + 1)
                dve.wait_ge(ada_in[3], i * 16 + 16)
                modulation_by_fold(nc.vector, dve, g, ada_raw[:, 3, :], product[:, 1, :], acc[:, 1, :, :], (i, i),
                                   fold_step[1], acc_used[1], ada_used[3])
            peeled(dve, n_lat, latents)
            for j in range(2):
                dve.wait_ge(ada_used[j], n_lat)
                dve.wait_ge(acc_used[j], n_lat)
            nc.vector.tensor_tensor(g.mod[:, 0:16, :], g.bank[4][:, 0:32].rearrange("p (j c) -> p j c", c=2),
                                    g.v("b_ada", 0, 16).unsqueeze(2).broadcast_to([P, 16, 2]), ALU.add
                                    ).then_inc(mod_ready, 1)
            dve.wait_ge(mod_ready, 1)
            nc.vector.scalar_tensor_tensor(g.amp1[:, :, :], g.mod[:, 8:16, :], 1.0,
                                           g.v("norm1", 0, 8).unsqueeze(2).broadcast_to([P, 8, 2]), ALU.add, ALU.mult
                                           ).then_inc(mod_ready, 1)
            for s in range(2):
                split_weights(nc, None, dve, 0, s, g.in_ring)
            dve.wait_ge(mod_ready, 2)


class Norm:
    PAIRS = KT // 2

    def __init__(self, nc, g, sem, name, x, gain_amp, shift, weights, source=None):
        self.nc, self.g, self.x, self.gain_amp, self.shift, self.weights, self.source = (
            nc, g, x, gain_amp, shift, weights, source)
        self.tmp = at(nc, name + "tmp", [P, 2, TOKENS], F32, 174)
        self.rstd_all = at(nc, name + "rstd_all", [P, TOKENS], F32, 184)
        self.root = at(nc, name + "root", [P, CHUNKS], F32, 190)
        self.rstd = at(nc, name + "rstd", [P, CHUNKS], F32, 190.125)
        self.rooted, self.rstd_ready, self.spread, self.rstd_all_ready = (
            sem(name + "rooted"), sem(name + "rstd_ready"), sem(name + "spread"), sem(name + "rstd_all_ready"))
        self.scaled = [sem(f"{name}scaled{s}") for s in range(2)]
        self.hi_done = [sem(f"{name}hi_done{s}") for s in range(2)]
        self.lo_done = [sem(f"{name}lo_done{s}") for s in range(2)]

    def wait_tile(self, eng, k):
        eng.wait_ge(self.lo_done[k % 2], len(SEGS) * (k // 2 + 1))

    @staticmethod
    def part(t, k, t0, n):
        return t[:, ds(k), t0:t0 + n].rearrange("p a t -> p (a t)")

    def sync(self, sp):
        for s in range(2):
            sp.dma_start(self.weights.raw[:, s, :], self.source[s, :, :]).then_inc(self.weights.raw_in[s], 16)

    def scalar(self, act):
        nc, g = self.nc, self.g
        nc.scalar.activation(self.root[:, :], g.bank[5][:, 0:CHUNKS], ACT.Sqrt, bias=g.eps[:, 0:1],
                             scale=1.0 / D_MODEL).then_inc(self.rooted, 1)
        if self.source is not None:
            for s in range(2):
                split_weights(nc, act, None, 0, s, self.weights)
        for b, (t0, n) in enumerate(TOK_BLOCKS):
            act.wait_ge(self.spread, b + 1)
            nc.scalar.activation(self.rstd_all[:, t0:t0 + n], g.bank[b][:, 0:n], ACT.Copy
                                 ).then_inc(self.rstd_all_ready, 1)
        with act.Fori(0, self.PAIRS) as i:
            for s in range(2):
                wait_apart(g, act, self.scaled[s], (i + 1) * len(SEGS))
                for t0, n, c in SEGS:
                    nc.scalar.activation(self.part(g.h_hi, i * 2 + s, t0, n), self.tmp[:, s, t0:t0 + n], ACT.Identity,
                                         bias=self.shift(i * 2 + s, c)).then_inc(self.hi_done[s], 1)

    def tensor(self, pe):
        nc, g = self.nc, self.g
        pe.wait_ge(self.rstd_ready, 1)
        for b, (c0, kc) in enumerate(GROUPS):
            for c in range(kc):
                last = nc.tensor.matmul(g.bank[b][:, c * P:(c + 1) * P],
                                        self.rstd[:, c0 + c:c0 + c + 1].broadcast_to([P, P]), g.ident[:, :],
                                        start=True, stop=True)
            last.then_inc(self.spread, 1)

    def vector(self, dve):
        nc, g = self.nc, self.g
        dve.wait_ge(self.rooted, 1)
        nc.vector.reciprocal(self.rstd[:, :], self.root[:, :]).then_inc(self.rstd_ready, 1)
        if self.source is not None:
            for s in range(2):
                split_weights(nc, None, dve, 0, s, self.weights)
        dve.wait_ge(self.rstd_all_ready, len(TOK_BLOCKS))

        def scale(i):
            for s in range(2):
                if not first(i):
                    dve.wait_ge(self.lo_done[s], i * len(SEGS))
                for t0, n, c in SEGS:
                    nc.vector.scalar_tensor_tensor(self.tmp[:, s, t0:t0 + n], self.part(self.x, i * 2 + s, t0, n),
                                                   self.gain_amp(i * 2 + s, c), self.rstd_all[:, t0:t0 + n],
                                                   ALU.mult, ALU.mult).then_inc(self.scaled[s], 1)

        def low(i):
            for s in range(2):
                dve.wait_ge(self.hi_done[s], (i + 1) * len(SEGS))
                for t0, n, c in SEGS:
                    nc.vector.scalar_tensor_tensor(
                        self.part(g.h_lo, i * 2 + s, t0, n), self.tmp[:, s, t0:t0 + n], self.shift(i * 2 + s, c),
                        self.part(g.h_hi, i * 2 + s, t0, n).bitcast(F32), ALU.add, ALU.subtract
                    ).then_inc(self.lo_done[s], 1)
        scale(0)
        with dve.Fori(1, self.PAIRS) as i:
            low(i - 1)
            scale(i)
        low(self.PAIRS - 1)

    def first_products(self, pe, banks, signal):
        nc, g, w = self.nc, self.g, self.weights
        for s in range(2):
            pe.wait_ge(w.lo_ready[s], 1)
        for k in range(KT):
            self.wait_tile(pe, k)
            for s in range(2):
                for b, (t0, n) in enumerate(TOK_BLOCKS):
                    last = exact_product(nc, g.bank[banks[3 * s + b]][:, 0:n], w.hi[:, s, k * P:(k + 1) * P],
                                         w.lo[:, s, k * P:(k + 1) * P], g.h_hi[:, k, t0:t0 + n],
                                         g.h_lo[:, k, t0:t0 + n], k == 0, k == KT - 1)
                    if k == KT - 1:
                        last.then_inc(signal(s, b), 1)


def split_weights(nc, act, dve, i, s, ring):
    if act is not None:
        act.wait_ge(ring.raw_in[s], i * 16 + 16)
        if not first(i):
            act.wait_ge(ring.used[s], i)
        nc.scalar.activation(ring.hi[:, s, :], ring.raw[:, s, :], ACT.Copy).then_inc(ring.hi_ready[s], 1)
    if dve is not None:
        dve.wait_ge(ring.hi_ready[s], i + 1)
        nc.vector.tensor_tensor(ring.lo[:, s, :], ring.raw[:, s, :], ring.hi[:, s, :].bitcast(F32),
                                ALU.subtract).then_inc(ring.lo_ready[s], 1)


class Ring:

    def __init__(self, nc, name, kb, sem=None, raw_slots=2):
        if sem is not None:
            two = lambda n: [sem(f"{name}{n}{s}") for s in range(2)]
            self.raw_in, self.hi_ready, self.lo_ready, self.used = (
                two(n) for n in ("raw_in", "hi_ready", "lo_ready", "used"))
        self.raw = at(nc, name + "raw", [P, raw_slots, D_MODEL], F32, kb)
        kb += 4 * raw_slots
        self.hi = at(nc, name + "hi", [P, 2, D_MODEL], F32R, kb)
        self.lo = at(nc, name + "lo", [P, 2, D_MODEL], F32R, kb + 8)


SLOTS = 3 * PER_HEAD
LEAD = 4
(S_SELF, S_LEVELS, S_HALF32, S_HALF64, S_KEYS, S_ADD, S_ADD2, S_OUT, S_OUT2, S_SUM, S_SPREAD) = (
    0, 1, 6, 7, 8, 9, 10, 11, 12, 13, 14)
S_GATES = 15
EARLY, LATE = (0, 1, 2, 4, 5, 6), (3, 7)
SPLIT_AT = {4: (0,), 5: (1, 2), 6: (3, 4), 7: (5,)}
S_EARLY = 8
OUT_UNITS = 3 * KT
S_HEAD_SPLIT = S_GATES + 1
S_LATE_WEIGHTS = S_GATES + 3
FIRST_BANKS = (0, 1, 3, 4, 5, 6)
MIX_BANKS = (3, 4, 5, 6, 7)
STATE_ORDER = ((0, 0), (1, 0), (0, 1), (1, 2), (0, 2), (1, 1))


class Banks:

    def __init__(self, sem):
        uses = [("vt", n) for n in range(3)] + [("diag",)]
        uses += [("level", l, d) for l in range(MASKED) for d in range(DIRS)]
        uses += [("half32",), ("half64", 0), ("half64", 1)]
        uses += [("kt", d, n) for d, n in STATE_ORDER] + [("ds", d, n) for d, n in STATE_ORDER]
        uses += [("out", n) for n in range(3)] + [("sum",)] + [("spread", n) for n in range(3)]
        uses += [("lru", d, ax, b) for d in range(DIRS) for ax in range(2) for b in range(3)]
        self.where, self.count = {}, dict.fromkeys(MIX_BANKS, 0)
        for i, name in enumerate(uses):
            b = MIX_BANKS[i % len(MIX_BANKS)]
            self.where[name] = (b, self.count[b])
            self.count[b] += 1
        self.full = {b: sem(f"bank_full{b}") for b in MIX_BANKS}
        self.free = {b: sem(f"bank_free{b}") for b in MIX_BANKS}

    def bank(self, name):
        return self.where[name][0]

    def wait_free(self, eng, h, name):
        b, n = self.where[name]
        eng.wait_ge(self.free[b], h * self.count[b] + n + 1)

    def wait_full(self, eng, h, name):
        b, n = self.where[name]
        eng.wait_ge(self.full[b], h * self.count[b] + n + 1)

    def wait_read(self, eng, h, name):
        b, n = self.where[name]
        eng.wait_ge(self.free[b], h * self.count[b] + n + 2)

    def filled(self, ins, name):
        ins.then_inc(self.full[self.bank(name)], 1)

    def read(self, ins, name):
        ins.then_inc(self.free[self.bank(name)], 1)


def state_steps(d, n):
    c0, k = GROUPS[n]
    steps = []
    for c in (range(c0, c0 + k) if d == 0 else reversed(range(c0, c0 + k))):
        if c == (1, 0)[d]:
            steps.append((c, None))
        elif c != (CHUNKS - 1, CTX_CHUNKS)[d]:
            steps.append((c, c + 1 - 2 * d))
    return steps


def unit_bank(h, u):
    return FIRST_BANKS[u] if first(h) and u < 6 else u % 2


def early_units(step):
    n = SLOTS - S_EARLY
    return range(OUT_UNITS * (step - S_EARLY) // n, OUT_UNITS * (step - S_EARLY + 1) // n) if step >= S_EARLY else ()


STATE_STEPS = sum(len(state_steps(d, n)) - 1 for d, n in STATE_ORDER)
CONV_N = 7
SERIES = 8
SMALL_STEPS = 4 + 2 + 5 + (SERIES - 1) + 4


def small_constants(nc, dve, g, small, done, from_act):
    count = [0]

    def link(ins):
        count[0] += 1
        ins.then_inc(done, 1)
        dve.wait_ge(done, count[0])
    t = lambda i: small[:, i, :]
    vec = nc.vector
    lam = g.vecs[:, VEC["lam"]:VEC["lam"] + 8]
    link(vec.tensor_tensor(t(5), g.vecs[:, VEC["lb"]:VEC["lb"] + 8], g.vecs[:, VEC["lb"] + 8:VEC["lb"] + 16],
                           ALU.subtract))
    link(vec.tensor_scalar(t(8), lam, -1.0, None, ALU.mult))
    link(vec.tensor_tensor(t(6), lam, t(8), ALU.max))
    link(vec.tensor_scalar(t(8), t(8), 0.0, None, ALU.max))
    dve.wait_ge(from_act, 1)
    link(vec.tensor_scalar(t(1), t(0), -1.0, 1.0, ALU.mult, ALU.add))
    link(vec.tensor_scalar(t(2), t(0), 1.0, -1.0, ALU.mult, ALU.add))
    dve.wait_ge(from_act, 2)
    link(vec.tensor_scalar(t(9), t(7), 2.0, None, ALU.add))
    link(vec.reciprocal(t(10), t(9)))
    link(vec.tensor_tensor(t(11), t(7), t(10), ALU.mult))
    link(vec.tensor_tensor(t(12), t(11), t(11), ALU.mult))
    link(vec.tensor_scalar(t(13), t(12), 1.0 / (2 * SERIES + 1), None, ALU.mult))
    for n in range(SERIES - 1, 0, -1):
        link(vec.scalar_tensor_tensor(t(13), t(13), 1.0 / (2 * n + 1), t(12), ALU.add, ALU.mult))
    link(vec.scalar_tensor_tensor(t(13), t(13), 1.0, t(11), ALU.add, ALU.mult))
    link(vec.scalar_tensor_tensor(t(13), t(13), 2.0, t(8), ALU.mult, ALU.add))
    link(vec.tensor_scalar(t(3), t(13), LRU_C, None, ALU.mult))
    link(vec.tensor_scalar(t(4), t(13), -LRU_C, None, ALU.mult))
    assert count[0] == SMALL_STEPS


def projections_and_mixers(nc, g, a):
    ctx = ExitStack()
    with ctx:
        ctx.enter_context(nc.cleanup_on_exit())
        sem = lambda n: nc.alloc_semaphore("mx_" + n)
        two = lambda n: [sem(f"{n}{s}") for s in range(2)]
        buf = lambda n, shape, kb, dt=F32: at(nc, "mx_" + n, shape, dt, kb)
        row = [P, TOKENS]
        norm = Norm(nc, g, sem, "norm1_", g.x_first, lambda k, c: g.amp1[:, ds(k), c], lambda k, c: g.m(k, c),
                    g.in_ring)
        ring, spilled = g.in_ring, sem("spilled")
        raw_in, lo_ready, used = ring.raw_in, ring.lo_ready, ring.used
        stage = buf("stage", [P, 2, TOKENS], 104)
        ada_raw, product = buf("ada_raw", [P, D_MODEL], 114), buf("fold_product", [P, D_MODEL], 118)
        at_row = lambda i: 122 + 5 * i
        q = [buf("q0", row, at_row(0)), buf("q1", row, at_row(2))]
        f = [buf("f0", row, at_row(1)), buf("f1", row, at_row(3))]
        k = [buf("k0", row, at_row(4)), buf("k1", row, at_row(5))]
        v = buf("v", row, at_row(6))
        scores = buf("scores", [P, CHUNKS, P], at_row(6))
        gate = buf("gate", row, at_row(7))
        v_tok = buf("v_tok", [P, CHUNKS, P], at_row(8))
        k_tok = [buf("k_tok0", [P, CHUNKS, P], at_row(9)), buf("k_tok1", [P, CHUNKS, P], at_row(10))]
        state = [buf("state0", [P, CHUNKS, P], at_row(11)), buf("state1", [P, CHUNKS, P], at_row(12))]
        lx, lg = buf("lx", row, at_row(13)), buf("lg", row, at_row(14))
        o_sq, o_gain = buf("o_sq", row, at_row(1)), buf("o_gain", row, at_row(3))
        xc = buf("xc", row, at_row(4))
        r = [buf("r0", row, at_row(5)), buf("r1", row, at_row(9))]
        ig = [buf("ig0", row, at_row(8)), buf("ig1", row, at_row(10))]
        dec, sq = buf("dec", row, at_row(11)), buf("sq", row, at_row(12))
        tiles = {T_LX: lx, T_LG: lg, T_V: v, T_GATE: gate, T_Q0: q[0], T_F0: f[0], T_Q1: q[1], T_F1: f[1]}
        diag = buf("diag", [P, CHUNKS, 32], 197)
        head_vecs = buf("head_vecs", [P, 9], 198.25)
        new_lru = buf("new_lru", [P, 8], 198.3125)
        root, rstd = buf("root", [P, CHUNKS], 198.375), buf("rstd", [P, CHUNKS], 198.4375)
        last_state = [buf("last0", [P, P], 198.5), buf("last1", [P, P], 199)]
        lru_w = buf("lru_w", [P, 4, P], 199.5)
        masks = buf("masks", [P, MASKS, 32], 201.5)
        small = buf("small", [P, 16, 8], 203)
        early_hi, early_lo = buf("early_hi", [P, 6, TOKENS], 0, F32R), buf("early_lo", [P, 6, TOKENS], 30, F32R)
        early_raw = buf("early_raw", [P, 6, TOKENS], 30)
        out_raw = buf("out_raw", [P, D_MODEL], 60)
        out_hi, out_lo = buf("out_hi", [P, 2, D_MODEL], 64, F32R), buf("out_lo", [P, 2, D_MODEL], 72, F32R)
        late_raw, late_w_lo = buf("late_raw", [P, KT, 2, P], at_row(0)), buf("late_w_lo", [P, KT, 2, P], at_row(0), F32R)
        late_w_hi = buf("late_w_hi", [P, KT, 2, P], at_row(0) + 8, F32R)
        late_hi = [buf("late_hi0", row, at_row(6), F32R), buf("late_hi1", row, at_row(4), F32R)]
        x_sq, sq_sum = buf("x_sq", [P, 2, TOKENS], at_row(8)), buf("sq_sum", row, at_row(10))
        late_lo = [buf("late_lo0", row, at_row(7), F32R), buf("late_lo1", row, at_row(14), F32R)]
        lb, one_lb, neg_lb = (small[:, i, :] for i in range(3))

        ada_in, fold_step, acc_ready, acc_used = sem("ada_in"), sem("fold_step"), sem("acc_ready"), sem("acc_used")
        stored = two("stored")
        unit_full, staged, mod_done = two("unit_full"), two("staged"), sem("mod_done")
        bk = Banks(sem)
        tile_in = {t: sem(f"tile_in{t}") for t in tiles}
        const_in, states_in, lru_w_in = sem("const_in"), sem("states_in"), sem("lru_w_in")
        zeroed, states_zero, small_act, small_dve = sem("zeroed"), sem("states_zero"), sem("small_act"), sem("small_dve")
        sig_ready, q_ready, gate_ready = sem("sig_ready"), sem("q_ready"), sem("gate_ready")
        kf_ready, qk_ready, tot_ready, placed = sem("kf_ready"), sem("qk_ready"), sem("tot_ready"), sem("placed")
        state_step, squared, rstd_ready, vecs_ready = (
            sem("state_step"), sem("squared"), sem("rstd_ready"), sem("vecs_ready"))
        head_done, head_stored, tile_done, tile_stored, last_stored, lru_stored = (
            sem("head_done"), sem("head_stored"), sem("tile_done"), sem("tile_stored"), sem("last_stored"),
            sem("lru_stored"))
        conv, lru_exp, ix_ready, gap_ready, gap_root, u_ready, scanned, lg_ready = (
            sem("conv"), sem("lru_exp"), sem("ix_ready"), sem("gap_ready"), sem("gap_root"), sem("u_ready"),
            sem("scanned"), sem("lg_ready"))
        early_in = [sem(f"early_in{k}") for k in range(6)]
        x_in = [sem("x_in_first"), sem("x_in_rest")]
        early_hi_ready, early_lo_ready, out_in, out_hi_ready, out_lo_ready = (
            sem("early_hi_ready"), sem("early_lo_ready"), sem("out_in"), sem("out_hi_ready"), sem("out_lo_ready"))
        early_full, early_added, late_full, late_added = (
            sem("early_full"), sem("early_added"), sem("late_full"), sem("late_added"))
        late_in, late_w_hi_ready, late_w_lo_ready, late_hi_ready, late_lo_ready = (
            sem("late_in"), sem("late_w_hi_ready"), sem("late_w_lo_ready"), sem("late_hi_ready"), sem("late_lo_ready"))
        x_squared, x_sq_added, x_summed = sem("x_squared"), sem("x_sq_added"), sem("x_summed")
        QK_N = 2 + LEVELS * DIRS * 2

        def qk_count(level, d):
            return 1 + d if level == 0 else 2 + (2 * (level - 1) + d) * 2 + 2

        def turns(eng, project, mix, out):
            def turn(h, last):
                for u in range(SLOTS):
                    project(h, u, last)
                    if u < SLOTS - LEAD:
                        if not first(h):
                            mix(h - 1, u + LEAD)
                    else:
                        mix(h, u + LEAD - SLOTS)
            turn(0, False)
            with eng.Fori(1, HEADS - 1) as h:
                turn(h, False)
            turn(HEADS - 1, True)
            for step in range(LEAD, SLOTS):
                out(step)
                mix(HEADS - 1, step)

        block = ctx.enter_context(nc.Block())

        @block.sync
        def _(sp):
            def load_tile(h, t):
                sp.wait_ge(stored[t % 2], (h * (PER_HEAD // 2) + t // 2) * 16 + 16)
                sp.dma_start(tiles[t][:, :], g.proj[ds(h * PER_HEAD + t), :, :].rearrange("a p n -> p (a n)")
                             ).then_inc(tile_in[t], 16)

            def load_weights(h, j):
                s, i = j % 2, h * (PER_HEAD // 2) + j // 2
                if not first(i):
                    sp.wait_ge(lo_ready[s], i)
                    sp.dma_start(ring.raw[:, s, :], a["w_in"][ds(i * 2 + s), :, :].rearrange("a p n -> p (a n)")
                                 ).then_inc(raw_in[s], 16)

            def load_modulation(n):
                if not first(n):
                    sp.wait_ge(acc_ready, n)
                sp.dma_start(ada_raw[:, :], a["w_ada"][ds(16 + n), :, :].rearrange("a p n -> p (a n)")
                             ).then_inc(ada_in, 16)

            def project(h, u, last):
                if u % 3 == 1:
                    j = u // 3
                    if j + 2 < PER_HEAD:
                        load_weights(h, j + 2)
                    elif not last:
                        load_weights(h + 1, j + 2 - PER_HEAD)
                    if not (last and j == PER_HEAD - 1):
                        load_modulation(h * PER_HEAD + j + 1)
                if u == 11:
                    if first(h):
                        sp.wait_ge(spilled, 16)
                        sp.wait_ge(zeroed, 1)
                    else:
                        bk.wait_full(sp, h - 1, ("out", 2))
                    load_tile(h, T_V)
                    load_tile(h, T_Q0)
                if u == 13:
                    load_tile(h, T_F0)
                    if not first(h):
                        sp.wait_ge(head_stored, h * 16)
                    load_tile(h, T_GATE)
                if u == 16:
                    load_tile(h, T_Q1)
                if u == 19:
                    load_tile(h, T_F1)

            def mix(h, step):
                if step == 5:
                    if not first(h):
                        sp.wait_ge(tile_stored, h * 16)
                    load_tile(h, T_LX)
                    load_tile(h, T_LG)
                    if not first(h):
                        sp.wait_ge(last_stored, h * 32)
                    sp.wait_ge(states_zero, h * 2 + 2)
                    for d, c in ((0, CTX_CHUNKS), (1, CHUNKS - 1)):
                        sp.dma_start(state[d][:, c, :], a["state_hgrn"][d, ds(h), :, :].rearrange("a p n -> p (a n)")
                                     ).then_inc(states_in, 16)
                    for ax, w in enumerate(("lru_wa", "lru_wx")):
                        for half in range(2):
                            part = slice(64 * half, 64 * half + 64)
                            sp.dma_start(lru_w[part, 2 * ax:2 * ax + 2, part],
                                         a[w][:, ds(h * 2 + half), :, :].rearrange("r a d e -> d (r a) e")
                                         ).then_inc(lru_w_in, 16)
                if step == S_OUT2:
                    for d in range(DIRS):
                        bk.wait_read(sp, h, ("ds", d, 0))
                        sp.dma_start(a["new_hgrn"][d, ds(h), :, :].rearrange("a p n -> p (a n)"), last_state[d][:, :]
                                     ).then_inc(last_stored, 16)
                if step == S_GATES and not is_last(h):
                    sp.wait_ge(head_done, h + 1)
                    sp.dma_start(g.mix_out[ds(h), :, :].rearrange("a p n -> p (a n)"), gate[:, :]
                                 ).then_inc(head_stored, 16)
                if step == SLOTS - 1 and not is_last(h):
                    sp.wait_ge(tile_done, h + 1)
                    sp.dma_start(g.mix_out[ds(h + HEADS), :, :].rearrange("a p n -> p (a n)"), lg[:, :]
                                 ).then_inc(tile_stored, 16)

            def out(step):
                if step == LEAD:
                    sp.wait_ge(used[1], IN_BLOCKS // 2)
                    sp.wait_ge(head_stored, (HEADS - 1) * 16)
                    sp.wait_ge(tile_stored, (HEADS - 1) * 16)
                    sp.dma_start(out_raw[:, :], a["w_out"][0, :, :]).then_inc(out_in, 16)
                for i in {LEAD: (0, 1, 2), LEAD + 2: (3, 4, 5)}.get(step, ()):
                    sp.dma_start(early_raw[:, i, :], g.mix_out[EARLY[i], :, :]).then_inc(early_in[i], 16)
                if step == LEAD + 2:
                    sp.wait_ge(acc_ready, IN_BLOCKS)
                    for s in range(2):
                        sp.wait_ge(stored[s], IN_BLOCKS // 2 * 16)
                    sp.dma_start(g.x[:, 0, :], g.x_scratch[:, 0:TOKENS]).then_inc(x_in[0], 16)
                    sp.dma_start(g.x[:, 1:KT, :].rearrange("p k t -> p (k t)"), g.x_scratch[:, TOKENS:KT * TOKENS]
                                 ).then_inc(x_in[1], 16)
                for u in early_units(step):
                    m, b = divmod(u, 3)
                    if b == 0 and m + 1 < KT:
                        sp.wait_ge(out_lo_ready, m + 1)
                        sp.dma_start(out_raw[:, :], a["w_out"][m + 1, :, :]).then_inc(out_in, 16)
                if step == S_HEAD_SPLIT:
                    sp.wait_ge(head_done, HEADS)
                    for j, k in enumerate(LATE):
                        sp.dma_start(late_raw[:, :, j, :], a["w_out"].rearrange("m p (k n) -> p m k n", k=KT)[:, :, k, :]
                                     ).then_inc(late_in, 16)

            load_modulation(0)
            sp.dma_start(masks[:, :, :], a["masks"]).then_inc(const_in, 16)
            sp.dma_start(g.x_scratch, g.x_first[:, :, :].rearrange("p k t -> p (k t)")).then_inc(spilled, 16)
            turns(sp, project, mix, out)
            sp.wait_ge(tile_done, HEADS)
            sp.dma_start(a["new_lru"], new_lru[:, :]).then_inc(lru_stored, 16)
            sp.wait_ge(lru_stored, 16)
            sp.wait_ge(last_stored, HEADS * 32)

        @block.gpsimd
        def _(pool):
            def fold(n):
                pool.wait_ge(ada_in, n * 16 + 16)
                modulation_by_fold(nc.gpsimd, pool, g, ada_raw[:, :], product[:, :], g.fold_acc, (n, n), fold_step,
                                   acc_used, acc_ready)
            peeled(pool, IN_BLOCKS, fold)

        @block.scalar
        def _(act):
            def to_sbuf(h, name, out, columns):
                bk.wait_full(act, h, name)
                bk.read(nc.scalar.activation(out, g.bank[bk.bank(name)][:, 0:columns], ACT.Copy), name)

            def flat(t, c0, kc):
                return t[:, c0:c0 + kc, :].rearrange("p c k -> p (c k)")

            def project(h, u, last):
                j, b = divmod(u, 3)
                s, i = j % 2, h * (PER_HEAD // 2) + j // 2
                t0, n = TOK_BLOCKS[b]
                if b == 0 and not first(i):
                    act.wait_ge(stored[s], i * 16)
                if b < 2:
                    act.wait_ge(unit_full[b], h * PER_HEAD + j + 1)
                else:
                    act.wait_ge(used[s], i + 1)
                nc.scalar.activation(stage[:, s, t0:t0 + n], g.bank[unit_bank(h, u)][:, 0:n], ACT.Copy
                                     ).then_inc(staged[s], 1)
                if b == 2:
                    act.wait_ge(staged[s], i * 3 + 3)
                    act.dma_start(g.proj[ds(h * PER_HEAD + j), :, :].rearrange("a p n -> p (a n)"), stage[:, s, :]
                                  ).then_inc(stored[s], 16)
                if b == 0 and not (last and j == PER_HEAD - 1) and not (first(h) and j == 0):
                    split_weights(nc, act, None, h * (PER_HEAD // 2) + (j + 1) // 2, 1 - s, ring)
                if u == 17:
                    act.wait_ge(tile_in[T_Q0], h * 16 + 16)
                    nc.scalar.activation(q[0][:, :], q[0][:, :], ACT.Silu).then_inc(q_ready, 1)
                    act.wait_ge(tile_in[T_GATE], h * 16 + 16)
                    nc.scalar.activation(gate[:, :], gate[:, :], ACT.Silu).then_inc(gate_ready, 1)
                if u == 18:
                    act.wait_ge(tile_in[T_Q1], h * 16 + 16)
                    nc.scalar.activation(q[1][:, :], q[1][:, :], ACT.Silu).then_inc(q_ready, 1)
                if u == 19:
                    for d in range(DIRS):
                        act.wait_ge(tile_in[(T_F0, T_F1)[d]], h * 16 + 16)
                        nc.scalar.activation(f[d][:, :], f[d][:, :], ACT.Sigmoid).then_inc(sig_ready, 1)

            def mix(h, step):
                if step == S_SELF:
                    if not first(h):
                        act.wait_ge(tile_done, h)
                    for n, (c0, kc) in enumerate(GROUPS):
                        to_sbuf(h, ("vt", n), flat(v_tok, c0, kc), kc * P)
                if step == S_HALF32:
                    bk.wait_full(act, h, ("half32",))
                    for j in range(4):
                        rows, cols = slice(32 * j, 32 * j + 32), slice(32 * (j ^ 1), 32 * (j ^ 1) + 32)
                        ins = nc.scalar.activation(
                            scores[rows, :, cols], g.bank[bk.bank(("half32",))][rows, 0:CHUNKS * 32].rearrange(
                                "p (c t) -> p c t", t=32), ACT.Copy)
                    bk.read(ins, ("half32",))
                if step == S_HALF64:
                    for part in range(2):
                        bk.wait_full(act, h, ("half64", part))
                        for j in range(2):
                            rows, cols = slice(64 * j, 64 * j + 64), slice(64 * (1 - j), 64 * (1 - j) + 64)
                            ins = nc.scalar.activation(
                                scores[rows, 5 * part:5 * part + 5, cols],
                                g.bank[bk.bank(("half64", part))][rows, 0:320].rearrange("p (c t) -> p c t", t=64),
                                ACT.Copy)
                        bk.read(ins, ("half64", part))
                    bk.wait_read(act, h, ("level", MASKED - 1, 1))
                    for j in range(4):
                        rows = slice(32 * j, 32 * j + 32)
                        ins = nc.scalar.activation(scores[rows, :, rows], diag[rows, :, :], ACT.Copy)
                    ins.then_inc(placed, 1)
                if step == S_KEYS:
                    for d, n in STATE_ORDER:
                        c0, kc = GROUPS[n]
                        to_sbuf(h, ("kt", d, n), flat(k_tok[d], c0, kc), kc * P)
                if step in (S_OUT, S_OUT2):
                    act.wait_ge(vecs_ready, h * 3 + 3)
                    for n in ((0,), (1, 2))[step - S_OUT]:
                        t0, tn = TOK_BLOCKS[n]
                        bk.wait_full(act, h, ("out", n))
                        out = g.bank[bk.bank(("out", n))][:, 0:tn]
                        nc.scalar.activation(o_sq[:, t0:t0 + tn], out, ACT.Square).then_inc(squared, 1)
                        bk.read(nc.scalar.activation(o_gain[:, t0:t0 + tn], out, ACT.Copy, scale=head_vecs[:, 4:5]),
                                ("out", n))
                if step == S_SUM:
                    bk.wait_full(act, h, ("sum",))
                    bk.read(nc.scalar.activation(root[:, :], g.bank[bk.bank(("sum",))][:, 0:CHUNKS], ACT.Sqrt,
                                                 bias=g.eps[:, 0:1], scale=1.0 / P), ("sum",))
                if S_GATES <= step < S_GATES + 4:
                    d, ax = divmod(step - S_GATES, 2)
                    for n, (t0, tn) in enumerate(TOK_BLOCKS):
                        name = ("lru", d, ax, n)
                        bk.wait_full(act, h, name)
                        bk.read(nc.scalar.activation((r, ig)[ax][d][:, t0:t0 + tn], g.bank[bk.bank(name)][:, 0:tn],
                                                     ACT.Sigmoid, bias=head_vecs[:, 2 * ax + d:2 * ax + d + 1]), name)
                if step in (S_GATES + 1, S_GATES + 4):
                    d = (step - S_GATES) // 4
                    if d:
                        act.wait_ge(scanned, h * 7 + 2)
                    for n in range(3):
                        bk.wait_read(act, h, ("lru", d, 0, n))
                    nc.scalar.activation(dec[:, :], r[d][:, :], ACT.Exp, scale=head_vecs[:, 7 + d:8 + d]
                                         ).then_inc(lru_exp, 1)
                    act.wait_ge(lru_exp, h * 6 + 3 * d + 1)
                    nc.scalar.activation(r[d][:, :], r[d][:, :], ACT.Tanh, scale=head_vecs[:, 5 + d:6 + d]
                                         ).then_inc(lru_exp, 1)
                    nc.scalar.activation(sq[:, :], dec[:, :], ACT.Square).then_inc(lru_exp, 1)
                if step in (S_GATES + 2, S_GATES + 5):
                    d = (step - S_GATES - 2) // 3
                    act.wait_ge(gap_ready, h * 2 + d + 1)
                    nc.scalar.activation(sq[:, :], sq[:, :], ACT.Sqrt).then_inc(gap_root, 1)
                if step == S_GATES + 6:
                    act.wait_ge(tile_in[T_LG], h * 16 + 16)
                    nc.scalar.activation(lg[:, :], lg[:, :], ACT.Gelu_apprx_tanh).then_inc(lg_ready, 1)

            def out_weights(m):
                act.wait_ge(out_in, m * 16 + 16)
                if m >= 2:
                    act.wait_ge(early_full, 3 * (m - 1))
                nc.scalar.activation(out_hi[:, m % 2, :], out_raw[:, :], ACT.Copy).then_inc(out_hi_ready, 1)

            def out(step):
                for i in SPLIT_AT.get(step - 1, ()):
                    act.wait_ge(early_in[i], 16)
                    nc.scalar.activation(early_hi[:, i, :], early_raw[:, i, :], ACT.Copy).then_inc(early_hi_ready, 1)
                if step == S_EARLY:
                    out_weights(0)
                for u in early_units(step):
                    m, b = divmod(u, 3)
                    if b == 0 and m + 1 < KT:
                        out_weights(m + 1)
                if step == S_HEAD_SPLIT:
                    act.wait_ge(head_done, HEADS)
                    nc.scalar.activation(late_hi[0][:, :], gate[:, :], ACT.Copy).then_inc(late_hi_ready, 1)
                if step == S_LATE_WEIGHTS:
                    act.wait_ge(late_in, 32)
                    nc.scalar.activation(late_w_hi[:, :, :, :], late_raw[:, :, :, :], ACT.Copy
                                         ).then_inc(late_w_hi_ready, 1)

            norm.scalar(act)
            act.wait_ge(small_dve, 3)
            nc.scalar.activation(lb, small[:, 5, :], ACT.Sigmoid).then_inc(small_act, 1)
            nc.scalar.activation(small[:, 7, :], small[:, 6, :], ACT.Exp, scale=-1.0).then_inc(small_act, 1)
            act.wait_ge(small_dve, SMALL_STEPS)
            turns(act, project, mix, out)
            act.wait_ge(tile_done, HEADS)
            nc.scalar.activation(late_hi[1][:, :], lg[:, :], ACT.Copy).then_inc(late_hi_ready, 1)
            for m in range(KT):
                act.wait_ge(late_added, 3 * m + 3)
                if m > 2:
                    act.wait_ge(x_sq_added, m - 2)
                nc.scalar.activation(x_sq[:, m % 2, :] if m else sq_sum[:, :], g.x[:, m, :], ACT.Square
                                     ).then_inc(x_squared, 1)
            for s in range(2):
                act.wait_ge(stored[s], IN_BLOCKS // 2 * 16)

        @block.tensor
        def _(pe):
            def blocks(tensor, c, size, j):
                return tensor[:, c * P + size * j:c * P + size * j + size]

            def project(h, u, last):
                j, b = divmod(u, 3)
                s, i = j % 2, h * (PER_HEAD // 2) + j // 2
                t0, n = TOK_BLOCKS[b]
                if not (first(h) and u < 6):
                    if b == 0:
                        pe.wait_ge(lo_ready[s], i + 1)
                    if b == 2:
                        pe.wait_ge(staged[s], i * 3 + 1)
                    elif s == 1:
                        pe.wait_ge(staged[0], i * 3 + b + 2)
                    elif not first(i):
                        pe.wait_ge(staged[1], (i - 1) * 3 + b + 2)
                    for kt in range(KT):
                        ins = exact_product(nc, g.bank[u % 2][:, 0:n], ring.hi[:, s, kt * P:(kt + 1) * P],
                                            ring.lo[:, s, kt * P:(kt + 1) * P], g.h_hi[:, kt, t0:t0 + n],
                                            g.h_lo[:, kt, t0:t0 + n], kt == 0, kt == KT - 1)
                    ins.then_inc(used[s] if b == 2 else unit_full[b], 1)
                if b == 2 and not (first(h) and j == 0):
                    modulation(h * PER_HEAD + j)

            def modulation(n):
                pe.wait_ge(acc_ready, n + 1)
                modulation_sum(nc, g, g.fold_acc, lambda c: g.bank[2][:, ds(n * 2 + c)]).then_inc(acc_used, 1)

            def square_scores(h, name):
                d = name[2]
                for c in range(CHUNKS):
                    for j in range(4):
                        ins = nc.tensor.matmul(g.bank[bk.bank(name)][32 * j:32 * j + 32, c * 32:(c + 1) * 32],
                                               blocks(k[d], c, 32, j), blocks(q[d], c, 32, j), start=True, stop=True)
                bk.filled(ins, name)

            def transpose(h, name, src, c0, kc):
                bk.wait_free(pe, h, name)
                for c in range(kc):
                    ins = nc.tensor.transpose(g.bank[bk.bank(name)][:, c * P:(c + 1) * P],
                                              src[:, (c0 + c) * P:(c0 + c + 1) * P], g.ident[:, :])
                bk.filled(ins, name)

            def mix(h, step):
                if step == S_SELF:
                    pe.wait_ge(tile_in[T_V], h * 16 + 16)
                    for n, (c0, kc) in enumerate(GROUPS):
                        transpose(h, ("vt", n), v, c0, kc)
                    bk.wait_free(pe, h, ("diag",))
                    pe.wait_ge(q_ready, h * 2 + 2)
                    pe.wait_ge(kf_ready, h * 4 + 4)
                    for c in range(CHUNKS):
                        for j in range(4):
                            for d in range(DIRS):
                                ins = nc.tensor.matmul(
                                    g.bank[bk.bank(("diag",))][32 * j:32 * j + 32, c * 32:(c + 1) * 32],
                                    blocks(k[d], c, 32, j), blocks(q[d], c, 32, j), start=(d == 0), stop=(d == 1))
                    bk.filled(ins, ("diag",))
                if S_LEVELS <= step < S_LEVELS + MASKED:
                    level = step - S_LEVELS
                    for d in range(DIRS):
                        name = ("level", level, d)
                        bk.wait_free(pe, h, name)
                        pe.wait_ge(qk_ready, h * QK_N + qk_count(level, d))
                        square_scores(h, name)
                if step == S_HALF32:
                    bk.wait_free(pe, h, ("half32",))
                    pe.wait_ge(qk_ready, h * QK_N + qk_count(MASKED, 1))
                    for c in range(CHUNKS):
                        for j in range(4):
                            d = j % 2
                            ins = nc.tensor.matmul(g.bank[bk.bank(("half32",))][32 * j:32 * j + 32, c * 32:(c + 1) * 32],
                                                   blocks(k[d], c, 32, j), blocks(q[d], c, 32, j ^ 1),
                                                   start=True, stop=True)
                    bk.filled(ins, ("half32",))
                if step == S_HALF64:
                    pe.wait_ge(qk_ready, h * QK_N + qk_count(MASKED + 1, 1))
                    for part in range(2):
                        name = ("half64", part)
                        bk.wait_free(pe, h, name)
                        for c in range(5):
                            for d in range(DIRS):
                                ins = nc.tensor.matmul(g.bank[bk.bank(name)][64 * d:64 * d + 64, c * 64:(c + 1) * 64],
                                                       blocks(k[d], 5 * part + c, 64, d),
                                                       blocks(q[d], 5 * part + c, 64, 1 - d), start=True, stop=True)
                        bk.filled(ins, name)
                if step == S_KEYS:
                    pe.wait_ge(qk_ready, h * QK_N + QK_N)
                    for d, n in STATE_ORDER:
                        transpose(h, ("kt", d, n), k[d], *GROUPS[n])
                if step in (S_ADD, S_ADD2):
                    for d, n in (STATE_ORDER[:4], STATE_ORDER[4:])[step - S_ADD]:
                        c0, kc = GROUPS[n]
                        name = ("ds", d, n)
                        bk.wait_read(pe, h, ("kt", d, n))
                        bk.wait_free(pe, h, name)
                        for c in range(kc):
                            ins = nc.tensor.matmul(g.bank[bk.bank(name)][:, c * P:(c + 1) * P], k_tok[d][:, c0 + c, :],
                                                   v_tok[:, c0 + c, :], start=True, stop=True)
                        bk.filled(ins, name)
                if step in (S_OUT, S_OUT2):
                    pe.wait_ge(placed, h + 1)
                    pe.wait_ge(states_in, h * 32 + 32)
                    for n in ((0,), (1, 2))[step - S_OUT]:
                        c0, kc = GROUPS[n]
                        name = ("out", n)
                        bk.wait_free(pe, h, name)
                        bk.wait_read(pe, h, ("ds",) + ((1, 0), (1, 1), (0, 2))[n])
                        for c in range(kc):
                            out = g.bank[bk.bank(name)][:, c * P:(c + 1) * P]
                            at_c = slice((c0 + c) * P, (c0 + c + 1) * P)
                            nc.tensor.matmul(out, v_tok[:, c0 + c, :], scores[:, c0 + c, :], start=True, stop=False)
                            nc.tensor.matmul(out, state[0][:, c0 + c, :], q[0][:, at_c], start=False, stop=False)
                            ins = nc.tensor.matmul(out, state[1][:, c0 + c, :], q[1][:, at_c], start=False, stop=True)
                        bk.filled(ins, name)
                if step == S_SUM:
                    bk.wait_free(pe, h, ("sum",))
                    pe.wait_ge(squared, h * 3 + 3)
                    for c in range(CHUNKS):
                        ins = nc.tensor.matmul(g.bank[bk.bank(("sum",))][:, c:c + 1], o_sq[:, c * P:(c + 1) * P],
                                               g.ones[:, 0:1], start=True, stop=True)
                    bk.filled(ins, ("sum",))
                if step == S_SPREAD:
                    pe.wait_ge(rstd_ready, h + 1)
                    for n, (c0, kc) in enumerate(GROUPS):
                        bk.wait_free(pe, h, ("spread", n))
                        for c in range(kc):
                            ins = nc.tensor.matmul(g.bank[bk.bank(("spread", n))][:, c * P:(c + 1) * P],
                                                   rstd[:, c0 + c:c0 + c + 1].broadcast_to([P, P]), g.ident[:, :],
                                                   start=True, stop=True)
                        bk.filled(ins, ("spread", n))
                if S_GATES <= step < S_GATES + 4:
                    d, ax = divmod(step - S_GATES, 2)
                    pe.wait_ge(conv, h * CONV_N + CONV_N)
                    pe.wait_ge(lru_w_in, h * 64 + 64)
                    for n, (t0, tn) in enumerate(TOK_BLOCKS):
                        name = ("lru", d, ax, n)
                        bk.wait_free(pe, h, name)
                        bk.filled(nc.tensor.matmul(g.bank[bk.bank(name)][:, 0:tn], lru_w[:, 2 * ax + d, :],
                                                   xc[:, t0:t0 + tn], start=True, stop=True), name)

            def out(step):
                for u in early_units(step):
                    m, b = divmod(u, 3)
                    t0, n = TOK_BLOCKS[b]
                    if u == 0:
                        pe.wait_ge(staged[1], IN_BLOCKS // 2 * 3)
                        pe.wait_ge(early_lo_ready, 6)
                    if b == 0:
                        pe.wait_ge(out_lo_ready, m + 1)
                    if u >= 2:
                        pe.wait_ge(early_added, u - 1)
                    for i, k in enumerate(EARLY):
                        ins = exact_product(nc, g.bank[u % 2][:, 0:n], out_hi[:, m % 2, k * P:(k + 1) * P],
                                            out_lo[:, m % 2, k * P:(k + 1) * P], early_hi[:, i, t0:t0 + n],
                                            early_lo[:, i, t0:t0 + n], i == 0, i == 5)
                    ins.then_inc(early_full, 1)

            norm.tensor(pe)
            pe.wait_ge(norm.rstd_all_ready, 3)
            modulation(0)
            norm.first_products(pe, FIRST_BANKS, lambda s, b: used[s] if b == 2 else unit_full[b])
            turns(pe, project, mix, out)
            pe.wait_ge(late_w_lo_ready, 1)
            pe.wait_ge(late_lo_ready, 2)
            for u in range(OUT_UNITS):
                m, b = divmod(u, 3)
                t0, n = TOK_BLOCKS[b]
                if u >= len(MIX_BANKS):
                    pe.wait_ge(late_added, u + 1 - len(MIX_BANKS))
                for j in range(2):
                    ins = exact_product(nc, g.bank[MIX_BANKS[u % len(MIX_BANKS)]][:, 0:n], late_w_hi[:, m, j, :],
                                        late_w_lo[:, m, j, :], late_hi[j][:, t0:t0 + n], late_lo[j][:, t0:t0 + n],
                                        j == 0, j == 1)
                ins.then_inc(late_full, 1)
            pe.wait_ge(x_sq_added, KT - 1)
            pe.wait_ge(late_added, OUT_UNITS)
            for c in range(CHUNKS):
                ins = nc.tensor.matmul(g.bank[5][:, c:c + 1], sq_sum[:, c * P:(c + 1) * P], g.ones[:, 0:1],
                                       start=True, stop=True)
            ins.then_inc(x_summed, 1)

        @block.vector
        def _(dve):
            def project(h, u, last):
                j, b = divmod(u, 3)
                if b == 0 and not (last and j == PER_HEAD - 1) and not (first(h) and j == 0):
                    split_weights(nc, None, dve, h * (PER_HEAD // 2) + (j + 1) // 2, 1 - j % 2, ring)
                if u == 19:
                    if not first(h):
                        dve.wait_ge(tile_done, h)
                    for d in range(DIRS):
                        at_h = ds(h + 4 * d)
                        dve.wait_ge(sig_ready, h * 2 + d + 1)
                        nc.vector.tensor_scalar(k[d][:, :], f[d][:, :], neg_lb[:, at_h], one_lb[:, at_h],
                                                ALU.mult, ALU.add).then_inc(kf_ready, 1)
                        nc.vector.tensor_scalar(f[d][:, :], f[d][:, :], one_lb[:, at_h], lb[:, at_h],
                                                ALU.mult, ALU.add).then_inc(kf_ready, 1)

            def one_level(h, level):
                size = 2 ** level
                pairs = TOKENS // (2 * size)
                for d in range(DIRS):
                    for name in ([("level", level, d)], [("half32",)], [("half64", 0), ("half64", 1)]
                                 )[max(0, level - MASKED + 1)]:
                        bk.wait_full(dve, h, name)
                    totals = f[d][:, :].rearrange("p (n two s) -> p n two s", two=2, s=size)
                    if level:
                        dve.wait_ge(tot_ready, h * 14 + 2 * (level - 1) + d + 1)
                    for t, half in ((q[d], 1 - d), (k[d], d)):
                        part = t[:, :].rearrange("p (n two b) -> p n two b", two=2, b=size)[:, :, half, :]
                        nc.vector.tensor_tensor(part, part, totals[:, :, 1 - half, 0:1].broadcast_to([P, pairs, size]),
                                                ALU.mult).then_inc(qk_ready, 1)
                    dve.wait_ge(qk_ready, h * QK_N + qk_count(level + 1, d))
                    if level < MASKED:
                        bk.wait_read(dve, h, ("level", level, 0) if d else ("level", level - 1, 1) if level else ("diag",))
                    nc.vector.tensor_tensor(totals[:, :, 0, 0], totals[:, :, 0, 0], totals[:, :, 1, 0], ALU.mult
                                            ).then_inc(tot_ready, 1)
                    if level < MASKED:
                        name, mask = ("level", level, d), 1 + 2 * level + d
                        bk.read(nc.vector.copy_predicated(
                            diag[:, :, :], masks[:, mask:mask + 1, :].bitcast(I32).broadcast_to([P, CHUNKS, 32]),
                            g.bank[bk.bank(name)][:, 0:CHUNKS * 32].rearrange("p (c t) -> p c t", t=32)), name)

            def states(h, order):
                for d, n in order:
                    name = ("ds", d, n)
                    bk.wait_full(dve, h, name)
                    if n:
                        before = [m for e, m in STATE_ORDER if e == d]
                        bk.wait_read(dve, h, ("ds", d, before[before.index(n) - 1]))
                    todo = state_steps(d, n)
                    for i, (c, into) in enumerate(todo):
                        if i:
                            dve.wait_ge(state_step, h * STATE_STEPS + state_at[d, n] + i)
                        c_in = c - GROUPS[n][0]
                        ins = nc.vector.scalar_tensor_tensor(
                            last_state[d][:, :] if into is None else state[d][:, into, :], state[d][:, c, :],
                            f[d][:, c * P:c * P + 1], g.bank[bk.bank(name)][:, c_in * P:(c_in + 1) * P],
                            ALU.mult, ALU.add)
                        if i == len(todo) - 1:
                            bk.read(ins, name)
                        else:
                            ins.then_inc(state_step, 1)
            state_at, total = {}, 0
            for d, n in STATE_ORDER:
                state_at[d, n] = total
                total += len(state_steps(d, n)) - 1
            assert total == STATE_STEPS

            def convolve(h, taps):
                for tap in taps:
                    if tap == CONV_LEFT:
                        nc.vector.tensor_scalar(xc[:, :], lx[:, :], g.v("conv_w", h + 4 * tap), g.v("conv_b", h),
                                                ALU.mult, ALU.add).then_inc(conv, 1)
                        continue
                    shift = tap - CONV_LEFT
                    dve.wait_ge(conv, h * CONV_N + 1 + 2 * (0, 1, 3).index(tap))
                    for t0, tn, _ in SEGS:
                        lo, hi = t0 + max(0, -shift), t0 + tn - max(0, shift)
                        nc.vector.scalar_tensor_tensor(xc[:, lo:hi], lx[:, lo + shift:hi + shift],
                                                       g.v("conv_w", h + 4 * tap), xc[:, lo:hi], ALU.mult, ALU.add
                                                       ).then_inc(conv, 1)

            def scan(h, d):
                dve.wait_ge(gap_root, h * 2 + d + 1)
                dve.wait_ge(ix_ready, h * 2 + d + 1)
                nc.vector.tensor_tensor(ig[d][:, :], ig[d][:, :], sq[:, :], ALU.mult).then_inc(u_ready, 1)
                dve.wait_ge(u_ready, h * 2 + d + 1)
                for t0, tn, c in SEGS:
                    view = lambda t: t[:, t0:t0 + tn] if d == 0 else t[:, t0:t0 + tn][:, ::-1]
                    nc.vector.tensor_tensor_scan(view(r[d]), view(dec), view(ig[d]),
                                                 g.v("h0", h + 4 * d) if c else 0.0, ALU.mult, ALU.add
                                                 ).then_inc(scanned, 1)

            def mix(h, step):
                if step == S_SELF:
                    bk.wait_full(dve, h, ("diag",))
                    for d in range(DIRS):
                        dve.wait_ge(kf_ready, h * 4 + 2 * d + 2)
                        nc.vector.tensor_tensor(q[d][:, :], q[d][:, :], f[d][:, :], ALU.mult).then_inc(qk_ready, 1)
                    bk.read(nc.vector.tensor_tensor(
                        diag[:, :, :], g.bank[bk.bank(("diag",))][:, 0:CHUNKS * 32].rearrange("p (c t) -> p c t", t=32),
                        masks[:, 0:1, :].broadcast_to([P, CHUNKS, 32]), ALU.mult), ("diag",))
                    if not first(h):
                        dve.wait_ge(scanned, h * 7)
                    nc.vector.memset(state[0][:, 0, :], 0.0).then_inc(states_zero, 1)
                    nc.vector.memset(state[1][:, CTX_CHUNKS - 1, :], 0.0).then_inc(states_zero, 1)
                if S_LEVELS <= step < S_LEVELS + LEVELS:
                    one_level(h, step - S_LEVELS)
                if step == S_KEYS:
                    nc.vector.tensor_copy(head_vecs[:, 0:4], g.vecs[:, VEC["ba"]:VEC["ba"] + 16].rearrange(
                        "p (n t) -> p n t", t=HEADS)[:, :, ds(h)].rearrange("p n a -> p (n a)")).then_inc(vecs_ready, 1)
                    nc.vector.tensor_copy(head_vecs[:, 4:5], g.v("hg_gain", h)).then_inc(vecs_ready, 1)
                    nc.vector.tensor_copy(head_vecs[:, 5:9], small[:, 3:5, :].rearrange(
                        "p n (d t) -> p (n d) t", t=HEADS)[:, :, ds(h)].rearrange("p n a -> p (n a)")
                                          ).then_inc(vecs_ready, 1)
                if step == S_ADD:
                    dve.wait_ge(states_in, h * 32 + 32)
                    dve.wait_ge(tot_ready, h * 14 + 14)
                    states(h, STATE_ORDER[:4])
                if step == S_ADD2:
                    states(h, STATE_ORDER[4:])
                if step == S_OUT:
                    dve.wait_ge(tile_in[T_LX], h * 16 + 16)
                    convolve(h, (CONV_LEFT, 0, 1))
                if step == S_OUT2:
                    convolve(h, (3,))
                if step == S_SUM:
                    bk.wait_read(dve, h, ("sum",))
                    nc.vector.reciprocal(rstd[:, :], root[:, :]).then_inc(rstd_ready, 1)
                if step == S_SPREAD:
                    dve.wait_ge(gate_ready, h + 1)
                    for n, (t0, tn) in enumerate(TOK_BLOCKS):
                        name = ("spread", n)
                        bk.wait_full(dve, h, name)
                        bk.wait_read(dve, h, ("out", n))
                        bk.read(nc.vector.tensor_tensor(o_gain[:, t0:t0 + tn], o_gain[:, t0:t0 + tn],
                                                        g.bank[bk.bank(name)][:, 0:tn], ALU.mult), name)
                    for n in range(3):
                        bk.wait_read(dve, h, ("spread", n))
                    nc.vector.tensor_tensor(gate[:, :], o_gain[:, :], gate[:, :], ALU.mult).then_inc(head_done, 1)
                if step in (S_GATES + 1, S_GATES + 3):
                    d = (step - S_GATES) // 2
                    for n in range(3):
                        bk.wait_read(dve, h, ("lru", d, 1, n))
                    nc.vector.tensor_tensor(ig[d][:, :], ig[d][:, :], xc[:, :], ALU.mult).then_inc(ix_ready, 1)
                if step in (S_GATES + 1, S_GATES + 4):
                    d = (step - S_GATES) // 4
                    dve.wait_ge(lru_exp, h * 6 + 3 * d + 3)
                    nc.vector.scalar_tensor_tensor(sq[:, :], sq[:, :], 1.0, r[d][:, :], ALU.add, ALU.mult
                                                   ).then_inc(gap_ready, 1)
                if step == S_GATES + 2:
                    scan(h, 0)
                if step == S_GATES + 5:
                    scan(h, 1)
                    dve.wait_ge(scanned, h * 7 + 4)
                    for d, t in ((0, CTX - 1), (1, 0)):
                        nc.vector.tensor_copy(new_lru[:, ds(h + 4 * d)], r[d][:, t:t + 1]).then_inc(scanned, 1)
                if step == S_GATES + 6:
                    dve.wait_ge(scanned, h * 7 + 6)
                    nc.vector.tensor_tensor(r[0][:, :], r[0][:, :], r[1][:, :], ALU.add).then_inc(scanned, 1)
                    dve.wait_ge(scanned, h * 7 + 7)
                    dve.wait_ge(lg_ready, h + 1)
                    nc.vector.tensor_tensor(lg[:, :], r[0][:, :], lg[:, :], ALU.mult).then_inc(tile_done, 1)

            def out_weights(m):
                dve.wait_ge(out_hi_ready, m + 1)
                nc.vector.tensor_tensor(out_lo[:, m % 2, :], out_raw[:, :], out_hi[:, m % 2, :].bitcast(F32),
                                        ALU.subtract).then_inc(out_lo_ready, 1)

            def add_to_x(u, bank, added):
                m, b = divmod(u, 3)
                t0, n = TOK_BLOCKS[b]
                xs = g.x[:, m, t0:t0 + n]
                nc.vector.scalar_tensor_tensor(xs, g.bank[bank][:, 0:n], g.m(16 + m, int(b > 0)), xs, ALU.mult, ALU.add
                                               ).then_inc(added, 1)

            def out(step):
                if step == LEAD:
                    dve.wait_ge(acc_used, IN_BLOCKS)
                    nc.vector.tensor_tensor(g.mod[:, 16:48, :], g.bank[2][:, 0:64].rearrange("p (j c) -> p j c", c=2),
                                            g.v("b_ada", 16, 32).unsqueeze(2).broadcast_to([P, 32, 2]), ALU.add
                                            ).then_inc(mod_done, 1)
                    dve.wait_ge(mod_done, 1)
                    nc.vector.scalar_tensor_tensor(g.amp2[:, :, :], g.mod[:, 32:40, :], 1.0,
                                                   g.v("norm2", 0, 8).unsqueeze(2).broadcast_to([P, 8, 2]),
                                                   ALU.add, ALU.mult).then_inc(mod_done, 1)
                    dve.wait_ge(mod_done, 2)
                for i in SPLIT_AT.get(step - 1, ()):
                    dve.wait_ge(early_hi_ready, i + 1)
                    nc.vector.tensor_tensor(early_lo[:, i, :], early_raw[:, i, :], early_hi[:, i, :].bitcast(F32),
                                            ALU.subtract).then_inc(early_lo_ready, 1)
                if step == S_EARLY:
                    out_weights(0)
                for u in early_units(step):
                    m, b = divmod(u, 3)
                    if b == 0 and m + 1 < KT:
                        out_weights(m + 1)
                    if u in (0, 3):
                        dve.wait_ge(x_in[u // 3], 16)
                    dve.wait_ge(early_full, u + 1)
                    add_to_x(u, u % 2, early_added)
                if step == S_HEAD_SPLIT:
                    dve.wait_ge(late_hi_ready, 1)
                    nc.vector.tensor_tensor(late_lo[0][:, :], gate[:, :], late_hi[0][:, :].bitcast(F32), ALU.subtract
                                            ).then_inc(late_lo_ready, 1)
                if step == S_LATE_WEIGHTS:
                    dve.wait_ge(late_w_hi_ready, 1)
                    nc.vector.tensor_tensor(late_w_lo[:, :, :, :], late_raw[:, :, :, :],
                                            late_w_hi[:, :, :, :].bitcast(F32), ALU.subtract).then_inc(late_w_lo_ready, 1)

            for free in bk.free.values():
                dve.sem_inc(free, 1)
            nc.vector.memset(lru_w[:, :, :], 0.0).then_inc(zeroed, 1)
            norm.vector(dve)
            small_constants(nc, dve, g, small, small_dve, small_act)
            dve.wait_ge(const_in, 16)
            turns(dve, project, mix, out)
            dve.wait_ge(late_hi_ready, 2)
            nc.vector.tensor_tensor(late_lo[1][:, :], lg[:, :], late_hi[1][:, :].bitcast(F32), ALU.subtract
                                    ).then_inc(late_lo_ready, 1)
            dve.wait_ge(early_added, OUT_UNITS)

            def add_squares(m):
                dve.wait_ge(x_squared, m + 1)
                if m > 1:
                    dve.wait_ge(x_sq_added, m - 1)
                nc.vector.tensor_tensor(sq_sum[:, :], sq_sum[:, :], x_sq[:, m % 2, :], ALU.add).then_inc(x_sq_added, 1)
            for u in range(OUT_UNITS):
                dve.wait_ge(late_full, u + 1)
                add_to_x(u, MIX_BANKS[u % len(MIX_BANKS)], late_added)
                if u % 3 == 2 and u > 5:
                    add_squares(u // 3 - 1)
            add_squares(KT - 1)
            dve.wait_ge(x_summed, 1)


def mlp(nc, g, a):
    ctx = ExitStack()
    with ctx:
        sem = lambda n: ctx.enter_context(nc.semaphore("ff_" + n))
        two = lambda n: [sem(f"{n}{s}") for s in range(2)]
        norm = Norm(nc, g, sem, "norm2_", g.x, lambda k, c: g.amp2[:, ds(k), c], lambda k, c: g.m(24 + k, c),
                    g.up_ring, a["w_ff1"])
        up = g.up_ring
        down = Ring(nc, "down_", 144, raw_slots=1)
        hid_hi = at(nc, "hid_hi", [P, 4, TOKENS], F32R, 164)
        hid_lo = at(nc, "hid_lo", [P, 4, TOKENS], F32R, 184)
        hid_relu = at(nc, "hid_relu", [P, 4, TOKENS], F32, 184)
        up_in, up_lo, up_used = up.raw_in, up.lo_ready, up.used
        down_in, down_hi, down_lo = sem("down_in"), sem("down_hi"), sem("down_lo")
        full = [sem(f"full{b}") for b in range(2)]
        relu_ready, squared, hid_hi_ready, hid_lo_ready = (
            sem("relu_ready"), sem("squared"), sem("hid_hi_ready"), sem("hid_lo_ready"))
        DOWN_BANKS = 4
        UNITS = KT * 3
        unit_full = [sem(f"unit_full{u}") for u in range(DOWN_BANKS)]
        unit_added = [sem(f"unit_added{u}") for u in range(DOWN_BANKS)]
        PER = UNITS // DOWN_BANKS
        pairs = FF_BLOCKS // 2
        block = ctx.enter_context(nc.Block())

        def over_pairs(eng, step):
            step(0, 0)
            step(1, 1)
            with eng.Fori(1, (pairs - 2) // 2) as i:
                step(i * 2, 0)
                step(i * 2 + 1, 1)
            step(pairs - 2, 0)

        @block.sync
        def _(sp):
            def load_up(p, s):
                if not first(p):
                    sp.wait_ge(up_lo[s], p)
                sp.dma_start(up.raw[:, s, :], a["w_ff1"][ds(p * 2 + s), :, :].rearrange("a p n -> p (a n)")
                             ).then_inc(up_in[s], 16)

            def load_down(p, s):
                if not (first(p) and s == 0):
                    sp.wait_ge(down_lo, p * 2 + s)
                sp.dma_start(down.raw[:, 0, :], a["w_ff2"][ds(p * 2 + s), :, :].rearrange("a p n -> p (a n)")
                             ).then_inc(down_in, 16)

            norm.sync(sp)
            for s in range(2):
                load_up(1, s)
            load_down(0, 0)
            load_down(0, 1)

            def step(p, parity):
                for s in range(2):
                    load_up(p + 2, s)
                for s in range(2):
                    load_down(p + 1, s)
            with sp.Fori(0, pairs - 2) as p:
                step(p, 0)
            for s in range(2):
                sp.wait_ge(up_lo[s], pairs)
                sp.dma_start(up.raw[:, s, :], a["w_ff2"][(pairs - 1) * 2 + s, :, :]).then_inc(up_in[s], 16)

        def down_weights(p, s, act=None, dve=None):
            if act is not None:
                act.wait_ge(down_in, (p * 2 + s) * 16 + 16)
                if not first(p):
                    act.wait_ge(unit_full[(UNITS - 1) % DOWN_BANKS], p * PER)
                nc.scalar.activation(down.hi[:, s, :], down.raw[:, 0, :], ACT.Copy).then_inc(down_hi, 1)
            else:
                dve.wait_ge(down_hi, p * 2 + s + 1)
                nc.vector.tensor_tensor(down.lo[:, s, :], down.raw[:, 0, :], down.hi[:, s, :].bitcast(F32), ALU.subtract
                                        ).then_inc(down_lo, 1)

        def hidden(p, parity, act=None, dve=None, tiles=range(2)):
            for s in tiles:
                for b, (t0, n) in enumerate(TOK_BLOCKS):
                    at_n = (p * 2 + s) * 3 + b + 1
                    bank = g.bank[3 * s + b if first(p) else b][:, 0:n]
                    dst = (slice(None), 2 * parity + s, slice(t0, t0 + n))
                    if act is not None:
                        if b < 2:
                            act.wait_ge(full[b], p * 2 + s + 1)
                        else:
                            act.wait_ge(up_used[s], p + 1)
                        nc.scalar.activation(hid_relu[dst], bank, ACT.Relu).then_inc(relu_ready, 1)
                        act.wait_ge(relu_ready, at_n)
                        nc.scalar.activation(hid_hi[dst], hid_relu[dst], ACT.Square).then_inc(hid_hi_ready, 1)
                        continue
                    dve.wait_ge(relu_ready, at_n)
                    nc.vector.tensor_tensor(bank, hid_relu[dst], bank, ALU.mult
                                            ).then_inc(squared, 1)
                    dve.wait_ge(squared, at_n)
                    dve.wait_ge(hid_hi_ready, at_n)
                    nc.vector.tensor_tensor(hid_lo[dst], bank, hid_hi[dst].bitcast(F32), ALU.subtract
                                            ).then_inc(hid_lo_ready, 1)

        @block.scalar
        def _(act):
            norm.scalar(act)
            for s in range(2):
                split_weights(nc, act, None, 1, s, up)
                hidden(0, 0, act=act, tiles=(s,))

            def step(p, parity):
                for s in range(2):
                    down_weights(p, s, act=act)
                hidden(p + 1, 1 - parity, act=act)
                for s in range(2):
                    split_weights(nc, act, None, p + 2, s, up)
            step(0, 0)
            step(1, 1)
            with act.Fori(1, (pairs - 2) // 2) as i:
                step(i * 2, 0)
                step(i * 2 + 1, 1)
            step(pairs - 2, 0)

        @block.vector
        def _(dve):
            def add(p, units):
                for u in units:
                    m, b = divmod(u, 3)
                    t0, n = TOK_BLOCKS[b]
                    dve.wait_ge(unit_full[u % DOWN_BANKS], p * PER + u // DOWN_BANKS + 1)
                    xs = g.x[:, m, t0:t0 + n]
                    nc.vector.scalar_tensor_tensor(xs, g.bank[3 + u % DOWN_BANKS][:, 0:n], g.m(40 + m, int(b > 0)), xs,
                                                   ALU.mult, ALU.add).then_inc(unit_added[u % DOWN_BANKS], 1)
            norm.vector(dve)
            for s in range(2):
                split_weights(nc, None, dve, 1, s, up)
                hidden(0, 0, dve=dve, tiles=(s,))

            def step(p, parity):
                for s in range(2):
                    down_weights(p, s, dve=dve)
                hidden(p + 1, 1 - parity, dve=dve)
                add(p, range(0, 8))
                for s in range(2):
                    split_weights(nc, None, dve, p + 2, s, up)
                add(p, range(8, UNITS))
            step(0, 0)
            step(1, 1)
            with dve.Fori(1, (pairs - 2) // 2) as i:
                step(i * 2, 0)
                step(i * 2 + 1, 1)
            step(pairs - 2, 0)
            add(pairs - 1, range(UNITS))
            for u in range(DOWN_BANKS):
                dve.wait_ge(unit_added[u], pairs * PER)

        @block.tensor
        def _(pe):
            def up_product(p):
                for s in range(2):
                    pe.wait_ge(up_lo[s], p + 1)
                    for b, (t0, n) in enumerate(TOK_BLOCKS):
                        after_first = isinstance(p, int) and p == 1 and s == 0
                        pe.wait_ge(hid_lo_ready, b + 1 if after_first else (p * 2 + s - 1) * 3 + b + 1)
                        for k in range(KT):
                            last = exact_product(nc, g.bank[b][:, 0:n], up.hi[:, s, k * P:(k + 1) * P],
                                                 up.lo[:, s, k * P:(k + 1) * P], g.h_hi[:, k, t0:t0 + n],
                                                 g.h_lo[:, k, t0:t0 + n], k == 0, k == KT - 1)
                        last.then_inc(up_used[s] if b == 2 else full[b], 1)

            def down_product(p, parity, weights=down):
                if weights is down:
                    pe.wait_ge(down_lo, p * 2 + 2)
                else:
                    for s in range(2):
                        pe.wait_ge(up_lo[s], pairs + 1)
                pe.wait_ge(hid_lo_ready, p * 6 + 6)
                for u in range(UNITS):
                    m, b = divmod(u, 3)
                    t0, n = TOK_BLOCKS[b]
                    if not (first(p) and u < DOWN_BANKS):
                        pe.wait_ge(unit_added[u % DOWN_BANKS], p * PER + u // DOWN_BANKS)
                    for s in range(2):
                        last = exact_product(nc, g.bank[3 + u % DOWN_BANKS][:, 0:n], weights.hi[:, s, m * P:(m + 1) * P],
                                             weights.lo[:, s, m * P:(m + 1) * P], hid_hi[:, 2 * parity + s, t0:t0 + n],
                                             hid_lo[:, 2 * parity + s, t0:t0 + n], s == 0, s == 1)
                    last.then_inc(unit_full[u % DOWN_BANKS], 1)

            norm.tensor(pe)
            norm.first_products(pe, range(6), lambda s, b: up_used[s] if b == 2 else full[b])

            def step(p, parity):
                up_product(p + 1)
                down_product(p, parity)
            over_pairs(pe, step)
            down_product(pairs - 1, 1, up)


def output(nc, g, a):
    ctx = ExitStack()
    with ctx:
        sem = lambda n: ctx.enter_context(nc.semaphore("y_" + n))
        SLOTS_Y, half_d = 4, D_MODEL // 2
        y = at(nc, "y_tok", [P, SLOTS_Y, D_MODEL], F32, 160)
        squares = at(nc, "y_squares", [P, 2, half_d], F32, 176)
        gain = at(nc, "y_gain", [P, D_MODEL], F32, 180)
        sums, total = at(nc, "y_sums", [P, CHUNKS, 2], F32, 184), at(nc, "y_total", [P, CHUNKS], F32, 185)
        root, rstd = at(nc, "y_root", [P, CHUNKS], F32, 186), at(nc, "y_rstd", [P, CHUNKS], F32, 187)
        gain_in, turned, squared, totalled, rooted, rstd_ready, scaled = (
            sem(n) for n in ("gain_in", "turned", "squared", "totalled", "rooted", "rstd_ready", "scaled"))
        stored = [sem(f"stored{s}") for s in range(SLOTS_Y)]
        banks = lambda c: (g.bank[2 * (c % SLOTS_Y)], g.bank[2 * (c % SLOTS_Y) + 1])
        block = ctx.enter_context(nc.Block())

        @block.tensor
        def _(pe):
            for c in range(CHUNKS):
                if c >= SLOTS_Y:
                    pe.wait_ge(scaled, 2 * (c - SLOTS_Y) + 2)
                for f in range(KT):
                    last = nc.tensor.transpose(banks(c)[f // 4][:, (f % 4) * P:(f % 4 + 1) * P],
                                               g.x[:, f, c * P:(c + 1) * P], g.ident[:, :])
                last.then_inc(turned, 1)

        @block.scalar
        def _(act):
            def square(c):
                act.wait_ge(turned, c + 1)
                for half in range(2):
                    if c:
                        act.wait_ge(squared, 2 * c + half - 1)
                    nc.scalar.activation(squares[:, half, :], banks(c)[half][:, :], ACT.Square,
                                         accum_out=sums[:, c, half:half + 1]).then_inc(squared, 1)
            square(0)
            for c in range(CHUNKS):
                if c + 1 < CHUNKS:
                    square(c + 1)
                act.wait_ge(totalled, c + 1)
                nc.scalar.activation(root[:, c:c + 1], total[:, c:c + 1], ACT.Sqrt, bias=g.eps[:, 0:1],
                                     scale=1.0 / D_MODEL).then_inc(rooted, 1)

        @block.vector
        def _(dve):
            def add(c):
                dve.wait_ge(squared, 2 * c + 2)
                nc.vector.tensor_tensor(total[:, c:c + 1], sums[:, c, 0:1], sums[:, c, 1:2], ALU.add
                                        ).then_inc(totalled, 1)

            def scale(c):
                dve.wait_ge(rstd_ready, c + 1)
                if c >= SLOTS_Y:
                    dve.wait_ge(stored[c % SLOTS_Y], c // SLOTS_Y * 16)
                for half in range(2):
                    part = slice(half * half_d, (half + 1) * half_d)
                    nc.vector.scalar_tensor_tensor(y[:, c % SLOTS_Y, part], banks(c)[half][:, :], rstd[:, c:c + 1],
                                                   gain[:, part], ALU.mult, ALU.mult).then_inc(scaled, 1)
            add(0)
            for c in range(CHUNKS):
                if c + 1 < CHUNKS:
                    add(c + 1)
                dve.wait_ge(rooted, c + 1)
                nc.vector.reciprocal(rstd[:, c:c + 1], root[:, c:c + 1]).then_inc(rstd_ready, 1)
                if c == 1:
                    dve.wait_ge(gain_in, 16)
                if c:
                    scale(c - 1)
            scale(CHUNKS - 1)

        @block.sync
        def _(sp):
            sp.dma_start(gain[:, :], a["final_gain"].broadcast_to([P, D_MODEL])).then_inc(gain_in, 16)
            for c in range(CHUNKS):
                t = c * P
                sp.wait_ge(scaled, 2 * c + 2)
                sp.dma_start(a["y_prompt"][t:t + P, :] if t < CTX else a["y_sample"][t - CTX:t - CTX + P, :],
                             y[:, c % SLOTS_Y, :]).then_inc(stored[c % SLOTS_Y], 16)
            for s in range(SLOTS_Y):
                sp.wait_ge(stored[s], 16 * len(range(s, CHUNKS, SLOTS_Y)))


def backbone_step(nc, a):
    g = Ctx()
    low = [BASE]

    def const(name, shape, dtype=F32):
        size = 4
        for n in shape[1:]:
            size *= n
        t = nc.alloc_sbuf_tensor_at(name, shape, dtype, offset=low[0])
        low[0] += (size + 31) // 32 * 32
        assert low[0] <= AREA
        return t
    g.ident, g.ones = const("ident_sb", [P, P]), const("ones", [P, P])
    g.vecs, g.eps, g.cond_s = const("vecs_sb", [P, NVEC]), const("eps", [P, 1]), const("cond_silu", [P, KT, 2])
    g.mod = const("mod", [P, ADA_BLOCKS, 2])
    g.fold_acc = const("fold_acc_rest", [P, 2, P])
    g.amp1, g.amp2 = const("amp1", [P, KT, 2]), const("amp2", [P, KT, 2])
    g.h_hi = at(nc, "h_hi", [P, KT, TOKENS], F32R, 0)
    g.h_lo = at(nc, "h_lo", [P, KT, TOKENS], F32R, 40)
    g.x = at(nc, "x", [P, KT, TOKENS], F32, 80)
    g.x_first = at(nc, "x_first", [P, KT, TOKENS], F32, 124)
    g.proj = nc.dram_tensor("proj", [IN_BLOCKS, P, TOKENS], F32, kind="Internal").ap()
    g.mix_out = nc.dram_tensor("mix_out", [KT, P, TOKENS], F32, kind="Internal").ap()
    g.x_scratch = nc.dram_tensor("x_scratch", [P, KT * TOKENS], F32, kind="Internal").ap()

    def v(name, i, n=1):
        return g.vecs[:, ds(VEC[name] + i, n)]
    g.v = v
    g.m = lambda j, c: g.mod[:, ds(j), c]
    ctx = ExitStack()
    with ctx:
        g.constants_ready = ctx.enter_context(nc.semaphore("constants_ready"))
        g.bank = [ctx.enter_context(nc.psum_tensor(f"bank{b}", [P, 512], F32)) for b in range(8)]
        sem = lambda n: ctx.enter_context(nc.semaphore(n))
        g.in_ring = Ring(nc, "in_", 80, sem)
        g.up_ring = Ring(nc, "up_", 120, sem)
        modulation_and_input(nc, g, a)
        projections_and_mixers(nc, g, a)
        mlp(nc, g, a)
        output(nc, g, a)


def shape_constants():
    import numpy as np
    key, query = np.arange(P)[:, None] % 32, np.arange(32)[None, :]
    masks = [key == query]
    for level in range(MASKED):
        size = 2 ** level
        same = key // (2 * size) == query // (2 * size)
        key_right, query_right = key // size % 2 == 1, query // size % 2 == 1
        masks += [same & ~key_right & query_right, same & key_right & ~query_right]
    masks = np.stack(masks, 1).astype(np.float32)
    quarter = D_MODEL // 4
    omega = (1.0 / (np.float32(10000.0) ** (np.arange(quarter, dtype=np.float32) / np.float32(quarter)))).astype(np.float32)

    def table(n):
        angle = np.arange(n, dtype=np.float32)[:, None] * omega
        both = np.concatenate([np.sin(angle), np.cos(angle)], 1)
        return both.reshape(n, 4, P).transpose(2, 1, 0).reshape(P, 4 * n)
    pos = np.concatenate([table(LAT // GRID_W), table(GRID_W)], 1).astype(np.float32)
    return {"ident": np.eye(P, dtype=np.float32), "masks": np.ascontiguousarray(masks), "pos": np.ascontiguousarray(pos)}


def kernel(**inputs):
    import numpy as np
    import concourse.bacc as bacc
    from concourse.bass_utils import run_bass_kernel_spmd

    w = {n: np.asarray(x) for n, x in inputs.items()}

    def column_tiles(m):
        return m.reshape(KT, P, -1, P).transpose(2, 1, 0, 3).reshape(-1, P, KT * P)

    def cols(x):
        return x.reshape(-1, P).T
    starts = (16, 20, 0, 8, 4, 12, 24, 28)
    order = [start + h for h in range(HEADS) for start in starts]
    vecs = np.concatenate([cols(w[n]) for n in (
        "b_ada", "norm1_gain", "norm2_gain", "hg_lb_logits", "hg_norm_gain", "conv_w", "conv_b",
        "lru_ba", "lru_bx", "lru_lambda", "state_rglru")], 1)
    arrays = {
        "x_prompt": w["x_prompt"][0], "x_sample": w["x_sample"][0],
        "cond": np.stack([w["c_ctx"].reshape(KT, P), w["c"].reshape(KT, P)], 2).transpose(1, 0, 2),
        "vecs": vecs, "w_ada": column_tiles(w["w_ada"][0]), "w_in": column_tiles(w["w_in"][0])[order],
        "w_out": column_tiles(w["w_out"][0]), "w_ff1": column_tiles(w["w_ff1"][0]),
        "w_ff2": w["w_ff2"][0].reshape(FF_BLOCKS, P, D_MODEL),
        "final_gain": w["final_gain"].reshape(1, D_MODEL), "state_hgrn": w["state_hgrn"][0, 0],
        "lru_wa": w["lru_wa"][0], "lru_wx": w["lru_wx"][0],
    }
    arrays.update(shape_constants())
    arrays = {"in_" + n: np.ascontiguousarray(x) for n, x in arrays.items()}
    nc = bacc.Bacc("TRN2", target_bir_lowering=False, num_devices=1)
    a = {n[3:]: nc.dram_tensor(n, x.shape, mybir.dt.from_np(x.dtype), kind="ExternalInput").ap()
         for n, x in arrays.items()}
    outs = {"y_prompt": (CTX, D_MODEL), "y_sample": (LAT, D_MODEL), "new_hgrn": (DIRS, HEADS, P, P), "new_lru": (P, 8)}
    for n, shape in outs.items():
        a[n] = nc.dram_tensor("out_" + n, shape, F32, kind="ExternalOutput").ap()
    backbone_step(nc, a)
    got = run_bass_kernel_spmd(nc, [arrays], core_ids=[0]).results[0]
    return (got["out_y_prompt"][None], got["out_y_sample"][None], got["out_new_hgrn"][None, None],
            np.ascontiguousarray(got["out_new_lru"].T).reshape(1, 1, DIRS, HEADS * P))
```
